# Optimizing a Trainium2 kernel written in Bass

```python
import jax, jax.numpy as jnp
from jax import lax
import numpy as np

D_MODEL = 1024
BATCH = 1
SEQ = 1024
DEPTH = 1
DEC_BATCH = 8
DEC_SEQ = 16
PAST_LEN = 512

CHUNK = 64
N_META = 16
CONV_WIDTH = 3
CONV_DIM = D_MODEL
SB_HEADS = 8
SB_HEAD_DIM = D_MODEL // SB_HEADS
SB_DIM = SB_HEADS * SB_HEAD_DIM
Q_BLOCK = 128
EPS = 1e-6
SPLITS = (CONV_DIM, CONV_DIM, CONV_DIM, CONV_DIM, SB_DIM, SB_DIM, SB_DIM, SB_DIM, D_MODEL, D_MODEL)
IN_DIM = sum(SPLITS)
SPLIT_OFFSETS = [int(o) for o in np.cumsum(SPLITS)[:-1]]

kernel_name = "gated_conv_stickbreak_hybrid_step"

def rmsnorm(x, g):
    xf = x.astype(jnp.float32)
    y = xf * lax.rsqrt(jnp.mean(xf * xf, axis=-1, keepdims=True) + EPS)
    return (y * g.astype(jnp.float32)).astype(x.dtype)

def in_projection(x, norm_g, w_in, b_in, q_norm_g, k_norm_g):
    bsz, t = x.shape[0], x.shape[1]
    xn = rmsnorm(x, norm_g)
    p = jnp.einsum('btd,de->bte', xn, w_in) + b_in
    b_c, c_c, h_c, z_c, q, k, v, z_s, g_c, g_s = jnp.split(p, SPLIT_OFFSETS, axis=-1)
    q = rmsnorm(q.reshape(bsz, t, SB_HEADS, SB_HEAD_DIM), q_norm_g)
    k = rmsnorm(k.reshape(bsz, t, SB_HEADS, SB_HEAD_DIM), k_norm_g)
    v = v.reshape(bsz, t, SB_HEADS, SB_HEAD_DIM)
    return b_c, c_c, h_c, z_c, q, k, v, z_s, g_c, g_s

def short_conv(u, prev, w):
    t = u.shape[1]
    full = jnp.concatenate([prev.astype(u.dtype), u], axis=1)
    y = w[0] * full[:, 0:t]
    for i in range(1, CONV_WIDTH):
        y = y + w[i] * full[:, i:i + t]
    return y, full[:, -(CONV_WIDTH - 1):]

def stick_breaking(q, k, v, q_pos, k_pos):
    scale = SB_HEAD_DIM ** -0.5
    z = jnp.einsum('bqhd,bkhd->bhqk', q, k).astype(jnp.float32) * scale
    mask = (k_pos[None, :] < q_pos[:, None])[None, None]
    log_beta = jax.nn.log_sigmoid(z)
    log_1m_beta = jnp.where(mask, jax.nn.log_sigmoid(-z), 0.0)
    suffix = lax.cumsum(log_1m_beta, axis=3, reverse=True) - log_1m_beta
    a = jnp.where(mask, jnp.exp(log_beta + suffix), 0.0)
    return jnp.einsum('bhqk,bkhd->bqhd', a.astype(v.dtype), v)

def merge_out(x, y_c, y_s, g_c, g_s, w_conv_o, w_sb_o, w_o):
    m = (jax.nn.sigmoid(g_c) * jnp.einsum('btc,cd->btd', y_c, w_conv_o)
         + jax.nn.sigmoid(g_s) * jnp.einsum('bte,ed->btd', y_s, w_sb_o))
    return x + jnp.einsum('btd,de->bte', m, w_o)

def prompt_layer(h, norm_g, w_in, b_in, q_norm_g, k_norm_g, conv_w, w_conv_o, w_sb_o, w_o):
    bsz, t = h.shape[0], h.shape[1]
    b_c, c_c, h_c, z_c, q, k, v, z_s, g_c, g_s = in_projection(h, norm_g, w_in, b_in, q_norm_g, k_norm_g)
    conv_out, conv_state = short_conv(c_c * h_c, jnp.zeros((bsz, CONV_WIDTH - 1, CONV_DIM), h.dtype), conv_w)
    y_c = jax.nn.silu(z_c) * (b_c * conv_out)
    nb = -(-t // Q_BLOCK)
    tp = nb * Q_BLOCK
    qp = jnp.pad(q, ((0, 0), (0, tp - t), (0, 0), (0, 0)))
    qb = qp.reshape(bsz, nb, Q_BLOCK, SB_HEADS, SB_HEAD_DIM).transpose(1, 0, 2, 3, 4)
    posb = jnp.arange(tp).reshape(nb, Q_BLOCK)
    k_pos = jnp.arange(t)
    ob = lax.map(lambda a: stick_breaking(a[0], k, v, a[1], k_pos), (qb, posb))
    o = ob.transpose(1, 0, 2, 3, 4).reshape(bsz, tp, SB_DIM)[:, :t]
    y_s = jax.nn.silu(z_s) * o
    y = merge_out(h, y_c, y_s, g_c, g_s, w_conv_o, w_sb_o, w_o)
    return y, k, v, conv_state

def sample_layer(h, k_past, v_past, conv_prev, norm_g, w_in, b_in, q_norm_g, k_norm_g, conv_w, w_conv_o, w_sb_o, w_o):
    bsz, s = h.shape[0], h.shape[1]
    p_len = k_past.shape[1]
    b_c, c_c, h_c, z_c, q, k, v, z_s, g_c, g_s = in_projection(h, norm_g, w_in, b_in, q_norm_g, k_norm_g)
    conv_out, conv_state = short_conv(c_c * h_c, conv_prev, conv_w)
    y_c = jax.nn.silu(z_c) * (b_c * conv_out)
    k_all = jnp.concatenate([k_past.astype(k.dtype), k], axis=1)
    v_all = jnp.concatenate([v_past.astype(v.dtype), v], axis=1)
    q_pos = p_len + jnp.arange(s)
    k_pos = jnp.arange(p_len + s)
    o = stick_breaking(q, k_all, v_all, q_pos, k_pos).reshape(bsz, s, SB_DIM)
    y_s = jax.nn.silu(z_s) * o
    y = merge_out(h, y_c, y_s, g_c, g_s, w_conv_o, w_sb_o, w_o)
    return y, k, v, conv_state

def setup_inputs(seed: int = 0) -> dict:
    key = jax.random.key(seed)
    ks = jax.random.split(key, 16)
    nrm = jax.random.normal
    f32 = jnp.float32
    return {
        "x_prompt": nrm(ks[0], (BATCH, SEQ, D_MODEL), f32),
        "x_sample": nrm(ks[1], (DEC_BATCH, DEC_SEQ, D_MODEL), f32),
        "cache_k": nrm(ks[2], (DEPTH, DEC_BATCH, PAST_LEN, SB_HEADS, SB_HEAD_DIM), f32),
        "cache_v": nrm(ks[3], (DEPTH, DEC_BATCH, PAST_LEN, SB_HEADS, SB_HEAD_DIM), f32),
        "state_conv": nrm(ks[4], (DEPTH, DEC_BATCH, CONV_WIDTH - 1, CONV_DIM), f32),
        "meta_tokens": nrm(ks[5], (N_META, D_MODEL), f32),
        "norm_g": 1.0 + 0.01 * nrm(ks[6], (DEPTH, D_MODEL), f32),
        "w_in": nrm(ks[7], (DEPTH, D_MODEL, IN_DIM), f32) * D_MODEL ** -0.5,
        "b_in": 0.01 * nrm(ks[8], (DEPTH, IN_DIM), f32),
        "q_norm_g": 1.0 + 0.01 * nrm(ks[9], (DEPTH, SB_HEAD_DIM), f32),
        "k_norm_g": 1.0 + 0.01 * nrm(ks[10], (DEPTH, SB_HEAD_DIM), f32),
        "conv_w": nrm(ks[11], (DEPTH, CONV_WIDTH, CONV_DIM), f32) * CONV_WIDTH ** -0.5,
        "w_conv_o": nrm(ks[12], (DEPTH, CONV_DIM, D_MODEL), f32) * CONV_DIM ** -0.5,
        "w_sb_o": nrm(ks[13], (DEPTH, SB_DIM, D_MODEL), f32) * SB_DIM ** -0.5,
        "w_o": nrm(ks[14], (DEPTH, D_MODEL, D_MODEL), f32) * D_MODEL ** -0.5,
    }

def reference(x_prompt, x_sample, cache_k, cache_v, state_conv, meta_tokens, norm_g, w_in, b_in,
              q_norm_g, k_norm_g, conv_w, w_conv_o, w_sb_o, w_o):
    meta = jnp.broadcast_to(meta_tokens.astype(x_prompt.dtype)[None], (x_prompt.shape[0], N_META, D_MODEL))
    hp = jnp.concatenate([meta, x_prompt], axis=1)
    hs = x_sample
    kp_list, vp_list, cp_list, ksl, vsl, csl = [], [], [], [], [], []
    for l in range(DEPTH):
        hp, kp, vp, cp = prompt_layer(hp, norm_g[l], w_in[l], b_in[l], q_norm_g[l], k_norm_g[l],
                                      conv_w[l], w_conv_o[l], w_sb_o[l], w_o[l])
        hs, ks_, vs_, cs_ = sample_layer(hs, cache_k[l], cache_v[l], state_conv[l], norm_g[l], w_in[l], b_in[l],
                                         q_norm_g[l], k_norm_g[l], conv_w[l], w_conv_o[l], w_sb_o[l], w_o[l])
        kp_list.append(kp); vp_list.append(vp); cp_list.append(cp)
        ksl.append(ks_); vsl.append(vs_); csl.append(cs_)
    y_prompt = hp[:, N_META:]
    y_sample = hs
    return (y_prompt, y_sample, jnp.stack(kp_list), jnp.stack(vp_list), jnp.stack(cp_list),
            jnp.stack(ksl), jnp.stack(vsl), jnp.stack(csl))


_drawn_inputs = setup_inputs


def setup_inputs(seed=0):
    import zlib

    import numpy as np

    out = dict(_drawn_inputs(seed))
    spreads = {}
    factors = {'norm_g': 3.89,
     'b_in': 4.118,
     'q_norm_g': 64.0,
     'k_norm_g': 24.748,
     'cache_k': 8.0,
     'cache_v': 8.0,
     'state_conv': 3.353}
    for name, (base, spread) in spreads.items():
        noise = np.random.default_rng([zlib.crc32(name.encode()), seed]).standard_normal(out[name].shape)
        drawn = base * np.exp(spread * noise) if base else spread * noise
        out[name] = __import__('jax').numpy.asarray(drawn.astype(out[name].dtype))
    for name, factor in factors.items():
        out[name] = (out[name] * factor).astype(out[name].dtype)
    return out
```

```python
from contextlib import ExitStack

import concourse.bass as bass
from concourse import mybir

F32 = mybir.dt.float32
F32R = mybir.dt.float32r
BF16 = mybir.dt.bfloat16
ALU = mybir.AluOpType
ACT = mybir.ActivationFunctionType

P = 128
D = 1024
KC = D // P
META, SEQ, NB, DS, PAST = 16, 1024, 8, 16, 512
HEADS, HD = 8, 128
PT = SEQ // P
SAMPLE0 = META + SEQ
TOK = SAMPLE0 + NB * DS
LIVE = TOK - META
TILES = PT + 2
SAMPLE_TILE, META_TILE = PT, PT + 1
EPS = 1e-6
SCALE = HD ** -0.5
HIDDEN = -1e30
OFF = {n: i * D for i, n in enumerate(["B", "C", "h", "z_c", "q", "k", "v", "z_s", "g_c", "g_s"])}
CH = [(0, META + 384), (META + 384, META + 768), (META + 768, TOK)]
CHL = [(META, META + 384), (META + 384, META + 768), (META + 768, TOK)]


def tile_cols(t):
    if t == META_TILE:
        return 0, META
    return META + t * P, META + (t + 1) * P


def row(t, i, a, b):
    return t[:, bass.ds(i, 1), a:b].rearrange("p o n -> p (o n)")


def split_product(pe, out, left, right, n, first=True, last=True):
    (lh, ll), (rh, rl) = left, right
    for k in range(n):
        pe.matmul(out, lh(k), rh(k), start=first and k == 0, stop=False)
        pe.matmul(out, lh(k), rl(k), start=False, stop=False)
        mm = pe.matmul(out, ll(k), rh(k), start=False, stop=last and k == n - 1)
    return mm


class Core:

    def __init__(self, nc, ctx):
        self.nc, self.ctx = nc, ctx

    def sem(self, name):
        return self.ctx.enter_context(self.nc.semaphore(name))

    def sb(self, ctx, name, shape, dt=F32):
        return ctx.enter_context(self.nc.sbuf_tensor(name, shape, dt))


def constants_and_norm(c, d):
    nc = c.nc
    with ExitStack() as ctx:
        gb = c.sb(ctx, "norm_gain", [P, D])
        b80 = c.sb(ctx, "bias_rows", [80, P])
        cw3 = c.sb(ctx, "conv_w_rows", [3, D])
        st16 = c.sb(ctx, "state_rows", [NB * 2, D])
        xr = c.sb(ctx, "x_rows", [P, 3, D])
        junk = c.sb(ctx, "squares", [P, D])
        xn = c.sb(ctx, "x_normed", [P, 2, D])
        ss = c.sb(ctx, "sumsq", [P, TILES])
        ms = c.sb(ctx, "meansq", [P, TILES])
        rs = c.sb(ctx, "rstd", [P, TILES])
        half = c.sb(ctx, "minus_half", [P, TILES])

        x_in = [c.sem(f"x_in{i}") for i in range(3)]
        small_in = c.sem("small_in")
        made = c.sem("constants_made")
        squared = c.sem("x_squared")
        mean_ok = c.sem("x_mean")
        rstd_ok = c.sem("x_rstd")
        normed = c.sem("x_is_normed")
        turned = c.sem("x_turned")
        hi_ok = c.sem("x_hi")
        lo_ok = c.sem("x_lo")
        small_turned = c.sem("small_turned")
        small_out = c.sem("small_out")

        rows = [P] * 9 + [META]

        def source(t):
            if t == META_TILE:
                return d["meta_tokens"]
            if t == SAMPLE_TILE:
                return d["x_sample"].rearrange("b s d -> (b s) d")
            return d["x_prompt"][0, t * P:(t + 1) * P, :]

        with nc.Block() as block:
            @block.sync
            def _(sp):
                for t in range(TILES):
                    if t >= 3:
                        sp.wait_ge(normed, t - 2)
                    sp.dma_start(xr[0:rows[t], t % 3, :], source(t)).then_inc(x_in[t % 3], 16)
                    if t == 0:
                        sp.dma_start(gb[:, :], d["norm_g"].to_broadcast([P, D])).then_inc(small_in, 16)
                    if t == 2:
                        sp.dma_start(b80[:, :], d["b_in"].rearrange("o (n p) -> (o n) p", p=P)).then_inc(small_in, 16)
                        sp.dma_start(cw3[:, :], d["conv_w"][0]).then_inc(small_in, 16)
                        sp.dma_start(st16[:, :], d["state_conv"][0].rearrange("b j c -> (b j) c")).then_inc(small_in, 16)

            @block.gpsimd
            def _(pool):
                pool.memset(c.ident[:, :], 0.0).then_inc(made, 1)
                pool.memset(c.identb[:, :], 0.0).then_inc(made, 1)
                pool.memset(c.mask[:, :], 0.0).then_inc(made, 1)
                pool.memset(c.mask_s[:, :], 0.0).then_inc(made, 1)
                pool.memset(half[:, :], -0.5).then_inc(made, 1)
                pool.wait_ge(made, 5)
                for m in (c.ident, c.identb):
                    pool.affine_select(out=m[:, :], in_=m[:, :], compare_op=ALU.not_equal, fill=1.0, base=0,
                                       pattern=[[-1, P]], channel_multiplier=1).then_inc(made, 1)
                for m in (c.mask, c.mask_s):
                    pool.affine_select(out=m[:, :], in_=m[:, :], compare_op=ALU.is_gt, fill=HIDDEN, base=0,
                                       pattern=[[-1, P]], channel_multiplier=1).then_inc(made, 1)
                pool.wait_ge(made, 9)
                pool.affine_select(out=c.mask_s[:, :].rearrange("p (b j) -> p b j", j=DS),
                                   in_=c.mask_s[:, :].rearrange("p (b j) -> p b j", j=DS),
                                   compare_op=ALU.is_gt, fill=HIDDEN, base=DS,
                                   pattern=[[DS, NB], [0, DS]], channel_multiplier=-1).then_inc(made, 1)
                for t in range(TILES):
                    n = rows[t]
                    pool.wait_ge(squared, t + 1)
                    pool.tensor_scalar(ms[0:n, t:t + 1], ss[0:n, t:t + 1], 1.0 / D, EPS,
                                       ALU.mult, ALU.add).then_inc(mean_ok, 1)
                    pool.wait_ge(mean_ok, t + 1)
                    pool.tensor_tensor(rs[0:n, t:t + 1], ms[0:n, t:t + 1], half[0:n, t:t + 1],
                                       ALU.pow).then_inc(rstd_ok, 1)

            @block.scalar
            def _(act):
                def hi(t, j):
                    n, (c0, c1) = rows[t], tile_cols(t)
                    act.wait_ge(turned, 2 * t + j + 1)
                    act.activation(c.xh[:, 4 * j:4 * j + 4, c0:c1],
                                   c.bank_t[j][:, :].rearrange("p (k n) -> p k n", k=4)[:, :, 0:n],
                                   ACT.Copy).then_inc(hi_ok, 1)

                for t in range(TILES + 1):
                    if t < TILES:
                        n = rows[t]
                        act.wait_ge(x_in[t % 3], 16 * (t // 3 + 1))
                        if t:
                            act.wait_ge(squared, t)
                        act.activation(junk[0:n, :], xr[0:n, t % 3, :], ACT.Square,
                                       accum_out=ss[0:n, t:t + 1]).then_inc(squared, 1)
                    if t >= 1:
                        hi(t - 1, 0)
                        hi(t - 1, 1)

            @block.vector
            def _(dve):
                def lo(t, j):
                    n, (c0, c1) = rows[t], tile_cols(t)
                    dve.wait_ge(hi_ok, 2 * t + j + 1)
                    dve.tensor_tensor(c.xl[:, 4 * j:4 * j + 4, c0:c1],
                                      c.bank_t[j][:, :].rearrange("p (k n) -> p k n", k=4)[:, :, 0:n],
                                      c.xh[:, 4 * j:4 * j + 4, c0:c1].bitcast(F32), ALU.subtract).then_inc(lo_ok, 1)

                dve.wait_ge(small_in, 64)
                for t in range(TILES + 1):
                    if t < TILES:
                        n = rows[t]
                        dve.wait_ge(rstd_ok, t + 1)
                        if t >= 2:
                            dve.wait_ge(turned, 2 * (t - 1))
                        dve.scalar_tensor_tensor(out=xn[0:n, t % 2, :], in0=xr[0:n, t % 3, :],
                                                 scalar=rs[0:n, t:t + 1], in1=gb[0:n, :],
                                                 op0=ALU.mult, op1=ALU.mult).then_inc(normed, 1)
                    if t >= 1:
                        lo(t - 1, 0)
                        lo(t - 1, 1)
                dve.wait_ge(small_turned, 1)
                dve.tensor_copy(c.bias[:, :], c.bank_o[:, 0:80]).then_inc(small_out, 1)
                dve.tensor_copy(c.conv_w[:, :, :], c.bank_o[:, 80:104].rearrange("p (k j) -> p k j", j=3)).then_inc(small_out, 1)
                dve.tensor_copy(c.state[:, :, :], c.bank_o[:, 128:256].rearrange("p (k j) -> p k j", j=16)).then_inc(small_out, 1)

            @block.tensor
            def _(pe):
                pe.wait_ge(made, 7)
                for t in range(TILES):
                    n = rows[t]
                    pe.wait_ge(normed, t + 1)
                    for j in range(2):
                        if t:
                            pe.wait_ge(lo_ok, 2 * (t - 1) + j + 1)
                        for k in range(4):
                            mm = pe.transpose(c.bank_t[j][:, k * P:k * P + n],
                                              xn[0:n, t % 2, (4 * j + k) * P:(4 * j + k + 1) * P], c.ident[0:n, 0:n])
                        mm.then_inc(turned, 1)
                pe.wait_ge(small_in, 64)
                pe.transpose(c.bank_o[:, 0:80], b80[:, :], c.ident[0:80, 0:80])
                for k in range(KC):
                    pe.transpose(c.bank_o[:, 80 + 3 * k:83 + 3 * k], cw3[:, k * P:(k + 1) * P], c.ident[0:3, 0:3])
                for k in range(KC):
                    mm = pe.transpose(c.bank_o[:, 128 + 16 * k:144 + 16 * k], st16[:, k * P:(k + 1) * P],
                                      c.ident[0:16, 0:16])
                mm.then_inc(small_turned, 1)


HELD = {}


def hold(eng, sem, value):
    eng.wait_ge(sem, value)
    eng.sem_inc(HELD["waits_held"], 1)


class WeightTiles:

    def __init__(self, c, ctx, name, slots, per_round):
        self.slots, self.per_round = slots, per_round
        self.raw = c.sb(ctx, name + "_raw", [P, slots, KC, P])
        self.hi = c.sb(ctx, name + "_hi", [P, slots, KC, P], F32R)
        self.lo = c.sb(ctx, name + "_lo", [P, slots, KC, P], F32R)
        self.raw_in = [c.sem(f"{name}_raw_in{s}") for s in range(slots)]
        self.hi_ok, self.lo_ok = c.sem(name + "_hi_ok"), c.sem(name + "_lo_ok")

    def count(self, i, j):
        return i * self.per_round + j

    def start_pool(self, pool):
        pool.sem_inc(self.lo_ok, self.slots)

    def load(self, sp, i, j, src):
        s = j % self.slots
        sp.wait_ge(self.lo_ok, self.count(i, j) + 1)
        sp.dma_start(self.raw[:, s, :, :], src).then_inc(self.raw_in[s], 16)

    def split_hi(self, act, i, j):
        s = j % self.slots
        loads = i * (self.per_round // self.slots) + j // self.slots + 1
        act.wait_ge(self.raw_in[s], 16 * loads)
        act.activation(self.hi[:, s, :, :], self.raw[:, s, :, :], ACT.Copy).then_inc(self.hi_ok, 1)

    def split_lo(self, pool, i, j):
        s = j % self.slots
        pool.wait_ge(self.hi_ok, self.count(i, j) + 1)
        pool.tensor_tensor(self.lo[:, s, :, :], self.raw[:, s, :, :], self.hi[:, s, :, :].bitcast(F32),
                           ALU.subtract).then_inc(self.lo_ok, 1)

    def ready(self, pe, i, j):
        pe.wait_ge(self.lo_ok, self.count(i, j) + 1 + self.slots)

    def product(self, pe, j, out, right):
        s = j % self.slots
        return split_product(pe, out, (lambda k: self.hi[:, s, k, :], lambda k: self.lo[:, s, k, :]), right, KC)


def x_moving(c, c0, c1):
    return (lambda k: c.xh[:, k, c0:c1], lambda k: c.xl[:, k, c0:c1])


def conv_branch(c, d, yh, yl):
    nc = c.nc
    w_cols = d["w_in"][0].rearrange("(k p) (n e) -> p k n e", p=P, e=P)
    names = ["C", "h", "B", "z_c"]
    with ExitStack() as ctx:
        w = WeightTiles(c, ctx, "wc", 2, 4)
        cs = c.sb(ctx, "c_part", [P, TOK])
        up = c.sb(ctx, "u_prompt", [P, SAMPLE0])
        us = c.sb(ctx, "u_sample", [P, NB, DS + 2])
        tap = c.sb(ctx, "conv_out", [P, LIVE])
        sg = c.sb(ctx, "sig_z", [P, LIVE])
        yt = c.sb(ctx, "y_conv", [P, LIVE])
        last = c.sb(ctx, "last_u", [P, KC, 2 + NB * 2])
        last_rows = c.sb(ctx, "last_u_rows", [2 + NB * 2, D])

        full = c.sem("conv_bank_full")
        c_out = c.sem("c_out")
        d_out = c.sem("hbz_out")
        u_ok = c.sem("u_ok")
        tap_ok = c.sem("tap_ok")
        sig_ok = c.sem("sig_ok")
        y_ok = c.sem("y_ok")
        yh_ok = c.sem("yh_ok")
        yl_ok = c.sem("yl_ok")
        last_ok = c.sem("last_ok")
        last_turned = c.sem("last_turned")
        last_out = c.sem("last_out")
        stored = c.sem("conv_state_stored")
        banks = [c.bank_p[0], c.bank_p[1]]

        def bias(name, i):
            return c.bias[:, bass.ds(i + OFF[name] // P, 1)]

        with nc.Block() as block:
            @block.sync
            def _(sp):
                with sp.Fori(0, KC) as i:
                    for j, name in enumerate(names):
                        w.load(sp, i, j, w_cols[:, :, bass.ds(i + OFF[name] // P, 1), :])
                sp.wait_ge(last_out, 2)
                sp.dma_start(d["conv_prompt"][0, 0], last_rows[0:2, :]).then_inc(stored, 16)
                sp.dma_start(d["conv_sample"][0].rearrange("b j c -> (b j) c"), last_rows[2:18, :]).then_inc(stored, 16)
                sp.wait_ge(stored, 32)

            @block.gpsimd
            def _(pool):
                w.start_pool(pool)
                with pool.Fori(0, KC) as i:
                    for j in range(4):
                        w.split_lo(pool, i, j)

            @block.tensor
            def _(pe):
                with pe.Fori(0, KC) as i:
                    for j, name in enumerate(names):
                        w.ready(pe, i, j)
                        for n, (c0, c1) in enumerate(CH if name in "Ch" else CHL):
                            q = 3 * j + n
                            if q < 2:
                                pe.wait_ge(d_out, 9 * i + q + 1)
                            elif q < 5:
                                pe.wait_ge(c_out, 3 * i + q - 1)
                            else:
                                pe.wait_ge(d_out, 9 * i + q - 4 + 2)
                            mm = w.product(pe, j, banks[q % 2][:, 0:c1 - c0], x_moving(c, c0, c1))
                            mm.then_inc(full, 1)
                pe.wait_ge(last_ok, 2 * KC)
                for k in range(KC):
                    mm = pe.transpose(c.bank_z[0:18, k * P:(k + 1) * P], last[:, k, :], c.ident[:, :])
                mm.then_inc(last_turned, 1)

            @block.scalar
            def _(act):
                def one_block(i, more):
                    def rest_of_y(n):
                        c0, c1 = CHL[n]
                        hold(act, y_ok, 3 * i + n + 1)
                        act.activation(row(yh, i, c0 - META, c1 - META),
                                       yt[:, c0 - META:c1 - META], ACT.Copy).then_inc(yh_ok, 1)

                    for n, (c0, c1) in enumerate(CH):
                        hold(act, full, 12 * i + n + 1)
                        act.activation(cs[:, c0:c1], banks[n % 2][:, 0:c1 - c0], ACT.Identity,
                                       bias=bias("C", i)).then_inc(c_out, 1)
                    w.split_hi(act, i, 2)
                    act.wait_ge(full, 12 * i + 6)
                    w.split_hi(act, i, 3)
                    for n, (c0, c1) in enumerate(CHL):
                        q = 9 + n
                        hold(act, full, 12 * i + q + 1)
                        act.activation(sg[:, c0 - META:c1 - META], banks[q % 2][:, 0:c1 - c0], ACT.Sigmoid,
                                       bias=bias("z_c", i)).then_inc(sig_ok, 1)
                        if n == 0 and more:
                            w.split_hi(act, i + 1, 0)
                        if n:
                            rest_of_y(n - 1)
                    if more:
                        w.split_hi(act, i + 1, 1)
                    rest_of_y(2)

                w.split_hi(act, 0, 0)
                w.split_hi(act, 0, 1)
                with act.Fori(0, KC - 1) as i:
                    one_block(i, True)
                one_block(KC - 1, False)

            @block.vector
            def _(dve):
                dve.sem_inc(d_out, 2)

                def sample(t):
                    return t[:, SEQ:LIVE].rearrange("p (b j) -> p b j", j=DS)

                with dve.Fori(0, KC) as i:
                    dve.tensor_copy(us[:, :, 0:2], c.state[:, bass.ds(i, 1), :].rearrange("p o (b j) -> p (o b) j", j=2)
                                    ).then_inc(u_ok, 1)
                    for n, (c0, c1) in enumerate(CH):
                        q = 3 + n
                        dve.wait_ge(full, 12 * i + q + 1)
                        dve.wait_ge(c_out, 3 * i + n + 1)
                        e = min(c1, SAMPLE0)
                        mm = dve.scalar_tensor_tensor(out=up[:, c0:e], in0=banks[q % 2][:, 0:e - c0], scalar=bias("h", i),
                                                      in1=cs[:, c0:e], op0=ALU.add, op1=ALU.mult)
                        if n < 2:
                            mm.then_inc(d_out, 1)
                    mm.then_inc(u_ok, 1)
                    dve.scalar_tensor_tensor(out=us[:, :, 2:DS + 2],
                                             in0=banks[1][:, 256:384].rearrange("p (b j) -> p b j", j=DS),
                                             scalar=bias("h", i),
                                             in1=cs[:, SAMPLE0:TOK].rearrange("p (b j) -> p b j", j=DS),
                                             op0=ALU.add, op1=ALU.mult).then_inc(d_out, 1)
                    dve.wait_ge(u_ok, 2 * i + 2)
                    dve.wait_ge(d_out, 9 * i + 3 + 2)
                    for r in range(3):
                        wr = c.conv_w[:, bass.ds(i, 1), r:r + 1].rearrange("p a b -> p (a b)")
                        pairs = [(tap[:, 0:SEQ], up[:, META - 2 + r:SAMPLE0 - 2 + r]),
                                 (sample(tap), us[:, :, r:r + DS])]
                        if r:
                            dve.wait_ge(tap_ok, 6 * i + 2 * r)
                        for dst, src in pairs:
                            if r == 0:
                                dve.tensor_scalar(dst, src, wr, None, ALU.mult).then_inc(tap_ok, 1)
                            else:
                                dve.scalar_tensor_tensor(out=dst, in0=src, scalar=wr, in1=dst,
                                                         op0=ALU.mult, op1=ALU.add).then_inc(tap_ok, 1)
                    dve.tensor_copy(last[:, bass.ds(i, 1), 0:2].rearrange("p o j -> p (o j)"),
                                    up[:, SAMPLE0 - 2:SAMPLE0]).then_inc(last_ok, 1)
                    dve.tensor_copy(last[:, bass.ds(i, 1), 2:18].rearrange("p o (b j) -> p (o b) j", j=2),
                                    us[:, :, DS:DS + 2]).then_inc(last_ok, 1)
                    dve.wait_ge(tap_ok, 6 * i + 6)
                    for n, (c0, c1) in enumerate(CHL):
                        q = 6 + n
                        t = tap[:, c0 - META:c1 - META]
                        dve.wait_ge(full, 12 * i + q + 1)
                        dve.scalar_tensor_tensor(out=t, in0=banks[q % 2][:, 0:c1 - c0], scalar=bias("B", i), in1=t,
                                                 op0=ALU.add, op1=ALU.mult).then_inc(d_out, 1)
                    for n, (c0, c1) in enumerate(CHL):
                        q = 9 + n
                        a, b = c0 - META, c1 - META
                        dve.wait_ge(sig_ok, 3 * i + n + 1)
                        dve.scalar_tensor_tensor(out=sg[:, a:b], in0=banks[q % 2][:, 0:c1 - c0], scalar=bias("z_c", i),
                                                 in1=sg[:, a:b], op0=ALU.add, op1=ALU.mult).then_inc(d_out, 1)
                        dve.wait_ge(d_out, 9 * i + 7 + n + 2)
                        dve.tensor_tensor(yt[:, a:b], sg[:, a:b], tap[:, a:b], ALU.mult).then_inc(y_ok, 1)
                        dve.wait_ge(yh_ok, 3 * i + n + 1)
                        dve.tensor_tensor(row(yl, i, a, b), yt[:, a:b],
                                          row(yh, i, a, b).bitcast(F32), ALU.subtract).then_inc(yl_ok, 1)
                dve.wait_ge(last_turned, 1)
                dve.tensor_copy(last_rows[:, 0:512], c.bank_z[0:18, 0:512]).then_inc(last_out, 1)
                dve.tensor_copy(last_rows[:, 512:1024], c.bank_z[0:18, 512:1024]).then_inc(last_out, 1)


def conv_gates(c, d, yh, yl):
    nc = c.nc
    w_cols = d["w_in"][0].rearrange("(k p) (n e) -> p k n e", p=P, e=P)
    co_cols = d["w_conv_o"][0].rearrange("(k p) (n e) -> p k n e", p=P, e=P)
    with ExitStack() as ctx:
        w = WeightTiles(c, ctx, "wg", 3, 3)
        gate = c.sb(ctx, "gate_c", [P, LIVE])
        outs = c.sb(ctx, "gates_out", [P, 2, LIVE])
        full = c.sem("gate_bank_full")
        g_ok = c.sem("gate_c_ok")
        m_ok = c.sem("m1_ok")
        s_ok = c.sem("gate_s_ok")
        m_stored = c.sem("m1_stored")
        s_stored = c.sem("gate_s_stored")
        banks = [c.bank_p[0], c.bank_p[1], c.bank_o]

        def bias(name, i):
            return c.bias[:, bass.ds(i + OFF[name] // P, 1)]

        with nc.Block() as block:
            @block.sync
            def _(sp):
                sp.sem_inc(m_stored, 16)
                sp.sem_inc(s_stored, 16)

                def load(i):
                    w.load(sp, i, 0, w_cols[:, :, bass.ds(i + OFF["g_c"] // P, 1), :])
                    w.load(sp, i, 1, co_cols[:, :, bass.ds(i, 1), :])
                    w.load(sp, i, 2, w_cols[:, :, bass.ds(i + OFF["g_s"] // P, 1), :])

                def store(i):
                    sp.wait_ge(m_ok, 3 * i + 3)
                    sp.dma_start(d["m1"][bass.ds(i, 1)].rearrange("o p n -> (o p) n"), outs[:, 0, :]).then_inc(m_stored, 16)
                    sp.wait_ge(s_ok, 3 * i + 3 + 3)
                    sp.dma_start(d["sgate"][bass.ds(i, 1)].rearrange("o p n -> (o p) n"), outs[:, 1, :]).then_inc(s_stored, 16)

                load(0)
                with sp.Fori(0, KC - 1) as i:
                    load(i + 1)
                    store(i)
                store(KC - 1)
                sp.wait_ge(m_stored, 16 * (KC + 1))
                sp.wait_ge(s_stored, 16 * (KC + 1))

            @block.gpsimd
            def _(pool):
                w.start_pool(pool)
                with pool.Fori(0, KC) as i:
                    for j in range(3):
                        w.split_lo(pool, i, j)

            @block.tensor
            def _(pe):
                with pe.Fori(0, KC) as i:
                    for j in range(3):
                        w.ready(pe, i, j)
                        for n, (c0, c1) in enumerate(CHL):
                            if j == 0:
                                pe.wait_ge(s_ok, 3 * i + n + 1)
                            elif j == 1:
                                pe.wait_ge(g_ok, 3 * i + n + 1)
                            else:
                                pe.wait_ge(m_ok, 3 * i + n + 1)
                            right = x_moving(c, c0, c1) if j != 1 else (
                                lambda k: yh[:, k, c0 - META:c1 - META], lambda k: yl[:, k, c0 - META:c1 - META])
                            w.product(pe, j, banks[n][:, 0:c1 - c0], right).then_inc(full, 1)

            @block.scalar
            def _(act):
                act.sem_inc(s_ok, 3)
                def one_block(i, more):
                    for n, (c0, c1) in enumerate(CHL):
                        hold(act, full, 9 * i + n + 1)
                        act.activation(gate[:, c0 - META:c1 - META], banks[n][:, 0:c1 - c0], ACT.Sigmoid,
                                       bias=bias("g_c", i)).then_inc(g_ok, 1)
                    if more:
                        w.split_hi(act, i + 1, 0)
                        act.wait_ge(full, 9 * i + 6)
                        w.split_hi(act, i + 1, 1)
                    act.wait_ge(s_stored, 16 * i + 16)
                    for n, (c0, c1) in enumerate(CHL):
                        hold(act, full, 9 * i + 6 + n + 1)
                        act.activation(outs[:, 1, c0 - META:c1 - META], banks[n][:, 0:c1 - c0], ACT.Sigmoid,
                                       bias=bias("g_s", i)).then_inc(s_ok, 1)
                    if more:
                        w.split_hi(act, i + 1, 2)

                for j in range(3):
                    w.split_hi(act, 0, j)
                with act.Fori(0, KC - 1) as i:
                    one_block(i, True)
                one_block(KC - 1, False)

            @block.vector
            def _(dve):
                with dve.Fori(0, KC) as i:
                    dve.wait_ge(m_stored, 16 * i + 16)
                    for n, (c0, c1) in enumerate(CHL):
                        dve.wait_ge(full, 9 * i + 3 + n + 1)
                        dve.wait_ge(g_ok, 3 * i + n + 1)
                        dve.tensor_tensor(outs[:, 0, c0 - META:c1 - META], banks[n][:, 0:c1 - c0],
                                          gate[:, c0 - META:c1 - META], ALU.mult).then_inc(m_ok, 1)


UNITS = PT + 1
SAMPLE_UNIT = PT
NPROJ, NT, NPV = 13, 34, 15
FIRST_BANKS = TILES


def block_of(u):
    return PT - 1 - u


def width(u):
    return PAST + P if u == SAMPLE_UNIT else META + P * (block_of(u) + 1)


def value_groups(u):
    if u == SAMPLE_UNIT:
        return [["new"], [0, 1, 2, 3]]
    items = ["meta"] + list(range(block_of(u) + 1))
    return [items[i:i + 4] for i in range(0, len(items), 4)]


def first_group(u):
    return sum(len(value_groups(v)) for v in range(u))


def transpose_plan(project):
    order = []
    for slot in range(1, UNITS):
        if slot == SAMPLE_UNIT:
            order += [("k", b) for b in range(NB)]
        if project and slot >= 2:
            order.append(("x", slot - 2))
        order += [("a", slot - 1, g) for g in range(len(value_groups(slot - 1)))]
    if project:
        order += [("x", TILES - 3), ("x", TILES - 2)]
    order += [("a", SAMPLE_UNIT, g) for g in range(2)]
    if project:
        order.append(("x", TILES - 1))
        assert len(order) == NT
    return {key: n for n, key in enumerate(order)}


def attention(c, d):
    nc = c.nc
    w_cols = d["w_in"][0].rearrange("(k p) (n e) -> p k n e", p=P, e=P)
    b_cols = d["b_in"].rearrange("o (n e) -> o n e", e=P)
    cache_k = d["cache_k"][0].rearrange("b (n p) h d -> b p n h d", p=P)
    cache_v = d["cache_v"][0].rearrange("b (n p) h d -> b p n h d", p=P)
    plans = {True: transpose_plan(True), False: transpose_plan(False)}
    with ExitStack() as ctx:
        wz = WeightTiles(c, ctx, "wz", 1, 1)
        w3 = c.sb(ctx, "wqkv_raw", [P, KC, 3 * P])
        w3h = c.sb(ctx, "wqkv_hi", [P, KC, 3 * P], F32R)
        w3l = c.sb(ctx, "wqkv_lo", [P, KC, 3 * P], F32R)
        bias3 = c.sb(ctx, "bias_qkv", [P, 2, 3 * P])
        gain = c.sb(ctx, "qk_gain", [P, 2, P])
        qk = c.sb(ctx, "qk_turned", [P, 2, 2, TOK])
        v = c.sb(ctx, "v_rows", [P, 2, TILES, P])
        qkn = c.sb(ctx, "qk_rows", [P, 2, 2 * P])
        junk = c.sb(ctx, "squares2", [P, 2, P])
        ss = c.sb(ctx, "qk_sumsq", [P, 2, 2])
        ms = c.sb(ctx, "qk_meansq", [P, 2, 2])
        rs = c.sb(ctx, "qk_rstd", [P, 2, 2])
        half = c.sb(ctx, "minus_half2", [P, 2])
        beta = c.sb(ctx, "beta", [P, 2, SAMPLE0])
        keep = c.sb(ctx, "one_minus_beta", [P, 2, SAMPLE0])
        at = c.sb(ctx, "a_turned", [P, 2, 4 * P])
        kc = c.sb(ctx, "cache_k_rows", [P, 2, PAST // P, P])
        vc = c.sb(ctx, "cache_v_rows", [P, 2, PAST // P, P])
        kt = c.sb(ctx, "cache_k_turned", [P, 2, PAST])
        qbd = c.sb(ctx, "q_block_diagonal", [P, NB * (P + DS)])
        ot = c.sb(ctx, "o_turned", [P, LIVE])
        zs = c.sb(ctx, "silu_z", [P, LIVE])

        gain_in, half_ok = c.sem("gain_in"), c.sem("half_ok")
        w3_in, w3_hi, w3_lo = c.sem("wqkv_in"), c.sem("wqkv_hi_ok"), c.sem("wqkv_lo_ok")
        b3_in = [c.sem(f"bias_qkv_in{q}") for q in range(2)]
        proj_ok, proj_out = c.sem("proj_bank_full"), c.sem("proj_bank_out")
        t_full, t_out = c.sem("turn_bank_full"), c.sem("turn_bank_out")
        rows_ok, sq_ok, mean_ok, rstd_ok = c.sem("qk_rows_ok"), c.sem("qk_sq"), c.sem("qk_mean"), c.sem("qk_rstd_ok")
        norm_ok = c.sem("qk_norm_ok")
        k_stored = [c.sem(f"k_stored{s}") for s in range(2)]
        v_stored = [c.sem(f"v_stored{q}") for q in range(2)]
        score_ok, kq_ok = c.sem("scores_ok"), c.sem("cache_scores_ok")
        keep_ok, beta_ok = c.sem("keep_ok"), c.sem("beta_ok")
        scan_ok, a_ok = c.sem("scan_ok"), c.sem("a_ok")
        pv_ok, cache_pv, o_out = c.sem("value_group_ok"), c.sem("cache_values_ok"), c.sem("o_out")
        k_in = [c.sem(f"cache_k_in{s}") for s in range(2)]
        v_in = [c.sem(f"cache_v_in{s}") for s in range(2)]
        qbd_ok = c.sem("q_block_ok")
        zsig_ok, zs_ok = c.sem("z_sig_ok"), c.sem("z_silu_ok")
        y_ok, y_stored = c.sem("y_s_ok"), c.sem("y_s_stored")

        def rows_of(t):
            return META if t == META_TILE else P

        def turn_bank(h, plan, key):
            n = plan[key]
            return FIRST_BANKS + NT * h + n, c.bank_t[n % 2]

        def head_block(name, h):
            return bass.ds(h + OFF[name] // P, 1)

        with nc.Block() as block:
            @block.sync
            def _(sp):
                def load_qkv(h, q):
                    for j, name in enumerate("qkv"):
                        sp.dma_start(w3[:, :, j * P:(j + 1) * P], w_cols[:, :, head_block(name, h), :]).then_inc(w3_in, 16)
                    for j, name in enumerate("qkv"):
                        sp.dma_start(bias3[:, q, j * P:(j + 1) * P],
                                     b_cols[:, head_block(name, h), :].rearrange("o n e -> o (n e)").to_broadcast([P, P])
                                     ).then_inc(b3_in[q], 16)

                def load_k(h, b):
                    sp.dma_start(kc[:, b % 2, :, :], cache_k[b][:, :, bass.ds(h, 1), :].rearrange("p n o d -> p n (o d)")
                                 ).then_inc(k_in[b % 2], 16)

                def load_v(h, b):
                    sp.dma_start(vc[:, b % 2, :, :], cache_v[b][:, :, bass.ds(h, 1), :].rearrange("p n o d -> p n (o d)")
                                 ).then_inc(v_in[b % 2], 16)

                def store(h, q, t):
                    n = rows_of(t)
                    sp.wait_ge(norm_ok, TILES * h + t + 1)
                    if t == SAMPLE_TILE:
                        dk, dv = (d[x][0].rearrange("b s h d -> (b s) h d") for x in ("k_sample", "v_sample"))
                    else:
                        c0, c1 = tile_cols(t)
                        dk, dv = (d[x][0, 0, c0:c1] for x in ("k_prompt", "v_prompt"))
                    sp.dma_start(dk[:, bass.ds(h, 1), :].rearrange("t o d -> t (o d)"),
                                 qkn[0:n, t % 2, P:2 * P]).then_inc(k_stored[t % 2], 16)
                    sp.dma_start(dv[:, bass.ds(h, 1), :].rearrange("t o d -> t (o d)"),
                                 v[0:n, q, t, :]).then_inc(v_stored[q], 16)

                def head(h, par, nxt, nxt2):
                    plan = plans[nxt]
                    if nxt2:
                        sp.wait_ge(w3_lo, 2 * h + 4)
                        sp.wait_ge(proj_out, FIRST_BANKS + NPROJ * h + 2)
                        load_qkv(h + 2, par)
                        sp.wait_ge(wz.lo_ok, h + 2 + 1)
                        sp.dma_start(wz.raw[:, 0, :, :], w_cols[:, :, head_block("z_s", h + 2), :]).then_inc(wz.raw_in[0], 16)
                    if nxt:
                        for t in range(7):
                            store(h + 1, 1 - par, t)
                    for b in range(2, NB + 2):
                        if b < NB or nxt:
                            hold(sp, t_full, turn_bank(h, plan, ("k", b - 2))[0] + 1)
                            load_k(h if b < NB else h + 1, b % NB)
                    if nxt:
                        for t in range(7, TILES):
                            store(h + 1, 1 - par, t)
                    for b in range(2, NB + 2):
                        if b < NB or nxt:
                            hold(sp, cache_pv, NB * h + b - 2 + 1 + 1)
                            load_v(h if b < NB else h + 1, b % NB)
                    sp.wait_ge(y_ok, h + 1)
                    sp.dma_start(d["ys"][bass.ds(h, 1)].rearrange("o p n -> (o p) n"), zs[:, :]).then_inc(y_stored, 16)

                for s in range(2):
                    sp.sem_inc(k_stored[s], 16)
                    sp.sem_inc(v_stored[s], 16)
                sp.sem_inc(y_stored, 16)
                load_qkv(0, 0)
                sp.dma_start(gain[:, 0, :], d["q_norm_g"].to_broadcast([P, P])).then_inc(gain_in, 16)
                sp.dma_start(gain[:, 1, :], d["k_norm_g"].to_broadcast([P, P])).then_inc(gain_in, 16)
                sp.dma_start(wz.raw[:, 0, :, :], w_cols[:, :, OFF["z_s"] // P, :]).then_inc(wz.raw_in[0], 16)
                for b in range(2):
                    load_k(0, b)
                    load_v(0, b)
                sp.wait_ge(w3_lo, 2)
                load_qkv(1, 1)
                sp.wait_ge(wz.lo_ok, 1 + 1)
                sp.dma_start(wz.raw[:, 0, :, :], w_cols[:, :, OFF["z_s"] // P + 1, :]).then_inc(wz.raw_in[0], 16)
                for t in range(TILES):
                    store(0, 0, t)
                with sp.Fori(0, HEADS // 2 - 1) as i:
                    head(2 * i, 0, True, True)
                    head(2 * i + 1, 1, True, True)
                head(HEADS - 2, 0, True, False)
                head(HEADS - 1, 1, False, False)
                for s in range(2):
                    sp.wait_ge(k_stored[s], 16 * (HEADS * TILES // 2 + 1))
                    sp.wait_ge(v_stored[s], 16 * (HEADS * TILES // 2 + 1))
                sp.wait_ge(y_stored, 16 * (HEADS + 1))

            @block.gpsimd
            def _(pool):
                def rstd(h, t):
                    n, s = rows_of(t), t % 2
                    a = 1 if t == META_TILE else 0
                    hold(pool, sq_ok, TILES * h + t + 1)
                    pool.tensor_scalar(ms[0:n, s, a:2], ss[0:n, s, a:2], 1.0 / HD, EPS, ALU.mult, ALU.add).then_inc(mean_ok, 1)
                    pool.wait_ge(mean_ok, TILES * h + t + 1)
                    pool.tensor_tensor(rs[0:n, s, a:2], ms[0:n, s, a:2], half[0:n, a:2], ALU.pow).then_inc(rstd_ok, 1)

                def split_qkv_lo(h):
                    for j in range(2):
                        k = slice(4 * j, 4 * j + 4)
                        pool.wait_ge(w3_hi, 2 * h + j + 1)
                        pool.tensor_tensor(w3l[:, k, :], w3[:, k, :], w3h[:, k, :].bitcast(F32),
                                           ALU.subtract).then_inc(w3_lo, 1)

                def head(h, par, nxt):
                    pool.wait_ge(t_out, FIRST_BANKS + NT * h + 2)
                    hold(pool, kq_ok, NB * h + 2)
                    pool.tensor_copy(qbd[:, :].rearrange("p (b w) -> p b w", w=P + DS)[:, :, 0:DS],
                                     qk[:, par, 0, SAMPLE0:TOK].rearrange("p (b j) -> p b j", j=DS)).then_inc(qbd_ok, 1)
                    if nxt:
                        split_qkv_lo(h + 1)
                        rstd(h + 1, 0)
                        wz.split_lo(pool, h + 1, 0)
                        for t in range(1, TILES):
                            rstd(h + 1, t)

                wz.start_pool(pool)
                pool.memset(half[:, :], -0.5).then_inc(half_ok, 1)
                pool.memset(qbd[:, :], 0.0).then_inc(half_ok, 1)
                pool.wait_ge(half_ok, 2)
                split_qkv_lo(0)
                wz.split_lo(pool, 0, 0)
                for t in range(TILES):
                    rstd(0, t)
                with pool.Fori(0, HEADS // 2 - 1) as i:
                    head(2 * i, 0, True)
                    head(2 * i + 1, 1, True)
                head(HEADS - 2, 0, True)
                head(HEADS - 1, 1, False)

            @block.tensor
            def _(pe):
                def project(h, t, number):
                    n, (c0, c1) = rows_of(t), tile_cols(t)
                    a = P if t == META_TILE else 0
                    num, bank = number
                    if t == 0:
                        pe.wait_ge(w3_lo, 2 * h + 2)
                    pe.wait_ge(proj_out, num + 1)
                    split_product(pe, bank[0:n, a:3 * P], (lambda k: c.xh[:, k, c0:c1], lambda k: c.xl[:, k, c0:c1]),
                                  (lambda k: w3h[:, k, a:3 * P], lambda k: w3l[:, k, a:3 * P]), KC).then_inc(proj_ok, 1)

                def turn_rows(h, t, number):
                    n = rows_of(t)
                    num, bank = number
                    pe.wait_ge(norm_ok, TILES * h + t + 1)
                    (hold if t == META_TILE else type(pe).wait_ge)(pe, t_out, num + 1)
                    if t != META_TILE:
                        pe.transpose(bank[:, 0:P], qkn[0:n, t % 2, 0:P], c.ident[0:n, 0:n])
                    pe.transpose(bank[:, P:P + n], qkn[0:n, t % 2, P:2 * P], c.ident[0:n, 0:n]).then_inc(t_full, 1)

                def silu_gate(h, par, n):
                    c0, c1 = CHL[n]
                    num = FIRST_BANKS + NPROJ * h + n
                    if n == 0:
                        wz.ready(pe, h, 0)
                    pe.wait_ge(proj_out, num + 1)
                    wz.product(pe, 0, c.bank_p[(par + n) % 2][:, 0:c1 - c0], x_moving(c, c0, c1)).then_inc(proj_ok, 1)

                def scores(h, par, u):
                    pe.wait_ge(beta_ok, UNITS * h + u + 1)
                    b = block_of(u)
                    q = qk[:, par, 0, META + b * P:META + (b + 1) * P]
                    w, diag = width(u), META + b * P
                    for a in range(0, w, 512):
                        e = min(a + 512, w)
                        m0, m1 = max(a, diag), e
                        mm = pe.matmul(c.bank_z[:, a:e], q, qk[:, par, 1, a:e], start=True, stop=m0 >= m1)
                        if m0 < m1:
                            mm = pe.matmul(c.bank_z[:, m0:m1], c.identb[:, :], c.mask[:, m0 - diag:m1 - diag],
                                           start=False, stop=True)
                    mm.then_inc(score_ok, 1)

                def sample_scores(h, par, plan):
                    pe.wait_ge(beta_ok, UNITS * h + SAMPLE_UNIT + 1)
                    pe.wait_ge(qbd_ok, h + 1)
                    pe.matmul(c.bank_z[:, PAST:PAST + P], qk[:, par, 0, SAMPLE0:TOK], qk[:, par, 1, SAMPLE0:TOK],
                              start=True, stop=False)
                    pe.matmul(c.bank_z[:, PAST:PAST + P], c.identb[:, :], c.mask_s[:, :], start=False, stop=True)

                    def turn_cache(b):
                        num, bank = turn_bank(h, plan, ("k", b))
                        pe.wait_ge(k_in[b % 2], 16 * (NB // 2 * h + b // 2 + 1))
                        pe.wait_ge(t_out, num + 1)
                        for n in range(PAST // P):
                            mm = pe.transpose(bank[:, n * P:(n + 1) * P], kc[:, b % 2, n, :], c.ident[:, :])
                        mm.then_inc(t_full, 1)

                    turn_cache(0)
                    for b in range(NB):
                        if b + 1 < NB:
                            turn_cache(b + 1)
                        pe.wait_ge(t_out, turn_bank(h, plan, ("k", b))[0] + 1 + 2)
                        pe.matmul(c.bank_z[:, 0:PAST], qbd[:, b * P:(b + 1) * P], kt[:, b % 2, :],
                                  start=b == 0, stop=b == NB - 1).then_inc(kq_ok, 1)

                def values(h, par, u, plan):
                    n_unit = UNITS * h + u
                    groups = value_groups(u)
                    pe.wait_ge(a_ok, n_unit + 1)
                    slot = (par + u) % 2

                    def turn(g):
                        num, bank = turn_bank(h, plan, ("a", u, g))
                        pe.wait_ge(t_out, num + 1)
                        for m, item in enumerate(groups[g]):
                            if item == "meta":
                                src, n = beta[:, slot, 0:META], META
                            elif item == "new":
                                src, n = beta[:, slot, PAST:PAST + P], P
                            else:
                                a = item * P + (0 if u == SAMPLE_UNIT else META)
                                src, n = beta[:, slot, a:a + P], P
                            mm = pe.transpose(bank[0:n, m * P:(m + 1) * P], src, c.ident[:, :])
                        mm.then_inc(t_full, 1)

                    def weigh(g):
                        gg = first_group(u) + g
                        pe.wait_ge(t_out, turn_bank(h, plan, ("a", u, g))[0] + 1 + 2)
                        if g == 0:
                            pe.wait_ge(o_out, n_unit + 1)
                        if groups[g] == [0, 1, 2, 3] and u == SAMPLE_UNIT:
                            for b in range(NB):
                                pe.wait_ge(v_in[b % 2], 16 * (NB // 2 * h + b // 2 + 1))
                                for n in range(PAST // P):
                                    mm = pe.matmul(c.bank_o[:, b * DS:(b + 1) * DS], vc[:, b % 2, n, :],
                                                   at[:, gg % 2, n * P + b * DS:n * P + (b + 1) * DS], start=False,
                                                   stop=b == NB - 1 and n == PAST // P - 1, skip_group_check=True)
                                mm.then_inc(cache_pv, 1)
                            return
                        for m, item in enumerate(groups[g]):
                            t = {"meta": META_TILE, "new": SAMPLE_TILE}.get(item, item)
                            n = rows_of(t)
                            mm = pe.matmul(c.bank_o[:, 0:P], v[0:n, par, t, :], at[0:n, gg % 2, m * P:(m + 1) * P],
                                           start=g == 0 and m == 0,
                                           stop=u != SAMPLE_UNIT and g == len(groups) - 1 and m == len(groups[g]) - 1,
                                           skip_group_check=u == SAMPLE_UNIT)
                        mm.then_inc(pv_ok, 1)

                    turn(0)
                    for g in range(len(groups)):
                        if g + 1 < len(groups):
                            turn(g + 1)
                        weigh(g)

                def head(h, par, nxt):
                    plan = plans[nxt]
                    first = FIRST_BANKS + NPROJ * h

                    def project_next(t):
                        if nxt:
                            project(h + 1, t, (first + 3 + t, c.bank_p[(par + 3 + t) % 2]))

                    def turn_next(t):
                        if nxt:
                            turn_rows(h + 1, t, turn_bank(h, plan, ("x", t)))

                    pe.wait_ge(t_out, FIRST_BANKS + NT * h + 2)
                    scores(h, par, 0)
                    for n in range(3):
                        silu_gate(h, par, n)
                    for u in range(1, UNITS):
                        if u == SAMPLE_UNIT:
                            sample_scores(h, par, plan)
                        else:
                            scores(h, par, u)
                        project_next(u - 1)
                        if u >= 2:
                            turn_next(u - 2)
                        values(h, par, u - 1, plan)
                    project_next(TILES - 2)
                    turn_next(TILES - 3)
                    project_next(TILES - 1)
                    turn_next(TILES - 2)
                    values(h, par, SAMPLE_UNIT, plan)
                    turn_next(TILES - 1)

                pe.sem_inc(kq_ok, 2)
                pe.sem_inc(pv_ok, 1)
                pe.sem_inc(cache_pv, 1)
                for t in range(TILES):
                    project(0, t, (t, c.bank_p[t % 2]))
                    if t:
                        turn_rows(0, t - 1, (t - 1, c.bank_t[(t - 1) % 2]))
                turn_rows(0, TILES - 1, (TILES - 1, c.bank_t[(TILES - 1) % 2]))
                with pe.Fori(0, HEADS // 2 - 1) as i:
                    head(2 * i, 0, True)
                    head(2 * i + 1, 1, True)
                head(HEADS - 2, 0, True)
                head(HEADS - 1, 1, False)

            @block.scalar
            def _(act):
                def split_qkv_hi(h):
                    act.wait_ge(w3_in, 48 * (h + 1))
                    for j in range(2):
                        k = slice(4 * j, 4 * j + 4)
                        act.activation(w3h[:, k, :], w3[:, k, :], ACT.Copy).then_inc(w3_hi, 1)

                def squares(h, t):
                    n, s = rows_of(t), t % 2
                    act.wait_ge(rows_ok, TILES * h + t + 1)
                    for j in range(1 if t == META_TILE else 0, 2):
                        mm = act.activation(junk[0:n, j, :], qkn[0:n, s, j * P:(j + 1) * P], ACT.Square,
                                            accum_out=ss[0:n, s, j:j + 1])
                    mm.then_inc(sq_ok, 1)

                def copy_rows(q, t, number):
                    n, (c0, c1) = rows_of(t), tile_cols(t)
                    num, bank = number
                    act.wait_ge(t_full, num + 1)
                    if t == META_TILE:
                        act.activation(qk[:, q, 1, c0:c1], bank[:, P:P + n], ACT.Copy).then_inc(t_out, 1)
                    else:
                        act.activation(qk[:, q, :, c0:c1], bank[:, 0:2 * P].rearrange("p (a n) -> p a n", a=2),
                                       ACT.Copy).then_inc(t_out, 1)

                def betas(h, par, u, plan):
                    slot, w = (par + u) % 2, width(u)
                    if u == SAMPLE_UNIT:
                        for b in range(NB):
                            num, bank = turn_bank(h, plan, ("k", b))
                            act.wait_ge(t_full, num + 1)
                            act.wait_ge(kq_ok, NB * h + b + 1)
                            act.activation(kt[:, b % 2, :], bank[:, :], ACT.Copy).then_inc(t_out, 1)
                        act.wait_ge(kq_ok, NB * h + NB + 2)
                    else:
                        act.wait_ge(score_ok, PT * h + u + 1)
                    act.activation(keep[:, slot, 0:w], c.bank_z[:, 0:w], ACT.Sigmoid, scale=-SCALE).then_inc(keep_ok, 1)
                    act.activation(beta[:, slot, 0:w], c.bank_z[:, 0:w], ACT.Sigmoid, scale=SCALE).then_inc(beta_ok, 1)

                def copy_a(h, u, plan):
                    for g, items in enumerate(value_groups(u)):
                        gg = first_group(u) + g
                        num, bank = turn_bank(h, plan, ("a", u, g))
                        act.wait_ge(t_full, num + 1)
                        if gg == 1:
                            act.wait_ge(cache_pv, NB * h + 1)
                        elif gg == 0:
                            act.wait_ge(pv_ok, NPV * h + 1)
                        else:
                            act.wait_ge(pv_ok, NPV * h + gg - 1 + 1)
                        a = 0
                        if items[0] == "meta":
                            a = P
                            act.activation(at[0:META, gg % 2, 0:P], bank[0:META, 0:P], ACT.Copy)
                        act.activation(at[:, gg % 2, a:len(items) * P], bank[:, a:len(items) * P], ACT.Copy).then_inc(t_out, 1)

                def z_sigmoid(h, par, n):
                    c0, c1 = CHL[n]
                    if n == 0:
                        act.wait_ge(y_stored, 16 * h + 16)
                    hold(act, proj_ok, FIRST_BANKS + NPROJ * h + n + 1)
                    act.activation(zs[:, c0 - META:c1 - META], c.bank_p[(par + n) % 2][:, 0:c1 - c0], ACT.Sigmoid,
                                   bias=c.bias[:, head_block("z_s", h)]).then_inc(zsig_ok, 1)

                def head(h, par, nxt):
                    plan = plans[nxt]

                    def rows_next(t):
                        if nxt:
                            copy_rows(1 - par, t, turn_bank(h, plan, ("x", t)))

                    def squares_next(t):
                        if nxt:
                            squares(h + 1, t)

                    if nxt:
                        act.wait_ge(proj_ok, FIRST_BANKS + NPROJ * h)
                        split_qkv_hi(h + 1)
                    betas(h, par, 0, plan)
                    for n in range(3):
                        z_sigmoid(h, par, n)
                    for u in range(1, UNITS):
                        betas(h, par, u, plan)
                        if u >= 2:
                            rows_next(u - 2)
                        copy_a(h, u - 1, plan)
                        squares_next(u - 1)
                        if u == 1 and nxt:
                            wz.split_hi(act, h + 1, 0)
                    rows_next(TILES - 3)
                    squares_next(TILES - 2)
                    squares_next(TILES - 1)
                    rows_next(TILES - 2)
                    copy_a(h, SAMPLE_UNIT, plan)
                    rows_next(TILES - 1)

                act.sem_inc(t_out, 2)
                act.sem_inc(beta_ok, 1)
                split_qkv_hi(0)
                wz.split_hi(act, 0, 0)
                for t in range(TILES):
                    squares(0, t)
                    if t:
                        copy_rows(0, t - 1, (t - 1, c.bank_t[(t - 1) % 2]))
                copy_rows(0, TILES - 1, (TILES - 1, c.bank_t[(TILES - 1) % 2]))
                with act.Fori(0, HEADS // 2 - 1) as i:
                    head(2 * i, 0, True)
                    head(2 * i + 1, 1, True)
                head(HEADS - 2, 0, True)
                head(HEADS - 1, 1, False)

            @block.vector
            def _(dve):
                def rows(h, q, pairs, t, number):
                    n, s = rows_of(t), t % 2
                    a = P if t == META_TILE else 0
                    num, bank = number
                    dve.wait_ge(proj_ok, num + 1)
                    if t == 0:
                        dve.wait_ge(b3_in[q], 48 * (pairs + 1))
                        dve.wait_ge(v_stored[q], 16 * TILES * pairs + 16)
                    dve.wait_ge(k_stored[s], 16 * (TILES // 2) * h + 16 * (t // 2) + 16)
                    dve.tensor_tensor(qkn[0:n, s, a:2 * P], bank[0:n, a:2 * P], bias3[0:n, q, a:2 * P],
                                      ALU.add).then_inc(rows_ok, 1)
                    dve.tensor_tensor(v[0:n, q, t, :], bank[0:n, 2 * P:3 * P], bias3[0:n, q, 2 * P:3 * P],
                                      ALU.add).then_inc(proj_out, 1)

                def normalise(h, t):
                    n, s = rows_of(t), t % 2
                    dve.wait_ge(rstd_ok, TILES * h + t + 1)
                    for j in range(1 if t == META_TILE else 0, 2):
                        mm = dve.scalar_tensor_tensor(out=qkn[0:n, s, j * P:(j + 1) * P], in0=qkn[0:n, s, j * P:(j + 1) * P],
                                                      scalar=rs[0:n, s, j:j + 1], in1=gain[0:n, j, :],
                                                      op0=ALU.mult, op1=ALU.mult)
                    mm.then_inc(norm_ok, 1)

                def sticks(h, par, u):
                    slot, w, n = (par + u) % 2, width(u), UNITS * h + u
                    dve.wait_ge(keep_ok, n + 1)
                    young_first = keep[:, slot, 0:w][:, ::-1]
                    dve.tensor_tensor_scan(young_first, young_first, young_first, 1.0,
                                           ALU.mult, ALU.bypass).then_inc(scan_ok, 1)
                    dve.wait_ge(scan_ok, n + 1)
                    dve.wait_ge(beta_ok, n + 1 + 1)
                    dve.tensor_tensor(beta[:, slot, 0:w - 1], beta[:, slot, 0:w - 1], keep[:, slot, 1:w],
                                      ALU.mult).then_inc(a_ok, 1)

                def take_o(h, u):
                    if u == SAMPLE_UNIT:
                        a = SEQ
                        dve.wait_ge(cache_pv, NB * h + NB + 1)
                    else:
                        a = block_of(u) * P
                        dve.wait_ge(pv_ok, NPV * h + first_group(u + 1) + 1)
                    dve.tensor_copy(ot[:, a:a + P], c.bank_o[:, 0:P]).then_inc(o_out, 1)

                def z_silu(h, par, n):
                    c0, c1 = CHL[n]
                    z = zs[:, c0 - META:c1 - META]
                    dve.wait_ge(zsig_ok, 3 * h + n + 1)
                    dve.scalar_tensor_tensor(out=z, in0=c.bank_p[(par + n) % 2][:, 0:c1 - c0],
                                             scalar=c.bias[:, head_block("z_s", h)], in1=z,
                                             op0=ALU.add, op1=ALU.mult).then_inc(proj_out, 1)

                def head(h, par, pairs, nxt):
                    first = FIRST_BANKS + NPROJ * h

                    def rows_next(t):
                        if nxt:
                            rows(h + 1, 1 - par, pairs + par, t, (first + 3 + t, c.bank_p[(par + 3 + t) % 2]))

                    def normalise_next(t):
                        if nxt:
                            normalise(h + 1, t)

                    sticks(h, par, 0)
                    for n in range(3):
                        z_silu(h, par, n)
                    for u in range(1, UNITS):
                        sticks(h, par, u)
                        rows_next(u - 1)
                        take_o(h, u - 1)
                        normalise_next(u - 1)
                    rows_next(TILES - 2)
                    normalise_next(TILES - 2)
                    rows_next(TILES - 1)
                    normalise_next(TILES - 1)
                    take_o(h, SAMPLE_UNIT)
                    dve.wait_ge(o_out, UNITS * h + UNITS + 1)
                    dve.tensor_tensor(zs[:, :], zs[:, :], ot[:, :], ALU.mult).then_inc(y_ok, 1)

                dve.sem_inc(proj_out, 2)
                dve.sem_inc(o_out, 1)
                dve.wait_ge(gain_in, 32)
                for t in range(TILES):
                    rows(0, 0, 0, t, (t, c.bank_p[t % 2]))
                    normalise(0, t)
                with dve.Fori(0, HEADS // 2 - 1) as i:
                    head(2 * i, 0, i, True)
                    head(2 * i + 1, 1, i, True)
                head(HEADS - 2, 0, HEADS // 2 - 1, True)
                head(HEADS - 1, 1, HEADS // 2 - 1, False)


def merge(c, d, mh, ml):
    nc = c.nc
    so_cols = d["w_sb_o"][0].rearrange("(k p) (n e) -> p k n e", p=P, e=P)
    with ExitStack() as ctx:
        w = WeightTiles(c, ctx, "ws", 2, 2)
        yr = c.sb(ctx, "y_s_raw", [P, 2, LIVE])
        yh = c.sb(ctx, "y_s_hi", [P, KC, LIVE], F32R)
        yl = c.sb(ctx, "y_s_lo", [P, KC, LIVE], F32R)
        sg = c.sb(ctx, "gate_s", [P, 2, LIVE])
        m1 = c.sb(ctx, "m_part", [P, 2, LIVE])
        y_in = [c.sem(f"y_s_in{s}") for s in range(2)]
        yh_ok, yl_ok = c.sem("y_s_hi_ok"), c.sem("y_s_lo_ok")
        g_in = [c.sem(f"gate_s_in{s}") for s in range(2)]
        m_in = [c.sem(f"m_part_in{s}") for s in range(2)]
        full = c.sem("so_bank_full")
        gated, summed = c.sem("so_gated"), c.sem("m_summed")
        mh_ok, ml_ok = c.sem("m_hi_ok"), c.sem("m_lo_ok")
        banks = [c.bank_p[0], c.bank_p[1], c.bank_o, c.bank_z[:, 0:512], c.bank_z[:, 512:1024], c.bank_z[:, 1024:1536]]

        with nc.Block() as block:
            @block.sync
            def _(sp):
                w.load(sp, 0, 0, so_cols[:, :, 0, :])
                for k in range(KC):
                    if k >= 2:
                        sp.wait_ge(yl_ok, k - 1)
                    sp.dma_start(yr[:, k % 2, :], d["ys"][k]).then_inc(y_in[k % 2], 16)
                w.load(sp, 0, 1, so_cols[:, :, 1, :])

                def one_pair(i, more):
                    for s in range(2):
                        sp.wait_ge(ml_ok, 2 * i + s + 1)
                        sp.dma_start(sg[:, s, :], d["sgate"][bass.ds(2 * i + s, 1)].rearrange("o p n -> (o p) n")).then_inc(g_in[s], 16)
                        sp.dma_start(m1[:, s, :], d["m1"][bass.ds(2 * i + s, 1)].rearrange("o p n -> (o p) n")).then_inc(m_in[s], 16)
                        if more:
                            w.load(sp, i + 1, s, so_cols[:, :, bass.ds(2 * i + 2 + s, 1), :])

                with sp.Fori(0, KC // 2 - 1) as i:
                    one_pair(i, True)
                one_pair(KC // 2 - 1, False)

            @block.gpsimd
            def _(pool):
                w.start_pool(pool)
                with pool.Fori(0, KC // 2) as i:
                    for s in range(2):
                        w.split_lo(pool, i, s)

            @block.scalar
            def _(act):
                for k in range(KC):
                    act.wait_ge(y_in[k % 2], 16 * (k // 2 + 1))
                    act.activation(yh[:, k, :], yr[:, k % 2, :], ACT.Copy).then_inc(yh_ok, 1)
                    if k == 0:
                        w.split_hi(act, 0, 0)
                w.split_hi(act, 0, 1)

                def one_pair(i, more):
                    for s in range(2):
                        if more:
                            act.wait_ge(full, 6 * i + 3 * s + 3)
                            w.split_hi(act, i + 1, s)
                        hold(act, summed, 6 * i + 3 * s + 3)
                        act.activation(row(mh, 2 * i + s, 0, LIVE), m1[:, s, :], ACT.Copy).then_inc(mh_ok, 1)

                with act.Fori(0, KC // 2 - 1) as i:
                    one_pair(i, True)
                one_pair(KC // 2 - 1, False)

            @block.vector
            def _(dve):
                dve.sem_inc(ml_ok, 2)
                dve.sem_inc(gated, 6)
                for k in range(KC):
                    dve.wait_ge(yh_ok, k + 1)
                    dve.tensor_tensor(yl[:, k, :], yr[:, k % 2, :], yh[:, k, :].bitcast(F32), ALU.subtract).then_inc(yl_ok, 1)
                with dve.Fori(0, KC // 2) as i:
                    for s in range(2):
                        dve.wait_ge(g_in[s], 16 * i + 16)
                        dve.wait_ge(m_in[s], 16 * i + 16)
                        for n, (c0, c1) in enumerate(CHL):
                            a, b = c0 - META, c1 - META
                            dve.wait_ge(full, 6 * i + 3 * s + n + 1)
                            dve.tensor_tensor(sg[:, s, a:b], banks[3 * s + n][:, 0:b - a], sg[:, s, a:b], ALU.mult).then_inc(gated, 1)
                            dve.wait_ge(gated, 6 * i + 3 * s + n + 1 + 6)
                            dve.tensor_tensor(m1[:, s, a:b], m1[:, s, a:b], sg[:, s, a:b], ALU.add).then_inc(summed, 1)
                        dve.wait_ge(mh_ok, 2 * i + s + 1)
                        dve.tensor_tensor(row(ml, 2 * i + s, 0, LIVE), m1[:, s, :],
                                          row(mh, 2 * i + s, 0, LIVE).bitcast(F32), ALU.subtract).then_inc(ml_ok, 1)

            @block.tensor
            def _(pe):
                pe.wait_ge(yl_ok, KC)
                with pe.Fori(0, KC // 2) as i:
                    for s in range(2):
                        w.ready(pe, i, s)
                        for n, (c0, c1) in enumerate(CHL):
                            a, b = c0 - META, c1 - META
                            pe.wait_ge(gated, 6 * i + 3 * s + n + 1)
                            w.product(pe, s, banks[3 * s + n][:, 0:b - a],
                                      (lambda k: yh[:, k, a:b], lambda k: yl[:, k, a:b])).then_inc(full, 1)


def output(c, d, mh, ml):
    nc = c.nc
    o_cols = d["w_o"][0].rearrange("(k p) (n e) -> p k n e", p=P, e=P)
    x_tiles = d["x_prompt"][0].rearrange("(t p) (n e) -> p t n e", p=P, e=P)
    y_tiles = d["y_prompt"][0].rearrange("(t p) (n e) -> p t n e", p=P, e=P)
    xs_rows = d["x_sample"].rearrange("b s (n e) -> (b s) n e", e=P)
    ys_rows = d["y_sample"].rearrange("b s (n e) -> (b s) n e", e=P)
    groups = [(0, 4), (4, 8), (8, 9)]
    with ExitStack() as ctx:
        w = WeightTiles(c, ctx, "wo", 2, 2)
        xt = c.sb(ctx, "x_again", [P, 2, PT + 1, P])
        yt = c.sb(ctx, "y_turned", [P, 2, LIVE])
        yo = c.sb(ctx, "y_rows", [P, 2, PT + 1, P])
        x_in = [c.sem(f"x_again_in{s}") for s in range(2)]
        full = c.sem("o_bank_full")
        copied = c.sem("o_copied")
        turned = c.sem("o_turned")
        added = c.sem("o_added")
        stored = [c.sem(f"y_stored{s}") for s in range(2)]
        banks = [c.bank_p[0], c.bank_p[1], c.bank_o]
        tbanks = [c.bank_t[0], c.bank_t[1], c.bank_z[:, 0:512]]

        with nc.Block() as block:
            @block.sync
            def _(sp):
                def load_x(i, s):
                    n = bass.ds(2 * i + s, 1)
                    sp.dma_start(xt[:, s, 0:PT, :], x_tiles[:, :, n, :].rearrange("p t o e -> p t (o e)")).then_inc(x_in[s], 16)
                    sp.dma_start(xt[:, s, PT, :], xs_rows[:, n, :].rearrange("p o e -> p (o e)")).then_inc(x_in[s], 16)

                def one_pair(i, more):
                    for s in range(2):
                        n = bass.ds(2 * i + s, 1)
                        if more:
                            w.load(sp, i + 1, s, o_cols[:, :, bass.ds(2 * i + 2 + s, 1), :])
                        sp.wait_ge(added, 6 * i + 3 * s + 3 + 6)
                        sp.dma_start(y_tiles[:, :, n, :].rearrange("p t o e -> p t (o e)"), yo[:, s, 0:PT, :]).then_inc(stored[s], 16)
                        sp.dma_start(ys_rows[:, n, :].rearrange("p o e -> p (o e)"), yo[:, s, PT, :]).then_inc(stored[s], 16)
                        if more:
                            load_x(i + 1, s)

                for s in range(2):
                    sp.sem_inc(stored[s], 32)
                    w.load(sp, 0, s, o_cols[:, :, s, :])
                    load_x(0, s)
                with sp.Fori(0, KC // 2 - 1) as i:
                    one_pair(i, True)
                one_pair(KC // 2 - 1, False)
                for s in range(2):
                    sp.wait_ge(stored[s], 32 * (KC // 2 + 1))

            @block.gpsimd
            def _(pool):
                w.start_pool(pool)
                with pool.Fori(0, KC // 2) as i:
                    w.split_lo(pool, i, 0)
                    w.split_lo(pool, i, 1)

            @block.scalar
            def _(act):
                w.split_hi(act, 0, 0)
                w.split_hi(act, 0, 1)

                def one_pair(i, more):
                    for s in range(2):
                        for n, (c0, c1) in enumerate(CHL):
                            act.wait_ge(full, 6 * i + 3 * s + n + 1)
                            act.activation(yt[:, s, c0 - META:c1 - META], banks[n][:, 0:c1 - c0], ACT.Copy).then_inc(copied, 1)
                        if more:
                            w.split_hi(act, i + 1, s)

                with act.Fori(0, KC // 2 - 1) as i:
                    one_pair(i, True)
                one_pair(KC // 2 - 1, False)

            @block.vector
            def _(dve):
                dve.sem_inc(added, 6)
                with dve.Fori(0, KC // 2) as i:
                    for s in range(2):
                        dve.wait_ge(x_in[s], 32 * i + 32)
                        dve.wait_ge(stored[s], 32 * i + 32)
                        for g, (a, b) in enumerate(groups):
                            dve.wait_ge(turned, 6 * i + 3 * s + g + 1)
                            dve.tensor_tensor(yo[:, s, a:b, :], tbanks[g][:, 0:(b - a) * P].rearrange("p (t e) -> p t e", e=P),
                                              xt[:, s, a:b, :], ALU.add).then_inc(added, 1)

            @block.tensor
            def _(pe):
                def product(i, s, first=False):
                    w.ready(pe, i, s)
                    for n, (c0, c1) in enumerate(CHL):
                        a, b = c0 - META, c1 - META
                        if not first:
                            pe.wait_ge(copied, 6 * i + 3 * s + n + 1 - 3)
                        w.product(pe, s, banks[n][:, 0:b - a],
                                  (lambda k: mh[:, k, a:b], lambda k: ml[:, k, a:b])).then_inc(full, 1)

                def turn(i, s):
                    for g, (a, b) in enumerate(groups):
                        pe.wait_ge(copied, 6 * i + 3 * s + (2, 3, 3)[g])
                        pe.wait_ge(added, 6 * i + 3 * s + g + 1 + 3)
                        for t in range(a, b):
                            mm = pe.transpose(tbanks[g][:, (t - a) * P:(t - a + 1) * P], yt[:, s, t * P:(t + 1) * P],
                                              c.ident[:, :])
                        mm.then_inc(turned, 1)

                product(0, 0, first=True)
                with pe.Fori(0, KC // 2 - 1) as i:
                    product(i, 1)
                    turn(i, 0)
                    product(i + 1, 0)
                    turn(i, 1)
                product(KC // 2 - 1, 1)
                turn(KC // 2 - 1, 0)
                turn(KC // 2 - 1, 1)


def build(nc, d):
    d["m1"] = nc.dram_tensor("m_part_scratch", (KC, P, LIVE), F32).ap()
    d["sgate"] = nc.dram_tensor("gate_scratch", (KC, P, LIVE), F32).ap()
    d["ys"] = nc.dram_tensor("y_s_scratch", (HEADS, P, LIVE), F32).ap()
    with ExitStack() as ctx:
        c = Core(nc, ctx)
        HELD["waits_held"] = c.sem("waits_held")
        c.bank_z = ctx.enter_context(nc.psum_tensor("bank_z", [P, 3 * 512], F32))
        c.bank_p = [ctx.enter_context(nc.psum_tensor(f"bank_p{i}", [P, 512], F32)) for i in range(2)]
        c.bank_t = [ctx.enter_context(nc.psum_tensor(f"bank_t{i}", [P, 512], F32)) for i in range(2)]
        c.bank_o = ctx.enter_context(nc.psum_tensor("bank_o", [P, 512], F32))
        c.ident, c.identb = c.sb(ctx, "ident", [P, P]), c.sb(ctx, "ident_bf16", [P, P], BF16)
        c.mask, c.mask_s = c.sb(ctx, "mask", [P, P], BF16), c.sb(ctx, "mask_samples", [P, P], BF16)
        c.bias = c.sb(ctx, "bias_turned", [P, 80])
        with ExitStack() as xs:
            c.xh = c.sb(xs, "x_hi", [P, KC, TOK], F32R)
            c.xl = c.sb(xs, "x_lo", [P, KC, TOK], F32R)
            with ExitStack() as ys:
                c.conv_w = c.sb(ys, "conv_w_turned", [P, KC, 3])
                c.state = c.sb(ys, "state_turned", [P, KC, 2 * NB])
                constants_and_norm(c, d)
                yh = c.sb(ys, "y_c_hi", [P, KC, LIVE], F32R)
                yl = c.sb(ys, "y_c_lo", [P, KC, LIVE], F32R)
                conv_branch(c, d, yh, yl)
                conv_gates(c, d, yh, yl)
            attention(c, d)
        mh = c.sb(ctx, "m_hi", [P, KC, LIVE], F32R)
        ml = c.sb(ctx, "m_lo", [P, KC, LIVE], F32R)
        merge(c, d, mh, ml)
        output(c, d, mh, ml)


INPUTS = ["x_prompt", "x_sample", "cache_k", "cache_v", "state_conv", "meta_tokens", "norm_g", "w_in", "b_in",
          "q_norm_g", "k_norm_g", "conv_w", "w_conv_o", "w_sb_o", "w_o"]
OUTPUTS = [("y_prompt", (1, SEQ, D)), ("y_sample", (NB, DS, D)), ("k_prompt", (1, 1, SAMPLE0, HEADS, HD)),
           ("v_prompt", (1, 1, SAMPLE0, HEADS, HD)), ("conv_prompt", (1, 1, 2, D)),
           ("k_sample", (1, NB, DS, HEADS, HD)), ("v_sample", (1, NB, DS, HEADS, HD)), ("conv_sample", (1, NB, 2, D))]


def kernel(**inputs):
    import numpy as np
    import concourse.bacc as bacc
    from concourse.bass_utils import run_bass_kernel_spmd as run

    nc = bacc.Bacc("TRN2", target_bir_lowering=False, num_devices=1)
    arrays, d = {}, {}
    for name in INPUTS:
        a = np.ascontiguousarray(inputs[name])
        arrays["in_" + name] = a
        d[name] = nc.dram_tensor("in_" + name, a.shape, mybir.dt.from_np(a.dtype), kind="ExternalInput").ap()
    for name, shape in OUTPUTS:
        d[name] = nc.dram_tensor("out_" + name, shape, F32, kind="ExternalOutput").ap()
    build(nc, d)
    r = run(nc, [arrays], core_ids=[0])
    return tuple(r.results[0]["out_" + name] for name, _ in OUTPUTS)
```

```python
from contextlib import ExitStack

import concourse.bass as bass
from concourse import mybir

F32 = mybir.dt.float32
F32R = mybir.dt.float32r
BF16 = mybir.dt.bfloat16
ALU = mybir.AluOpType
ACT = mybir.ActivationFunctionType

P = 128
D = 1024
KC = D // P
META, SEQ, NB, DS, PAST = 16, 1024, 8, 16, 512
HEADS, HD = 8, 128
PT = SEQ // P
SAMPLE0 = META + SEQ
TOK = SAMPLE0 + NB * DS
LIVE = TOK - META
TILES = PT + 2
SAMPLE_TILE, META_TILE = PT, PT + 1
EPS = 1e-6
SCALE = HD ** -0.5
HIDDEN = -1e30
OFF = {n: i * D for i, n in enumerate(["B", "C", "h", "z_c", "q", "k", "v", "z_s", "g_c", "g_s"])}
CH = [(0, META + 384), (META + 384, META + 768), (META + 768, TOK)]
CHL = [(META, META + 384), (META + 384, META + 768), (META + 768, TOK)]


def tile_cols(t):
    if t == META_TILE:
        return 0, META
    return META + t * P, META + (t + 1) * P


def row(t, i, a, b):
    return t[:, bass.ds(i, 1), a:b].rearrange("p o n -> p (o n)")


def split_product(pe, out, left, right, n, first=True, last=True):
    (lh, ll), (rh, rl) = left, right
    for k in range(n):
        pe.matmul(out, lh(k), rh(k), start=first and k == 0, stop=False)
        pe.matmul(out, lh(k), rl(k), start=False, stop=False)
        mm = pe.matmul(out, ll(k), rh(k), start=False, stop=last and k == n - 1)
    return mm


class Core:

    def __init__(self, nc, ctx):
        self.nc, self.ctx = nc, ctx

    def sem(self, name):
        return self.ctx.enter_context(self.nc.semaphore(name))

    def sb(self, ctx, name, shape, dt=F32):
        return ctx.enter_context(self.nc.sbuf_tensor(name, shape, dt))


def constants_and_norm(c, d):
    nc = c.nc
    with ExitStack() as ctx:
        gb = c.sb(ctx, "norm_gain", [P, D])
        b80 = c.sb(ctx, "bias_rows", [80, P])
        cw3 = c.sb(ctx, "conv_w_rows", [3, D])
        st16 = c.sb(ctx, "state_rows", [NB * 2, D])
        xr = c.sb(ctx, "x_rows", [P, 3, D])
        junk = c.sb(ctx, "squares", [P, D])
        xn = c.sb(ctx, "x_normed", [P, 2, D])
        ss = c.sb(ctx, "sumsq", [P, TILES])
        ms = c.sb(ctx, "meansq", [P, TILES])
        rs = c.sb(ctx, "rstd", [P, TILES])
        half = c.sb(ctx, "minus_half", [P, TILES])

        x_in = [c.sem(f"x_in{i}") for i in range(3)]
        small_in = c.sem("small_in")
        made = c.sem("constants_made")
        squared = c.sem("x_squared")
        mean_ok = c.sem("x_mean")
        rstd_ok = c.sem("x_rstd")
        normed = c.sem("x_is_normed")
        turned = c.sem("x_turned")
        hi_ok = c.sem("x_hi")
        lo_ok = c.sem("x_lo")
        small_turned = c.sem("small_turned")
        small_out = c.sem("small_out")

        rows = [P] * 9 + [META]

        def source(t):
            if t == META_TILE:
                return d["meta_tokens"]
            if t == SAMPLE_TILE:
                return d["x_sample"].rearrange("b s d -> (b s) d")
            return d["x_prompt"][0, t * P:(t + 1) * P, :]

        with nc.Block() as block:
            @block.sync
            def _(sp):
                for t in range(TILES):
                    if t >= 3:
                        sp.wait_ge(normed, t - 2)
                    sp.dma_start(xr[0:rows[t], t % 3, :], source(t)).then_inc(x_in[t % 3], 16)
                    if t == 0:
                        sp.dma_start(gb[:, :], d["norm_g"].to_broadcast([P, D])).then_inc(small_in, 16)
                    if t == 2:
                        sp.dma_start(b80[:, :], d["b_in"].rearrange("o (n p) -> (o n) p", p=P)).then_inc(small_in, 16)
                        sp.dma_start(cw3[:, :], d["conv_w"][0]).then_inc(small_in, 16)
                        sp.dma_start(st16[:, :], d["state_conv"][0].rearrange("b j c -> (b j) c")).then_inc(small_in, 16)

            @block.gpsimd
            def _(pool):
                pool.memset(c.ident[:, :], 0.0).then_inc(made, 1)
                pool.memset(c.identb[:, :], 0.0).then_inc(made, 1)
                pool.memset(c.mask[:, :], 0.0).then_inc(made, 1)
                pool.memset(c.mask_s[:, :], 0.0).then_inc(made, 1)
                pool.memset(half[:, :], -0.5).then_inc(made, 1)
                pool.wait_ge(made, 5)
                for m in (c.ident, c.identb):
                    pool.affine_select(out=m[:, :], in_=m[:, :], compare_op=ALU.not_equal, fill=1.0, base=0,
                                       pattern=[[-1, P]], channel_multiplier=1).then_inc(made, 1)
                for m in (c.mask, c.mask_s):
                    pool.affine_select(out=m[:, :], in_=m[:, :], compare_op=ALU.is_gt, fill=HIDDEN, base=0,
                                       pattern=[[-1, P]], channel_multiplier=1).then_inc(made, 1)
                pool.wait_ge(made, 9)
                pool.affine_select(out=c.mask_s[:, :].rearrange("p (b j) -> p b j", j=DS),
                                   in_=c.mask_s[:, :].rearrange("p (b j) -> p b j", j=DS),
                                   compare_op=ALU.is_gt, fill=HIDDEN, base=DS,
                                   pattern=[[DS, NB], [0, DS]], channel_multiplier=-1).then_inc(made, 1)
                for t in range(TILES):
                    n = rows[t]
                    pool.wait_ge(squared, t + 1)
                    pool.tensor_scalar(ms[0:n, t:t + 1], ss[0:n, t:t + 1], 1.0 / D, EPS,
                                       ALU.mult, ALU.add).then_inc(mean_ok, 1)
                    pool.wait_ge(mean_ok, t + 1)
                    pool.tensor_tensor(rs[0:n, t:t + 1], ms[0:n, t:t + 1], half[0:n, t:t + 1],
                                       ALU.pow).then_inc(rstd_ok, 1)

            @block.scalar
            def _(act):
                def hi(t, j):
                    n, (c0, c1) = rows[t], tile_cols(t)
                    act.wait_ge(turned, 2 * t + j + 1)
                    act.activation(c.xh[:, 4 * j:4 * j + 4, c0:c1],
                                   c.bank_t[j][:, :].rearrange("p (k n) -> p k n", k=4)[:, :, 0:n],
                                   ACT.Copy).then_inc(hi_ok, 1)

                for t in range(TILES + 1):
                    if t < TILES:
                        n = rows[t]
                        act.wait_ge(x_in[t % 3], 16 * (t // 3 + 1))
                        if t:
                            act.wait_ge(squared, t)
                        act.activation(junk[0:n, :], xr[0:n, t % 3, :], ACT.Square,
                                       accum_out=ss[0:n, t:t + 1]).then_inc(squared, 1)
                    if t >= 1:
                        hi(t - 1, 0)
                        hi(t - 1, 1)

            @block.vector
            def _(dve):
                def lo(t, j):
                    n, (c0, c1) = rows[t], tile_cols(t)
                    dve.wait_ge(hi_ok, 2 * t + j + 1)
                    dve.tensor_tensor(c.xl[:, 4 * j:4 * j + 4, c0:c1],
                                      c.bank_t[j][:, :].rearrange("p (k n) -> p k n", k=4)[:, :, 0:n],
                                      c.xh[:, 4 * j:4 * j + 4, c0:c1].bitcast(F32), ALU.subtract).then_inc(lo_ok, 1)

                dve.wait_ge(small_in, 64)
                for t in range(TILES + 1):
                    if t < TILES:
                        n = rows[t]
                        dve.wait_ge(rstd_ok, t + 1)
                        if t >= 2:
                            dve.wait_ge(turned, 2 * (t - 1))
                        dve.scalar_tensor_tensor(out=xn[0:n, t % 2, :], in0=xr[0:n, t % 3, :],
                                                 scalar=rs[0:n, t:t + 1], in1=gb[0:n, :],
                                                 op0=ALU.mult, op1=ALU.mult).then_inc(normed, 1)
                    if t >= 1:
                        lo(t - 1, 0)
                        lo(t - 1, 1)
                dve.wait_ge(small_turned, 1)
                dve.tensor_copy(c.bias[:, :], c.bank_o[:, 0:80]).then_inc(small_out, 1)
                dve.tensor_copy(c.conv_w[:, :, :], c.bank_o[:, 80:104].rearrange("p (k j) -> p k j", j=3)).then_inc(small_out, 1)
                dve.tensor_copy(c.state[:, :, :], c.bank_o[:, 128:256].rearrange("p (k j) -> p k j", j=16)).then_inc(small_out, 1)

            @block.tensor
            def _(pe):
                pe.wait_ge(made, 7)
                for t in range(TILES):
                    n = rows[t]
                    pe.wait_ge(normed, t + 1)
                    for j in range(2):
                        if t:
                            pe.wait_ge(lo_ok, 2 * (t - 1) + j + 1)
                        for k in range(4):
                            mm = pe.transpose(c.bank_t[j][:, k * P:k * P + n],
                                              xn[0:n, t % 2, (4 * j + k) * P:(4 * j + k + 1) * P], c.ident[0:n, 0:n])
                        mm.then_inc(turned, 1)
                pe.wait_ge(small_in, 64)
                pe.transpose(c.bank_o[:, 0:80], b80[:, :], c.ident[0:80, 0:80])
                for k in range(KC):
                    pe.transpose(c.bank_o[:, 80 + 3 * k:83 + 3 * k], cw3[:, k * P:(k + 1) * P], c.ident[0:3, 0:3])
                for k in range(KC):
                    mm = pe.transpose(c.bank_o[:, 128 + 16 * k:144 + 16 * k], st16[:, k * P:(k + 1) * P],
                                      c.ident[0:16, 0:16])
                mm.then_inc(small_turned, 1)


HELD = {}


def hold(eng, sem, value):
    eng.wait_ge(sem, value)
    eng.sem_inc(HELD["waits_held"], 1)


class WeightTiles:

    def __init__(self, c, ctx, name, slots, per_round):
        self.slots, self.per_round = slots, per_round
        self.raw = c.sb(ctx, name + "_raw", [P, slots, KC, P])
        self.hi = c.sb(ctx, name + "_hi", [P, slots, KC, P], F32R)
        self.lo = c.sb(ctx, name + "_lo", [P, slots, KC, P], F32R)
        self.raw_in = [c.sem(f"{name}_raw_in{s}") for s in range(slots)]
        self.hi_ok, self.lo_ok = c.sem(name + "_hi_ok"), c.sem(name + "_lo_ok")

    def count(self, i, j):
        return i * self.per_round + j

    def start_pool(self, pool):
        pool.sem_inc(self.lo_ok, self.slots)

    def load(self, sp, i, j, src):
        s = j % self.slots
        sp.wait_ge(self.lo_ok, self.count(i, j) + 1)
        sp.dma_start(self.raw[:, s, :, :], src).then_inc(self.raw_in[s], 16)

    def split_hi(self, act, i, j):
        s = j % self.slots
        loads = i * (self.per_round // self.slots) + j // self.slots + 1
        act.wait_ge(self.raw_in[s], 16 * loads)
        act.activation(self.hi[:, s, :, :], self.raw[:, s, :, :], ACT.Copy).then_inc(self.hi_ok, 1)

    def split_lo(self, pool, i, j):
        s = j % self.slots
        pool.wait_ge(self.hi_ok, self.count(i, j) + 1)
        pool.tensor_tensor(self.lo[:, s, :, :], self.raw[:, s, :, :], self.hi[:, s, :, :].bitcast(F32),
                           ALU.subtract).then_inc(self.lo_ok, 1)

    def ready(self, pe, i, j):
        pe.wait_ge(self.lo_ok, self.count(i, j) + 1 + self.slots)

    def product(self, pe, j, out, right):
        s = j % self.slots
        return split_product(pe, out, (lambda k: self.hi[:, s, k, :], lambda k: self.lo[:, s, k, :]), right, KC)


def x_moving(c, c0, c1):
    return (lambda k: c.xh[:, k, c0:c1], lambda k: c.xl[:, k, c0:c1])


def conv_branch(c, d, yh, yl):
    nc = c.nc
    w_cols = d["w_in"][0].rearrange("(k p) (n e) -> p k n e", p=P, e=P)
    names = ["C", "h", "B", "z_c"]
    with ExitStack() as ctx:
        w = WeightTiles(c, ctx, "wc", 2, 4)
        cs = c.sb(ctx, "c_part", [P, TOK])
        up = c.sb(ctx, "u_prompt", [P, SAMPLE0])
        us = c.sb(ctx, "u_sample", [P, NB, DS + 2])
        tap = c.sb(ctx, "conv_out", [P, LIVE])
        sg = c.sb(ctx, "sig_z", [P, LIVE])
        yt = c.sb(ctx, "y_conv", [P, LIVE])
        last = c.sb(ctx, "last_u", [P, KC, 2 + NB * 2])
        last_rows = c.sb(ctx, "last_u_rows", [2 + NB * 2, D])

        full = c.sem("conv_bank_full")
        c_out = c.sem("c_out")
        d_out = c.sem("hbz_out")
        u_ok = c.sem("u_ok")
        tap_ok = c.sem("tap_ok")
        sig_ok = c.sem("sig_ok")
        y_ok = c.sem("y_ok")
        yh_ok = c.sem("yh_ok")
        yl_ok = c.sem("yl_ok")
        last_ok = c.sem("last_ok")
        last_turned = c.sem("last_turned")
        last_out = c.sem("last_out")
        stored = c.sem("conv_state_stored")
        banks = [c.bank_p[0], c.bank_p[1]]

        def bias(name, i):
            return c.bias[:, bass.ds(i + OFF[name] // P, 1)]

        with nc.Block() as block:
            @block.sync
            def _(sp):
                with sp.Fori(0, KC) as i:
                    for j, name in enumerate(names):
                        w.load(sp, i, j, w_cols[:, :, bass.ds(i + OFF[name] // P, 1), :])
                sp.wait_ge(last_out, 2)
                sp.dma_start(d["conv_prompt"][0, 0], last_rows[0:2, :]).then_inc(stored, 16)
                sp.dma_start(d["conv_sample"][0].rearrange("b j c -> (b j) c"), last_rows[2:18, :]).then_inc(stored, 16)
                sp.wait_ge(stored, 32)

            @block.gpsimd
            def _(pool):
                w.start_pool(pool)
                with pool.Fori(0, KC) as i:
                    for j in range(4):
                        w.split_lo(pool, i, j)

            @block.tensor
            def _(pe):
                with pe.Fori(0, KC) as i:
                    for j, name in enumerate(names):
                        w.ready(pe, i, j)
                        for n, (c0, c1) in enumerate(CH if name in "Ch" else CHL):
                            q = 3 * j + n
                            if q < 2:
                                pe.wait_ge(d_out, 9 * i + q + 1)
                            elif q < 5:
                                pe.wait_ge(c_out, 3 * i + q - 1)
                            else:
                                pe.wait_ge(d_out, 9 * i + q - 4 + 2)
                            mm = w.product(pe, j, banks[q % 2][:, 0:c1 - c0], x_moving(c, c0, c1))
                            mm.then_inc(full, 1)
                pe.wait_ge(last_ok, 2 * KC)
                for k in range(KC):
                    mm = pe.transpose(c.bank_z[0:18, k * P:(k + 1) * P], last[:, k, :], c.ident[:, :])
                mm.then_inc(last_turned, 1)

            @block.scalar
            def _(act):
                def one_block(i, more):
                    def rest_of_y(n):
                        c0, c1 = CHL[n]
                        hold(act, y_ok, 3 * i + n + 1)
                        act.activation(row(yh, i, c0 - META, c1 - META),
                                       yt[:, c0 - META:c1 - META], ACT.Copy).then_inc(yh_ok, 1)

                    for n, (c0, c1) in enumerate(CH):
                        hold(act, full, 12 * i + n + 1)
                        act.activation(cs[:, c0:c1], banks[n % 2][:, 0:c1 - c0], ACT.Identity,
                                       bias=bias("C", i)).then_inc(c_out, 1)
                    w.split_hi(act, i, 2)
                    act.wait_ge(full, 12 * i + 6)
                    w.split_hi(act, i, 3)
                    for n, (c0, c1) in enumerate(CHL):
                        q = 9 + n
                        hold(act, full, 12 * i + q + 1)
                        act.activation(sg[:, c0 - META:c1 - META], banks[q % 2][:, 0:c1 - c0], ACT.Sigmoid,
                                       bias=bias("z_c", i)).then_inc(sig_ok, 1)
                        if n == 0 and more:
                            w.split_hi(act, i + 1, 0)
                        if n:
                            rest_of_y(n - 1)
                    if more:
                        w.split_hi(act, i + 1, 1)
                    rest_of_y(2)

                w.split_hi(act, 0, 0)
                w.split_hi(act, 0, 1)
                with act.Fori(0, KC - 1) as i:
                    one_block(i, True)
                one_block(KC - 1, False)

            @block.vector
            def _(dve):
                dve.sem_inc(d_out, 2)

                def sample(t):
                    return t[:, SEQ:LIVE].rearrange("p (b j) -> p b j", j=DS)

                with dve.Fori(0, KC) as i:
                    dve.tensor_copy(us[:, :, 0:2], c.state[:, bass.ds(i, 1), :].rearrange("p o (b j) -> p (o b) j", j=2)
                                    ).then_inc(u_ok, 1)
                    for n, (c0, c1) in enumerate(CH):
                        q = 3 + n
                        dve.wait_ge(full, 12 * i + q + 1)
                        dve.wait_ge(c_out, 3 * i + n + 1)
                        e = min(c1, SAMPLE0)
                        mm = dve.scalar_tensor_tensor(out=up[:, c0:e], in0=banks[q % 2][:, 0:e - c0], scalar=bias("h", i),
                                                      in1=cs[:, c0:e], op0=ALU.add, op1=ALU.mult)
                        if n < 2:
                            mm.then_inc(d_out, 1)
                    mm.then_inc(u_ok, 1)
                    dve.scalar_tensor_tensor(out=us[:, :, 2:DS + 2],
                                             in0=banks[1][:, 256:384].rearrange("p (b j) -> p b j", j=DS),
                                             scalar=bias("h", i),
                                             in1=cs[:, SAMPLE0:TOK].rearrange("p (b j) -> p b j", j=DS),
                                             op0=ALU.add, op1=ALU.mult).then_inc(d_out, 1)
                    dve.wait_ge(u_ok, 2 * i + 2)
                    dve.wait_ge(d_out, 9 * i + 3 + 2)
                    for r in range(3):
                        wr = c.conv_w[:, bass.ds(i, 1), r:r + 1].rearrange("p a b -> p (a b)")
                        pairs = [(tap[:, 0:SEQ], up[:, META - 2 + r:SAMPLE0 - 2 + r]),
                                 (sample(tap), us[:, :, r:r + DS])]
                        if r:
                            dve.wait_ge(tap_ok, 6 * i + 2 * r)
                        for dst, src in pairs:
                            if r == 0:
                                dve.tensor_scalar(dst, src, wr, None, ALU.mult).then_inc(tap_ok, 1)
                            else:
                                dve.scalar_tensor_tensor(out=dst, in0=src, scalar=wr, in1=dst,
                                                         op0=ALU.mult, op1=ALU.add).then_inc(tap_ok, 1)
                    dve.tensor_copy(last[:, bass.ds(i, 1), 0:2].rearrange("p o j -> p (o j)"),
                                    up[:, SAMPLE0 - 2:SAMPLE0]).then_inc(last_ok, 1)
                    dve.tensor_copy(last[:, bass.ds(i, 1), 2:18].rearrange("p o (b j) -> p (o b) j", j=2),
                                    us[:, :, DS:DS + 2]).then_inc(last_ok, 1)
                    dve.wait_ge(tap_ok, 6 * i + 6)
                    for n, (c0, c1) in enumerate(CHL):
                        q = 6 + n
                        t = tap[:, c0 - META:c1 - META]
                        dve.wait_ge(full, 12 * i + q + 1)
                        dve.scalar_tensor_tensor(out=t, in0=banks[q % 2][:, 0:c1 - c0], scalar=bias("B", i), in1=t,
                                                 op0=ALU.add, op1=ALU.mult).then_inc(d_out, 1)
                    for n, (c0, c1) in enumerate(CHL):
                        q = 9 + n
                        a, b = c0 - META, c1 - META
                        dve.wait_ge(sig_ok, 3 * i + n + 1)
                        dve.scalar_tensor_tensor(out=sg[:, a:b], in0=banks[q % 2][:, 0:c1 - c0], scalar=bias("z_c", i),
                                                 in1=sg[:, a:b], op0=ALU.add, op1=ALU.mult).then_inc(d_out, 1)
                        dve.wait_ge(d_out, 9 * i + 7 + n + 2)
                        dve.tensor_tensor(yt[:, a:b], sg[:, a:b], tap[:, a:b], ALU.mult).then_inc(y_ok, 1)
                        dve.wait_ge(yh_ok, 3 * i + n + 1)
                        dve.tensor_tensor(row(yl, i, a, b), yt[:, a:b],
                                          row(yh, i, a, b).bitcast(F32), ALU.subtract).then_inc(yl_ok, 1)
                dve.wait_ge(last_turned, 1)
                dve.tensor_copy(last_rows[:, 0:512], c.bank_z[0:18, 0:512]).then_inc(last_out, 1)
                dve.tensor_copy(last_rows[:, 512:1024], c.bank_z[0:18, 512:1024]).then_inc(last_out, 1)


def conv_gates(c, d, yh, yl):
    nc = c.nc
    w_cols = d["w_in"][0].rearrange("(k p) (n e) -> p k n e", p=P, e=P)
    co_cols = d["w_conv_o"][0].rearrange("(k p) (n e) -> p k n e", p=P, e=P)
    with ExitStack() as ctx:
        w = WeightTiles(c, ctx, "wg", 3, 3)
        gate = c.sb(ctx, "gate_c", [P, LIVE])
        outs = c.sb(ctx, "gates_out", [P, 2, LIVE])
        full = c.sem("gate_bank_full")
        g_ok = c.sem("gate_c_ok")
        m_ok = c.sem("m1_ok")
        s_ok = c.sem("gate_s_ok")
        m_stored = c.sem("m1_stored")
        s_stored = c.sem("gate_s_stored")
        banks = [c.bank_p[0], c.bank_p[1], c.bank_o]

        def bias(name, i):
            return c.bias[:, bass.ds(i + OFF[name] // P, 1)]

        with nc.Block() as block:
            @block.sync
            def _(sp):
                sp.sem_inc(m_stored, 16)
                sp.sem_inc(s_stored, 16)

                def load(i):
                    w.load(sp, i, 0, w_cols[:, :, bass.ds(i + OFF["g_c"] // P, 1), :])
                    w.load(sp, i, 1, co_cols[:, :, bass.ds(i, 1), :])
                    w.load(sp, i, 2, w_cols[:, :, bass.ds(i + OFF["g_s"] // P, 1), :])

                def store(i):
                    sp.wait_ge(m_ok, 3 * i + 3)
                    sp.dma_start(d["m1"][bass.ds(i, 1)].rearrange("o p n -> (o p) n"), outs[:, 0, :]).then_inc(m_stored, 16)
                    sp.wait_ge(s_ok, 3 * i + 3 + 3)
                    sp.dma_start(d["sgate"][bass.ds(i, 1)].rearrange("o p n -> (o p) n"), outs[:, 1, :]).then_inc(s_stored, 16)

                load(0)
                with sp.Fori(0, KC - 1) as i:
                    load(i + 1)
                    store(i)
                store(KC - 1)
                sp.wait_ge(m_stored, 16 * (KC + 1))
                sp.wait_ge(s_stored, 16 * (KC + 1))

            @block.gpsimd
            def _(pool):
                w.start_pool(pool)
                with pool.Fori(0, KC) as i:
                    for j in range(3):
                        w.split_lo(pool, i, j)

            @block.tensor
            def _(pe):
                with pe.Fori(0, KC) as i:
                    for j in range(3):
                        w.ready(pe, i, j)
                        for n, (c0, c1) in enumerate(CHL):
                            if j == 0:
                                pe.wait_ge(s_ok, 3 * i + n + 1)
                            elif j == 1:
                                pe.wait_ge(g_ok, 3 * i + n + 1)
                            else:
                                pe.wait_ge(m_ok, 3 * i + n + 1)
                            right = x_moving(c, c0, c1) if j != 1 else (
                                lambda k: yh[:, k, c0 - META:c1 - META], lambda k: yl[:, k, c0 - META:c1 - META])
                            w.product(pe, j, banks[n][:, 0:c1 - c0], right).then_inc(full, 1)

            @block.scalar
            def _(act):
                act.sem_inc(s_ok, 3)
                def one_block(i, more):
                    for n, (c0, c1) in enumerate(CHL):
                        hold(act, full, 9 * i + n + 1)
                        act.activation(gate[:, c0 - META:c1 - META], banks[n][:, 0:c1 - c0], ACT.Sigmoid,
                                       bias=bias("g_c", i)).then_inc(g_ok, 1)
                    if more:
                        w.split_hi(act, i + 1, 0)
                        act.wait_ge(full, 9 * i + 6)
                        w.split_hi(act, i + 1, 1)
                    act.wait_ge(s_stored, 16 * i + 16)
                    for n, (c0, c1) in enumerate(CHL):
                        hold(act, full, 9 * i + 6 + n + 1)
                        act.activation(outs[:, 1, c0 - META:c1 - META], banks[n][:, 0:c1 - c0], ACT.Sigmoid,
                                       bias=bias("g_s", i)).then_inc(s_ok, 1)
                    if more:
                        w.split_hi(act, i + 1, 2)

                for j in range(3):
                    w.split_hi(act, 0, j)
                with act.Fori(0, KC - 1) as i:
                    one_block(i, True)
                one_block(KC - 1, False)

            @block.vector
            def _(dve):
                with dve.Fori(0, KC) as i:
                    dve.wait_ge(m_stored, 16 * i + 16)
                    for n, (c0, c1) in enumerate(CHL):
                        dve.wait_ge(full, 9 * i + 3 + n + 1)
                        dve.wait_ge(g_ok, 3 * i + n + 1)
                        dve.tensor_tensor(outs[:, 0, c0 - META:c1 - META], banks[n][:, 0:c1 - c0],
                                          gate[:, c0 - META:c1 - META], ALU.mult).then_inc(m_ok, 1)


ORDER = [7, 6, 5, 4, "samples", 3, 2, 1, 0]
UNITS = len(ORDER)
SAMPLE_UNIT = ORDER.index("samples")
PROMPT_UNITS = UNITS - 1
FIRST_P, NPROJ = TILES + 1, TILES + 3
FIRST_T, NT, NGROUPS = TILES, 50, 14


def width(u):
    return PAST + P if u == SAMPLE_UNIT else META + P * (ORDER[u] + 1)


def value_groups(u):
    if u == SAMPLE_UNIT:
        return [["new"], [0, 1, 2, 3]]
    items = ["meta"] + list(range(ORDER[u] + 1))
    return [items[i:i + 4] for i in range(0, len(items), 4)]


def prompt_units_before(u):
    return u - (u > SAMPLE_UNIT)


def groups_before(u):
    return sum(len(value_groups(v)) for v in range(u) if v != SAMPLE_UNIT)


def slot_steps(slot, nxt):
    before, after = [], []
    if slot < UNITS and slot != SAMPLE_UNIT:
        before.append(("m", slot))
    if slot == 0:
        before += [("k", 0), ("k", 1)]
    elif slot < UNITS + 1:
        groups = [("a", slot - 1, g) for g in range(len(value_groups(slot - 1)))]
        before += groups[:2]
        if slot <= 3:
            after += [("k", 2 * slot)] + groups[2:] + [("k", 2 * slot + 1)]
        if slot > SAMPLE_UNIT and slot < UNITS:
            after += [("v", 2 * (slot - SAMPLE_UNIT - 1)), ("v", 2 * (slot - SAMPLE_UNIT - 1) + 1)]
        if slot >= 2 and nxt:
            after.append(("x", slot - 2))
        if slot == UNITS and nxt:
            after += [("x", TILES - 2), ("x", TILES - 1)]
    return before, after


def turn_plan(nxt):
    order = [step for slot in range(UNITS + 1) for part in slot_steps(slot, nxt) for step in part]
    assert not nxt or len(order) == NT
    return {key: n for n, key in enumerate(order)}


def attention(c, d):
    nc = c.nc
    w_cols = d["w_in"][0].rearrange("(k p) (n e) -> p k n e", p=P, e=P)
    b_cols = d["b_in"].rearrange("o (n e) -> o n e", e=P)
    cache_k = d["cache_k"][0].rearrange("b (n p) h d -> b p n h d", p=P)
    cache_v = d["cache_v"][0].rearrange("b (n p) h d -> b p n h d", p=P)
    plans = {True: turn_plan(True), False: turn_plan(False)}
    with ExitStack() as ctx:
        wz = WeightTiles(c, ctx, "wz", 1, 1)
        w3 = c.sb(ctx, "wqkv_raw", [P, KC, 3 * P])
        w3h = c.sb(ctx, "wqkv_hi", [P, KC, 3 * P], F32R)
        w3l = c.sb(ctx, "wqkv_lo", [P, KC, 3 * P], F32R)
        bias3 = c.sb(ctx, "bias_qkv", [P, 2, 3 * P])
        gain = c.sb(ctx, "qk_gain", [P, 2, P])
        qk = c.sb(ctx, "qk_turned", [P, 2, 2, TOK])
        v = c.sb(ctx, "v_rows", [P, 2, TILES, P])
        qkn = c.sb(ctx, "qk_rows", [P, 2, 2 * P])
        junk = c.sb(ctx, "squares2", [P, 2, P])
        ss = c.sb(ctx, "qk_sumsq", [P, 2, 2])
        ms = c.sb(ctx, "qk_meansq", [P, 2, 2])
        rs = c.sb(ctx, "qk_rstd", [P, 2, 2])
        half = c.sb(ctx, "minus_half2", [P, 2])
        beta = c.sb(ctx, "beta", [P, 2, SAMPLE0])
        keep = c.sb(ctx, "one_minus_beta", [P, 2, SAMPLE0])
        at = c.sb(ctx, "a_turned", [P, 2, 4 * P])
        ats = c.sb(ctx, "a_samples_turned", [P, PAST + P])
        kc = c.sb(ctx, "cache_k_rows", [P, 2, PAST // P, P])
        vc = c.sb(ctx, "cache_v_rows", [P, 2, PAST // P, P])
        kt = c.sb(ctx, "cache_k_turned", [P, 2, PAST])
        qbd = c.sb(ctx, "q_block_diagonal", [P, NB * (P + DS)])
        ot = c.sb(ctx, "o_turned", [P, LIVE])
        zs = c.sb(ctx, "silu_z", [P, LIVE])
        y_again = w3[:, :, :].rearrange("p k e -> p (k e)")

        gain_in, half_ok = c.sem("gain_in"), c.sem("half_ok")
        w3_in, w3_hi, w3_lo = c.sem("wqkv_in"), c.sem("wqkv_hi_ok"), c.sem("wqkv_lo_ok")
        b3_in = [c.sem(f"bias_qkv_in{q}") for q in range(2)]
        proj_ok, proj_out = c.sem("proj_bank_full"), c.sem("proj_bank_out")
        t_full, t_out = c.sem("turn_bank_full"), c.sem("turn_bank_out")
        rows_ok, sq_ok, mean_ok, rstd_ok = c.sem("qk_rows_ok"), c.sem("qk_sq"), c.sem("qk_mean"), c.sem("qk_rstd_ok")
        norm_ok = c.sem("qk_norm_ok")
        k_stored = [c.sem(f"k_stored{s}") for s in range(2)]
        v_stored = [c.sem(f"v_stored{q}") for q in range(2)]
        score_ok, kq_ok = c.sem("scores_ok"), c.sem("cache_scores_ok")
        keep_ok, beta_ok = c.sem("keep_ok"), c.sem("beta_ok")
        scan_ok, a_ok = c.sem("scan_ok"), c.sem("a_ok")
        pv_ok, o_out = c.sem("value_group_ok"), c.sem("o_out")
        k_in = [c.sem(f"cache_k_in{s}") for s in range(2)]
        v_in = [c.sem(f"cache_v_in{s}") for s in range(2)]
        qbd_ok = c.sem("q_block_ok")
        zsig_ok = c.sem("z_sig_ok")
        y_ok, y_stored = c.sem("y_s_ok"), c.sem("y_s_stored")
        y_in = [c.sem(f"y_s_in{s}") for s in range(2)]
        yh_ok, yl_ok = c.sem("y_s_hi_ok"), c.sem("y_s_lo_ok")

        def rows_of(t):
            return META if t == META_TILE else P

        def turn_bank(h, plan, key):
            n = plan[key]
            return FIRST_T + NT * h + n, c.bank_t[n % 2]

        def proj_bank(h, par, n):
            return FIRST_P + NPROJ * h + n, c.bank_p[(FIRST_P + par + n) % 2]

        def z_bank(h, par, n):
            if n:
                return proj_bank(h, par, n - 1)
            return FIRST_P + NPROJ * h - 1, c.bank_p[(FIRST_P + par - 1) % 2]

        def head_block(name, h):
            return bass.ds(h + OFF[name] // P, 1)

        def all_heads(eng, head):
            with eng.Fori(0, HEADS // 2 - 1) as i:
                head(2 * i, 0, i, True, True)
                head(2 * i + 1, 1, i, True, True)
            head(HEADS - 2, 0, HEADS // 2 - 1, True, False)
            head(HEADS - 1, 1, HEADS // 2 - 1, False, False)

        with nc.Block() as block:
            @block.sync
            def _(sp):
                def load_qkv(h, q):
                    for j, name in enumerate("qkv"):
                        sp.dma_start(w3[:, :, j * P:(j + 1) * P], w_cols[:, :, head_block(name, h), :]).then_inc(w3_in, 16)
                    for j, name in enumerate("qkv"):
                        sp.dma_start(bias3[:, q, j * P:(j + 1) * P],
                                     b_cols[:, head_block(name, h), :].rearrange("o n e -> o (n e)").to_broadcast([P, P])
                                     ).then_inc(b3_in[q], 16)

                def load_z(h):
                    sp.dma_start(wz.raw[:, 0, :, :], w_cols[:, :, head_block("z_s", h), :]).then_inc(wz.raw_in[0], 16)

                def load_k(h, b):
                    sp.dma_start(kc[:, b % 2, :, :], cache_k[b][:, :, bass.ds(h, 1), :].rearrange("p n o d -> p n (o d)")
                                 ).then_inc(k_in[b % 2], 16)

                def load_v(h, b):
                    sp.dma_start(vc[:, b % 2, :, :], cache_v[b][:, :, bass.ds(h, 1), :].rearrange("p n o d -> p n (o d)")
                                 ).then_inc(v_in[b % 2], 16)

                def store(h, q, t):
                    n = rows_of(t)
                    sp.wait_ge(norm_ok, TILES * h + t + 1)
                    if t == SAMPLE_TILE:
                        dk, dv = (d[x][0].rearrange("b s h d -> (b s) h d") for x in ("k_sample", "v_sample"))
                    else:
                        c0, c1 = tile_cols(t)
                        dk, dv = (d[x][0, 0, c0:c1] for x in ("k_prompt", "v_prompt"))
                    sp.dma_start(dk[:, bass.ds(h, 1), :].rearrange("t o d -> t (o d)"),
                                 qkn[0:n, t % 2, P:2 * P]).then_inc(k_stored[t % 2], 16)
                    sp.dma_start(dv[:, bass.ds(h, 1), :].rearrange("t o d -> t (o d)"),
                                 v[0:n, q, t, :]).then_inc(v_stored[q], 16)

                def head(h, par, pairs, nxt, nxt2):
                    plan = plans[nxt]

                    def next_cache(kind, load, b):
                        if b + 2 < NB or nxt:
                            hold(sp, t_full, turn_bank(h, plan, (kind, b))[0] + 1)
                            load(h if b + 2 < NB else h + 1, (b + 2) % NB)

                    for slot in range(UNITS):
                        if slot <= 3:
                            next_cache("k", load_k, 2 * slot)
                            next_cache("k", load_k, 2 * slot + 1)
                        if slot == 0 and nxt2:
                            sp.wait_ge(w3_lo, 2 * h + 4)
                            load_qkv(h + 2, par)
                        if slot == 1 and nxt2:
                            sp.wait_ge(wz.lo_ok, h + 2 + 1)
                            load_z(h + 2)
                        if slot and nxt:
                            store(h + 1, 1 - par, slot - 1)
                        if slot > SAMPLE_UNIT:
                            for b in range(2):
                                next_cache("v", load_v, 2 * (slot - SAMPLE_UNIT - 1) + b)
                        if slot and not nxt and slot < UNITS - 1:
                            k = slot - 1
                            if k == 0:
                                sp.wait_ge(w3_lo, 2 * HEADS)
                                sp.wait_ge(y_stored, 16 * HEADS)
                            if k >= 2:
                                sp.wait_ge(yl_ok, k - 1)
                            sp.dma_start(y_again[:, (k % 2) * LIVE:(k % 2 + 1) * LIVE], d["ys"][k]).then_inc(y_in[k % 2], 16)
                    if nxt:
                        store(h + 1, 1 - par, TILES - 2)
                        sp.wait_ge(y_ok, h + 1)
                        sp.dma_start(d["ys"][bass.ds(h, 1)].rearrange("o p n -> (o p) n"), ot[:, :]).then_inc(y_stored, 16)
                        store(h + 1, 1 - par, TILES - 1)

                for s in range(2):
                    sp.sem_inc(k_stored[s], 16)
                    sp.sem_inc(v_stored[s], 16)
                sp.sem_inc(y_stored, 16)
                load_qkv(0, 0)
                sp.dma_start(gain[:, 0, :], d["q_norm_g"].to_broadcast([P, P])).then_inc(gain_in, 16)
                sp.dma_start(gain[:, 1, :], d["k_norm_g"].to_broadcast([P, P])).then_inc(gain_in, 16)
                load_z(0)
                for b in range(2):
                    load_k(0, b)
                    load_v(0, b)
                sp.wait_ge(w3_lo, 2)
                load_qkv(1, 1)
                sp.wait_ge(wz.lo_ok, 1 + 1)
                load_z(1)
                for t in range(TILES):
                    store(0, 0, t)
                all_heads(sp, head)
                for s in range(2):
                    sp.wait_ge(k_stored[s], 16 * (HEADS * TILES // 2 + 1))
                    sp.wait_ge(v_stored[s], 16 * (HEADS * TILES // 2 + 1))

            @block.gpsimd
            def _(pool):
                def rstd(h, t):
                    n, s = rows_of(t), t % 2
                    a = 1 if t == META_TILE else 0
                    hold(pool, sq_ok, TILES * h + t + 1)
                    pool.tensor_scalar(ms[0:n, s, a:2], ss[0:n, s, a:2], 1.0 / HD, EPS, ALU.mult, ALU.add).then_inc(mean_ok, 1)
                    pool.wait_ge(mean_ok, TILES * h + t + 1)
                    pool.tensor_tensor(rs[0:n, s, a:2], ms[0:n, s, a:2], half[0:n, a:2], ALU.pow).then_inc(rstd_ok, 1)

                def split_qkv_lo(h):
                    for j in range(2):
                        k = slice(4 * j, 4 * j + 4)
                        pool.wait_ge(w3_hi, 2 * h + j + 1)
                        pool.tensor_tensor(w3l[:, k, :], w3[:, k, :], w3h[:, k, :].bitcast(F32),
                                           ALU.subtract).then_inc(w3_lo, 1)

                def head(h, par, pairs, nxt, nxt2):
                    pool.wait_ge(t_out, FIRST_T + NT * h + 1)
                    hold(pool, kq_ok, NB * h + 2)
                    pool.tensor_copy(qbd[:, :].rearrange("p (b w) -> p b w", w=P + DS)[:, :, 0:DS],
                                     qk[:, par, 0, SAMPLE0:TOK].rearrange("p (b j) -> p b j", j=DS)).then_inc(qbd_ok, 1)
                    if nxt:
                        split_qkv_lo(h + 1)
                        rstd(h + 1, 0)
                        wz.split_lo(pool, h + 1, 0)
                        for t in range(1, TILES):
                            rstd(h + 1, t)

                wz.start_pool(pool)
                pool.memset(half[:, :], -0.5).then_inc(half_ok, 1)
                pool.memset(qbd[:, :], 0.0).then_inc(half_ok, 1)
                pool.wait_ge(half_ok, 2)
                split_qkv_lo(0)
                wz.split_lo(pool, 0, 0)
                for t in range(TILES):
                    rstd(0, t)
                all_heads(pool, head)

            @block.tensor
            def _(pe):
                def project(h, t, number):
                    n, (c0, c1) = rows_of(t), tile_cols(t)
                    a = P if t == META_TILE else 0
                    num, bank = number
                    if t == 0:
                        pe.wait_ge(w3_lo, 2 * h + 2)
                    pe.wait_ge(proj_out, num + 1)
                    split_product(pe, bank[0:n, a:3 * P], (lambda k: c.xh[:, k, c0:c1], lambda k: c.xl[:, k, c0:c1]),
                                  (lambda k: w3h[:, k, a:3 * P], lambda k: w3l[:, k, a:3 * P]), KC).then_inc(proj_ok, 1)

                def turn_rows(h, t, number):
                    n = rows_of(t)
                    num, bank = number
                    pe.wait_ge(norm_ok, TILES * h + t + 1)
                    if t == META_TILE:
                        hold(pe, t_out, num + 1)
                    else:
                        pe.wait_ge(t_out, num + 1)
                        pe.transpose(bank[:, 0:P], qkn[0:n, t % 2, 0:P], c.ident[0:n, 0:n])
                    pe.transpose(bank[:, P:P + n], qkn[0:n, t % 2, P:2 * P], c.ident[0:n, 0:n]).then_inc(t_full, 1)

                def silu_gate(h, n, number):
                    c0, c1 = CHL[n]
                    num, bank = number
                    if n == 0:
                        wz.ready(pe, h, 0)
                    pe.wait_ge(proj_out, num + 1)
                    wz.product(pe, 0, bank[:, 0:c1 - c0], x_moving(c, c0, c1)).then_inc(proj_ok, 1)

                def scores(h, par, u, plan):
                    pe.wait_ge(beta_ok, UNITS * h + u + 1)
                    if u == SAMPLE_UNIT:
                        pe.matmul(c.bank_z[:, 0:P], qk[:, par, 0, SAMPLE0:TOK], qk[:, par, 1, SAMPLE0:TOK],
                                  start=True, stop=False)
                        pe.matmul(c.bank_z[:, 0:P], c.identb[:, :], c.mask_s[:, :], start=False, stop=True).then_inc(score_ok, 1)
                        return
                    b = ORDER[u]
                    q = qk[:, par, 0, META + b * P:META + (b + 1) * P]
                    w, diag = P * (b + 1), b * P
                    for a in range(0, w, 512):
                        e = min(a + 512, w)
                        mm = pe.matmul(c.bank_z[:, a:e], q, qk[:, par, 1, META + a:META + e], start=True, stop=e < w)
                    pe.matmul(c.bank_z[:, diag:w], c.identb[:, :], c.mask[:, :], start=False, stop=True).then_inc(score_ok, 1)
                    num, bank = turn_bank(h, plan, ("m", u))
                    pe.wait_ge(t_out, num + 1)
                    pe.matmul(bank[:, 0:META], q, qk[:, par, 1, 0:META], start=True, stop=True).then_inc(t_full, 1)

                def turn_cache(h, par, plan, b):
                    num, bank = turn_bank(h, plan, ("k", b))
                    pe.wait_ge(k_in[b % 2], 16 * (NB // 2 * h + b // 2 + 1))
                    pe.wait_ge(t_out, num + 1)
                    for n in range(PAST // P):
                        mm = pe.transpose(bank[:, n * P:(n + 1) * P], kc[:, b % 2, n, :], c.ident[:, :])
                    mm.then_inc(t_full, 1)

                def cache_scores(h, plan, b):
                    if b == 0:
                        pe.wait_ge(qbd_ok, h + 1)
                    pe.wait_ge(t_out, turn_bank(h, plan, ("k", b))[0] + 1 + 2)
                    pe.matmul(c.bank_s[:, 0:PAST], qbd[:, b * P:(b + 1) * P], kt[:, b % 2, :],
                              start=b == 0, stop=b == NB - 1).then_inc(kq_ok, 1)

                def turn_a(h, par, plan, u, g):
                    slot = (par + u) % 2
                    num, bank = turn_bank(h, plan, ("a", u, g))
                    if g == 0:
                        pe.wait_ge(a_ok, UNITS * h + u + 1)
                    pe.wait_ge(t_out, num + 1)
                    for m, item in enumerate(value_groups(u)[g]):
                        if item == "meta":
                            src, n = beta[:, slot, 0:META], META
                        elif item == "new":
                            src, n = beta[:, slot, PAST:PAST + P], P
                        else:
                            a = item * P + (0 if u == SAMPLE_UNIT else META)
                            src, n = beta[:, slot, a:a + P], P
                        mm = pe.transpose(bank[0:n, m * P:(m + 1) * P], src, c.ident[:, :])
                    mm.then_inc(t_full, 1)

                def weigh(h, par, plan, u, g):
                    groups, gg = value_groups(u), groups_before(u) + g
                    pe.wait_ge(t_out, turn_bank(h, plan, ("a", u, g))[0] + 1 + 2)
                    if g == 0:
                        pe.wait_ge(o_out, PROMPT_UNITS * h + prompt_units_before(u) + 1)
                    for m, item in enumerate(groups[g]):
                        t = META_TILE if item == "meta" else item
                        n = rows_of(t)
                        mm = pe.matmul(c.bank_o[:, 0:P], v[0:n, par, t, :], at[0:n, gg % 2, m * P:(m + 1) * P],
                                       start=g == 0 and m == 0, stop=g == len(groups) - 1 and m == len(groups[g]) - 1)
                    mm.then_inc(pv_ok, 1)

                def cache_values(h, par, plan, b):
                    num, bank = turn_bank(h, plan, ("v", b))
                    pe.wait_ge(t_out, num + 1)
                    pe.wait_ge(t_out, turn_bank(h, plan, ("a", SAMPLE_UNIT, 1))[0] + 1 + 2)
                    pe.wait_ge(v_in[b % 2], 16 * (NB // 2 * h + b // 2 + 1))
                    pe.matmul(bank[:, 0:DS], v[:, par, SAMPLE_TILE, :], ats[:, PAST + b * DS:PAST + (b + 1) * DS],
                              start=True, stop=False)
                    for n in range(PAST // P):
                        mm = pe.matmul(bank[:, 0:DS], vc[:, b % 2, n, :], ats[:, n * P + b * DS:n * P + (b + 1) * DS],
                                       start=False, stop=n == PAST // P - 1)
                    mm.then_inc(t_full, 1)

                def head(h, par, pairs, nxt, nxt2):
                    plan = plans[nxt]
                    pe.wait_ge(t_out, FIRST_T + NT * h + 2)
                    scores(h, par, 0, plan)
                    turn_cache(h, par, plan, 0)
                    turn_cache(h, par, plan, 1)
                    silu_gate(h, 1, z_bank(h, par, 1))
                    cache_scores(h, plan, 0)
                    cache_scores(h, plan, 1)
                    silu_gate(h, 2, z_bank(h, par, 2))
                    for slot in range(1, UNITS + 1):
                        u = slot - 1
                        if slot < UNITS:
                            scores(h, par, slot, plan)
                        groups = len(value_groups(u))
                        for g in range(min(groups, 2)):
                            turn_a(h, par, plan, u, g)
                        if nxt:
                            project(h + 1, u, proj_bank(h, par, 2 + u))
                        weighed = 0
                        for step in slot_steps(slot, nxt)[1]:
                            if slot == UNITS and step[0] == "x" and step[1] >= TILES - 2:
                                break
                            if step[0] == "k":
                                turn_cache(h, par, plan, step[1])
                            elif step[0] == "a":
                                turn_a(h, par, plan, u, step[2])
                            elif step[0] == "v":
                                cache_values(h, par, plan, step[1])
                            else:
                                turn_rows(h + 1, step[1], turn_bank(h, plan, step))
                            if u != SAMPLE_UNIT and weighed < groups:
                                weigh(h, par, plan, u, weighed)
                                weighed += 1
                        if u != SAMPLE_UNIT:
                            for g in range(weighed, groups):
                                weigh(h, par, plan, u, g)
                        if slot <= 3:
                            cache_scores(h, plan, 2 * slot)
                            cache_scores(h, plan, 2 * slot + 1)
                    if nxt:
                        project(h + 1, TILES - 1, proj_bank(h, par, 2 + TILES - 1))
                        turn_rows(h + 1, TILES - 2, turn_bank(h, plan, ("x", TILES - 2)))
                        silu_gate(h + 1, 0, proj_bank(h, par, 2 + TILES))
                        turn_rows(h + 1, TILES - 1, turn_bank(h, plan, ("x", TILES - 1)))

                pe.sem_inc(kq_ok, 2)
                pe.sem_inc(pv_ok, 2)
                for t in range(TILES):
                    project(0, t, (t, c.bank_p[t % 2]))
                    if t:
                        turn_rows(0, t - 1, (t - 1, c.bank_t[(t - 1) % 2]))
                silu_gate(0, 0, (TILES, c.bank_p[TILES % 2]))
                turn_rows(0, TILES - 1, (TILES - 1, c.bank_t[(TILES - 1) % 2]))
                all_heads(pe, head)

            @block.scalar
            def _(act):
                def split_qkv_hi(h):
                    act.wait_ge(w3_in, 48 * (h + 1))
                    for j in range(2):
                        k = slice(4 * j, 4 * j + 4)
                        act.activation(w3h[:, k, :], w3[:, k, :], ACT.Copy).then_inc(w3_hi, 1)

                def squares(h, t):
                    n, s = rows_of(t), t % 2
                    act.wait_ge(rows_ok, TILES * h + t + 1)
                    for j in range(1 if t == META_TILE else 0, 2):
                        mm = act.activation(junk[0:n, j, :], qkn[0:n, s, j * P:(j + 1) * P], ACT.Square,
                                            accum_out=ss[0:n, s, j:j + 1])
                    mm.then_inc(sq_ok, 1)

                def copy_rows(q, t, number):
                    n, (c0, c1) = rows_of(t), tile_cols(t)
                    num, bank = number
                    act.wait_ge(t_full, num + 1)
                    if t == META_TILE:
                        act.activation(qk[:, q, 1, c0:c1], bank[:, P:P + n], ACT.Copy).then_inc(t_out, 1)
                    else:
                        act.activation(qk[:, q, :, c0:c1], bank[:, 0:2 * P].rearrange("p (a n) -> p a n", a=2),
                                       ACT.Copy).then_inc(t_out, 1)

                def sigmoids(slot, parts, first, second):
                    for m, (dst, scale, sem) in enumerate([(keep, -SCALE, first), (beta, SCALE, second)]):
                        for n, (a, e, z) in enumerate(parts):
                            mm = act.activation(dst[:, slot, a:e], z, ACT.Sigmoid, scale=scale)
                        if sem is not None:
                            mm.then_inc(sem, 1)

                def betas(h, par, u, plan):
                    slot, w = (par + u) % 2, width(u)
                    act.wait_ge(score_ok, UNITS * h + u + 1)
                    if u == SAMPLE_UNIT:
                        act.wait_ge(kq_ok, NB * h + NB + 2)
                        sigmoids(slot, [(0, PAST, c.bank_s[:, :]), (PAST, PAST + P, c.bank_z[:, 0:P])], keep_ok, beta_ok)
                        return
                    num, bank = turn_bank(h, plan, ("m", u))
                    act.wait_ge(t_full, num + 1)
                    sigmoids(slot, [(0, META, bank[:, 0:META])], None, t_out)
                    sigmoids(slot, [(META, w, c.bank_z[:, 0:w - META])], keep_ok, beta_ok)

                def copy_cache_k(h, plan, b):
                    num, bank = turn_bank(h, plan, ("k", b))
                    act.wait_ge(t_full, num + 1)
                    act.wait_ge(kq_ok, NB * h + b + 1)
                    act.activation(kt[:, b % 2, :], bank[:, :], ACT.Copy).then_inc(t_out, 1)

                def copy_a(h, plan, u, g):
                    items, gg = value_groups(u)[g], groups_before(u) + g
                    num, bank = turn_bank(h, plan, ("a", u, g))
                    act.wait_ge(t_full, num + 1)
                    if u == SAMPLE_UNIT:
                        a, n = (PAST, P) if items == ["new"] else (0, PAST)
                        act.activation(ats[:, a:a + n], bank[:, 0:n], ACT.Copy).then_inc(t_out, 1)
                        return
                    act.wait_ge(pv_ok, NGROUPS * h + gg + 1)
                    a = 0
                    if items[0] == "meta":
                        a = P
                        act.activation(at[0:META, gg % 2, 0:P], bank[0:META, 0:P], ACT.Copy)
                    act.activation(at[:, gg % 2, a:len(items) * P], bank[:, a:len(items) * P], ACT.Copy).then_inc(t_out, 1)

                def copy_o(h, plan, b):
                    num, bank = turn_bank(h, plan, ("v", b))
                    act.wait_ge(t_full, num + 1)
                    act.activation(ot[:, SEQ + b * DS:SEQ + (b + 1) * DS], bank[:, 0:DS], ACT.Copy).then_inc(t_out, 1)

                def z_sigmoid(h, n, number):
                    c0, c1 = CHL[n]
                    num, bank = number
                    hold(act, proj_ok, num + 1)
                    act.activation(zs[:, c0 - META:c1 - META], bank[:, 0:c1 - c0], ACT.Sigmoid,
                                   bias=c.bias[:, head_block("z_s", h)]).then_inc(zsig_ok, 1)

                def split_y_hi(k, src):
                    act.activation(c.xh[:, k, 0:LIVE], src, ACT.Copy).then_inc(yh_ok, 1)

                def head(h, par, pairs, nxt, nxt2):
                    plan = plans[nxt]

                    def turned(step):
                        if step[0] == "k":
                            copy_cache_k(h, plan, step[1])
                        elif step[0] == "a":
                            copy_a(h, plan, step[1], step[2])
                        elif step[0] == "v":
                            copy_o(h, plan, step[1])
                        elif step[0] == "x":
                            copy_rows(1 - par, step[1], turn_bank(h, plan, step))

                    betas(h, par, 0, plan)
                    turned(("k", 0))
                    turned(("k", 1))
                    if nxt:
                        split_qkv_hi(h + 1)
                    z_sigmoid(h, 1, z_bank(h, par, 1))
                    z_sigmoid(h, 2, z_bank(h, par, 2))
                    for slot in range(1, UNITS + 1):
                        before, after = slot_steps(slot, nxt)
                        if slot < UNITS:
                            betas(h, par, slot, plan)
                        for step in before:
                            turned(step)
                        for step in after:
                            if slot < UNITS or step[1] < TILES - 2:
                                turned(step)
                        if nxt:
                            squares(h + 1, slot - 1)
                        if slot == 1 and nxt:
                            wz.split_hi(act, h + 1, 0)
                        if not nxt and slot < UNITS - 1:
                            k = slot - 1
                            act.wait_ge(y_in[k % 2], 16 * (k // 2 + 1))
                            split_y_hi(k, y_again[:, (k % 2) * LIVE:(k % 2 + 1) * LIVE])
                    if nxt:
                        turned(("x", TILES - 2))
                        squares(h + 1, TILES - 1)
                        act.wait_ge(y_ok, h + 1)
                        z_sigmoid(h + 1, 0, proj_bank(h, par, 2 + TILES))
                        turned(("x", TILES - 1))
                    else:
                        act.wait_ge(y_ok, HEADS)
                        split_y_hi(HEADS - 1, ot[:, :])

                act.sem_inc(t_out, 2)
                act.sem_inc(beta_ok, 1)
                split_qkv_hi(0)
                wz.split_hi(act, 0, 0)
                for t in range(TILES):
                    squares(0, t)
                    if t:
                        copy_rows(0, t - 1, (t - 1, c.bank_t[(t - 1) % 2]))
                z_sigmoid(0, 0, (TILES, c.bank_p[TILES % 2]))
                copy_rows(0, TILES - 1, (TILES - 1, c.bank_t[(TILES - 1) % 2]))
                all_heads(act, head)

            @block.vector
            def _(dve):
                def rows(h, q, pairs, t, number):
                    n, s = rows_of(t), t % 2
                    a = P if t == META_TILE else 0
                    num, bank = number
                    dve.wait_ge(proj_ok, num + 1)
                    if t == 0:
                        dve.wait_ge(b3_in[q], 48 * (pairs + 1))
                        dve.wait_ge(v_stored[q], 16 * TILES * pairs + 16)
                    dve.wait_ge(k_stored[s], 16 * (TILES // 2) * h + 16 * (t // 2) + 16)
                    dve.tensor_tensor(qkn[0:n, s, a:2 * P], bank[0:n, a:2 * P], bias3[0:n, q, a:2 * P],
                                      ALU.add).then_inc(rows_ok, 1)
                    dve.tensor_tensor(v[0:n, q, t, :], bank[0:n, 2 * P:3 * P], bias3[0:n, q, 2 * P:3 * P],
                                      ALU.add).then_inc(proj_out, 1)

                def normalise(h, t):
                    n, s = rows_of(t), t % 2
                    dve.wait_ge(rstd_ok, TILES * h + t + 1)
                    for j in range(1 if t == META_TILE else 0, 2):
                        mm = dve.scalar_tensor_tensor(out=qkn[0:n, s, j * P:(j + 1) * P], in0=qkn[0:n, s, j * P:(j + 1) * P],
                                                      scalar=rs[0:n, s, j:j + 1], in1=gain[0:n, j, :],
                                                      op0=ALU.mult, op1=ALU.mult)
                    mm.then_inc(norm_ok, 1)

                def sticks(h, par, u):
                    slot, w, n = (par + u) % 2, width(u), UNITS * h + u
                    dve.wait_ge(keep_ok, n + 1)
                    young_first = keep[:, slot, 0:w][:, ::-1]
                    dve.tensor_tensor_scan(young_first, young_first, young_first, 1.0,
                                           ALU.mult, ALU.bypass).then_inc(scan_ok, 1)
                    dve.wait_ge(scan_ok, n + 1)
                    dve.wait_ge(beta_ok, n + 1 + 1)
                    dve.tensor_tensor(beta[:, slot, 0:w - 1], beta[:, slot, 0:w - 1], keep[:, slot, 1:w],
                                      ALU.mult).then_inc(a_ok, 1)

                def take_o(h, u):
                    if u == SAMPLE_UNIT:
                        return
                    if u == 0:
                        dve.wait_ge(y_stored, 16 * h + 16)
                    a = ORDER[u] * P
                    dve.wait_ge(pv_ok, NGROUPS * h + groups_before(u + 1) + 2)
                    dve.tensor_copy(ot[:, a:a + P], c.bank_o[:, 0:P]).then_inc(o_out, 1)

                def z_silu(h, n, number):
                    c0, c1 = CHL[n]
                    z = zs[:, c0 - META:c1 - META]
                    dve.wait_ge(zsig_ok, 3 * h + n + 1)
                    dve.scalar_tensor_tensor(out=z, in0=number[1][:, 0:c1 - c0],
                                             scalar=c.bias[:, head_block("z_s", h)], in1=z,
                                             op0=ALU.add, op1=ALU.mult).then_inc(proj_out, 1)

                def split_y_lo(k, src):
                    dve.wait_ge(yh_ok, k + 1)
                    dve.tensor_tensor(c.xl[:, k, 0:LIVE], src, c.xh[:, k, 0:LIVE].bitcast(F32), ALU.subtract).then_inc(yl_ok, 1)

                def head(h, par, pairs, nxt, nxt2):
                    plan = plans[nxt]
                    sticks(h, par, 0)
                    for n in (1, 2):
                        z_silu(h, n, z_bank(h, par, n))
                    for slot in range(1, UNITS + 1):
                        if slot < UNITS:
                            sticks(h, par, slot)
                        if nxt:
                            rows(h + 1, 1 - par, pairs + par, slot - 1, proj_bank(h, par, 2 + slot - 1))
                        take_o(h, slot - 1)
                        if nxt:
                            normalise(h + 1, slot - 1)
                        elif slot < UNITS - 1:
                            k = slot - 1
                            split_y_lo(k, y_again[:, (k % 2) * LIVE:(k % 2 + 1) * LIVE])
                    dve.wait_ge(o_out, PROMPT_UNITS * h + PROMPT_UNITS + 1)
                    dve.wait_ge(t_out, turn_bank(h, plan, ("v", NB - 1))[0] + 1 + 2)
                    dve.tensor_tensor(ot[:, :], zs[:, :], ot[:, :], ALU.mult).then_inc(y_ok, 1)
                    if nxt:
                        rows(h + 1, 1 - par, pairs + par, TILES - 1, proj_bank(h, par, 2 + TILES - 1))
                        normalise(h + 1, TILES - 1)
                        z_silu(h + 1, 0, proj_bank(h, par, 2 + TILES))
                    else:
                        split_y_lo(HEADS - 1, ot[:, :])

                dve.sem_inc(proj_out, 2)
                dve.sem_inc(o_out, 1)
                dve.wait_ge(gain_in, 32)
                for t in range(TILES):
                    rows(0, 0, 0, t, (t, c.bank_p[t % 2]))
                    normalise(0, t)
                z_silu(0, 0, (TILES, c.bank_p[TILES % 2]))
                all_heads(dve, head)


def merge(c, d, mh, ml):
    nc = c.nc
    so_cols = d["w_sb_o"][0].rearrange("(k p) (n e) -> p k n e", p=P, e=P)
    with ExitStack() as ctx:
        w = WeightTiles(c, ctx, "ws", 2, 2)
        sg = c.sb(ctx, "gate_s", [P, 2, LIVE])
        m1 = c.sb(ctx, "m_part", [P, 2, LIVE])
        g_in = [c.sem(f"gate_s_in{s}") for s in range(2)]
        m_in = [c.sem(f"m_part_in{s}") for s in range(2)]
        full = c.sem("so_bank_full")
        gated, summed = c.sem("so_gated"), c.sem("m_summed")
        mh_ok, ml_ok = c.sem("m_hi_ok"), c.sem("m_lo_ok")
        banks = [c.bank_p[0], c.bank_p[1], c.bank_o, c.bank_z[:, 0:512], c.bank_z[:, 512:1024], c.bank_s[:, :]]

        with nc.Block() as block:
            @block.sync
            def _(sp):
                for s in range(2):
                    w.load(sp, 0, s, so_cols[:, :, s, :])

                def one_pair(i, more):
                    for s in range(2):
                        sp.wait_ge(ml_ok, 2 * i + s + 1)
                        sp.dma_start(sg[:, s, :], d["sgate"][bass.ds(2 * i + s, 1)].rearrange("o p n -> (o p) n")).then_inc(g_in[s], 16)
                        sp.dma_start(m1[:, s, :], d["m1"][bass.ds(2 * i + s, 1)].rearrange("o p n -> (o p) n")).then_inc(m_in[s], 16)
                        if more:
                            w.load(sp, i + 1, s, so_cols[:, :, bass.ds(2 * i + 2 + s, 1), :])

                with sp.Fori(0, KC // 2 - 1) as i:
                    one_pair(i, True)
                one_pair(KC // 2 - 1, False)

            @block.gpsimd
            def _(pool):
                w.start_pool(pool)
                with pool.Fori(0, KC // 2) as i:
                    for s in range(2):
                        w.split_lo(pool, i, s)

            @block.scalar
            def _(act):
                for s in range(2):
                    w.split_hi(act, 0, s)

                def one_pair(i, more):
                    for s in range(2):
                        if more:
                            act.wait_ge(full, 6 * i + 3 * s + 3)
                            w.split_hi(act, i + 1, s)
                        hold(act, summed, 6 * i + 3 * s + 3)
                        act.activation(row(mh, 2 * i + s, 0, LIVE), m1[:, s, :], ACT.Copy).then_inc(mh_ok, 1)

                with act.Fori(0, KC // 2 - 1) as i:
                    one_pair(i, True)
                one_pair(KC // 2 - 1, False)

            @block.vector
            def _(dve):
                dve.sem_inc(ml_ok, 2)
                dve.sem_inc(gated, 6)
                with dve.Fori(0, KC // 2) as i:
                    for s in range(2):
                        dve.wait_ge(g_in[s], 16 * i + 16)
                        dve.wait_ge(m_in[s], 16 * i + 16)
                        for n, (c0, c1) in enumerate(CHL):
                            a, b = c0 - META, c1 - META
                            dve.wait_ge(full, 6 * i + 3 * s + n + 1)
                            dve.tensor_tensor(sg[:, s, a:b], banks[3 * s + n][:, 0:b - a], sg[:, s, a:b], ALU.mult).then_inc(gated, 1)
                            dve.wait_ge(gated, 6 * i + 3 * s + n + 1 + 6)
                            dve.tensor_tensor(m1[:, s, a:b], m1[:, s, a:b], sg[:, s, a:b], ALU.add).then_inc(summed, 1)
                        dve.wait_ge(mh_ok, 2 * i + s + 1)
                        dve.tensor_tensor(row(ml, 2 * i + s, 0, LIVE), m1[:, s, :],
                                          row(mh, 2 * i + s, 0, LIVE).bitcast(F32), ALU.subtract).then_inc(ml_ok, 1)

            @block.tensor
            def _(pe):
                with pe.Fori(0, KC // 2) as i:
                    for s in range(2):
                        w.ready(pe, i, s)
                        for n, (c0, c1) in enumerate(CHL):
                            a, b = c0 - META, c1 - META
                            pe.wait_ge(gated, 6 * i + 3 * s + n + 1)
                            w.product(pe, s, banks[3 * s + n][:, 0:b - a],
                                      x_moving(c, a, b)).then_inc(full, 1)


def output(c, d, mh, ml):
    nc = c.nc
    o_cols = d["w_o"][0].rearrange("(k p) (n e) -> p k n e", p=P, e=P)
    x_tiles = d["x_prompt"][0].rearrange("(t p) (n e) -> p t n e", p=P, e=P)
    y_tiles = d["y_prompt"][0].rearrange("(t p) (n e) -> p t n e", p=P, e=P)
    xs_rows = d["x_sample"].rearrange("b s (n e) -> (b s) n e", e=P)
    ys_rows = d["y_sample"].rearrange("b s (n e) -> (b s) n e", e=P)
    groups = [(0, 4), (4, 8), (8, 9)]
    with ExitStack() as ctx:
        w = WeightTiles(c, ctx, "wo", 2, 2)
        xt = c.sb(ctx, "x_again", [P, 2, PT + 1, P])
        yt = c.sb(ctx, "y_turned", [P, 2, LIVE])
        yo = c.sb(ctx, "y_rows", [P, 2, PT + 1, P])
        x_in = [c.sem(f"x_again_in{s}") for s in range(2)]
        full = c.sem("o_bank_full")
        copied = c.sem("o_copied")
        turned = c.sem("o_turned")
        added = c.sem("o_added")
        stored = [c.sem(f"y_stored{s}") for s in range(2)]
        banks = [c.bank_p[0], c.bank_p[1], c.bank_o]
        tbanks = [c.bank_t[0], c.bank_t[1], c.bank_z[:, 0:512]]

        with nc.Block() as block:
            @block.sync
            def _(sp):
                def load_x(i, s):
                    n = bass.ds(2 * i + s, 1)
                    sp.dma_start(xt[:, s, 0:PT, :], x_tiles[:, :, n, :].rearrange("p t o e -> p t (o e)")).then_inc(x_in[s], 16)
                    sp.dma_start(xt[:, s, PT, :], xs_rows[:, n, :].rearrange("p o e -> p (o e)")).then_inc(x_in[s], 16)

                def one_pair(i, more):
                    for s in range(2):
                        n = bass.ds(2 * i + s, 1)
                        if more:
                            w.load(sp, i + 1, s, o_cols[:, :, bass.ds(2 * i + 2 + s, 1), :])
                        sp.wait_ge(added, 6 * i + 3 * s + 3 + 6)
                        sp.dma_start(y_tiles[:, :, n, :].rearrange("p t o e -> p t (o e)"), yo[:, s, 0:PT, :]).then_inc(stored[s], 16)
                        sp.dma_start(ys_rows[:, n, :].rearrange("p o e -> p (o e)"), yo[:, s, PT, :]).then_inc(stored[s], 16)
                        if more:
                            load_x(i + 1, s)

                for s in range(2):
                    sp.sem_inc(stored[s], 32)
                    w.load(sp, 0, s, o_cols[:, :, s, :])
                    load_x(0, s)
                with sp.Fori(0, KC // 2 - 1) as i:
                    one_pair(i, True)
                one_pair(KC // 2 - 1, False)
                for s in range(2):
                    sp.wait_ge(stored[s], 32 * (KC // 2 + 1))

            @block.gpsimd
            def _(pool):
                w.start_pool(pool)
                with pool.Fori(0, KC // 2) as i:
                    w.split_lo(pool, i, 0)
                    w.split_lo(pool, i, 1)

            @block.scalar
            def _(act):
                w.split_hi(act, 0, 0)
                w.split_hi(act, 0, 1)

                def one_pair(i, more):
                    for s in range(2):
                        for n, (c0, c1) in enumerate(CHL):
                            act.wait_ge(full, 6 * i + 3 * s + n + 1)
                            act.activation(yt[:, s, c0 - META:c1 - META], banks[n][:, 0:c1 - c0], ACT.Copy).then_inc(copied, 1)
                        if more:
                            w.split_hi(act, i + 1, s)

                with act.Fori(0, KC // 2 - 1) as i:
                    one_pair(i, True)
                one_pair(KC // 2 - 1, False)

            @block.vector
            def _(dve):
                dve.sem_inc(added, 6)
                with dve.Fori(0, KC // 2) as i:
                    for s in range(2):
                        dve.wait_ge(x_in[s], 32 * i + 32)
                        dve.wait_ge(stored[s], 32 * i + 32)
                        for g, (a, b) in enumerate(groups):
                            dve.wait_ge(turned, 6 * i + 3 * s + g + 1)
                            dve.tensor_tensor(yo[:, s, a:b, :], tbanks[g][:, 0:(b - a) * P].rearrange("p (t e) -> p t e", e=P),
                                              xt[:, s, a:b, :], ALU.add).then_inc(added, 1)

            @block.tensor
            def _(pe):
                def product(i, s, first=False):
                    w.ready(pe, i, s)
                    for n, (c0, c1) in enumerate(CHL):
                        a, b = c0 - META, c1 - META
                        if not first:
                            pe.wait_ge(copied, 6 * i + 3 * s + n + 1 - 3)
                        w.product(pe, s, banks[n][:, 0:b - a],
                                  (lambda k: mh[:, k, a:b], lambda k: ml[:, k, a:b])).then_inc(full, 1)

                def turn(i, s):
                    for g, (a, b) in enumerate(groups):
                        pe.wait_ge(copied, 6 * i + 3 * s + (2, 3, 3)[g])
                        pe.wait_ge(added, 6 * i + 3 * s + g + 1 + 3)
                        for t in range(a, b):
                            mm = pe.transpose(tbanks[g][:, (t - a) * P:(t - a + 1) * P], yt[:, s, t * P:(t + 1) * P],
                                              c.ident[:, :])
                        mm.then_inc(turned, 1)

                product(0, 0, first=True)
                with pe.Fori(0, KC // 2 - 1) as i:
                    product(i, 1)
                    turn(i, 0)
                    product(i + 1, 0)
                    turn(i, 1)
                product(KC // 2 - 1, 1)
                turn(KC // 2 - 1, 0)
                turn(KC // 2 - 1, 1)


def build(nc, d):
    d["m1"] = nc.dram_tensor("m_part_scratch", (KC, P, LIVE), F32).ap()
    d["sgate"] = nc.dram_tensor("gate_scratch", (KC, P, LIVE), F32).ap()
    d["ys"] = nc.dram_tensor("y_s_scratch", (HEADS, P, LIVE), F32).ap()
    with ExitStack() as ctx:
        c = Core(nc, ctx)
        HELD["waits_held"] = c.sem("waits_held")
        c.bank_z = ctx.enter_context(nc.psum_tensor("bank_z", [P, 2 * 512], F32))
        c.bank_s = ctx.enter_context(nc.psum_tensor("bank_s", [P, 512], F32))
        c.bank_p = [ctx.enter_context(nc.psum_tensor(f"bank_p{i}", [P, 512], F32)) for i in range(2)]
        c.bank_t = [ctx.enter_context(nc.psum_tensor(f"bank_t{i}", [P, 512], F32)) for i in range(2)]
        c.bank_o = ctx.enter_context(nc.psum_tensor("bank_o", [P, 512], F32))
        c.ident, c.identb = c.sb(ctx, "ident", [P, P]), c.sb(ctx, "ident_bf16", [P, P], BF16)
        c.mask, c.mask_s = c.sb(ctx, "mask", [P, P], BF16), c.sb(ctx, "mask_samples", [P, P], BF16)
        c.bias = c.sb(ctx, "bias_turned", [P, 80])
        with ExitStack() as xs:
            c.xh = c.sb(xs, "x_hi", [P, KC, TOK], F32R)
            c.xl = c.sb(xs, "x_lo", [P, KC, TOK], F32R)
            with ExitStack() as ys:
                c.conv_w = c.sb(ys, "conv_w_turned", [P, KC, 3])
                c.state = c.sb(ys, "state_turned", [P, KC, 2 * NB])
                constants_and_norm(c, d)
                yh = c.sb(ys, "y_c_hi", [P, KC, LIVE], F32R)
                yl = c.sb(ys, "y_c_lo", [P, KC, LIVE], F32R)
                conv_branch(c, d, yh, yl)
                conv_gates(c, d, yh, yl)
            attention(c, d)
            mh = c.sb(xs, "m_hi", [P, KC, LIVE], F32R)
            ml = c.sb(xs, "m_lo", [P, KC, LIVE], F32R)
            merge(c, d, mh, ml)
            output(c, d, mh, ml)


INPUTS = ["x_prompt", "x_sample", "cache_k", "cache_v", "state_conv", "meta_tokens", "norm_g", "w_in", "b_in",
          "q_norm_g", "k_norm_g", "conv_w", "w_conv_o", "w_sb_o", "w_o"]
OUTPUTS = [("y_prompt", (1, SEQ, D)), ("y_sample", (NB, DS, D)), ("k_prompt", (1, 1, SAMPLE0, HEADS, HD)),
           ("v_prompt", (1, 1, SAMPLE0, HEADS, HD)), ("conv_prompt", (1, 1, 2, D)),
           ("k_sample", (1, NB, DS, HEADS, HD)), ("v_sample", (1, NB, DS, HEADS, HD)), ("conv_sample", (1, NB, 2, D))]


def kernel(**inputs):
    import numpy as np
    import concourse.bacc as bacc
    from concourse.bass_utils import run_bass_kernel_spmd as run

    nc = bacc.Bacc("TRN2", target_bir_lowering=False, num_devices=1)
    arrays, d = {}, {}
    for name in INPUTS:
        a = np.ascontiguousarray(inputs[name])
        arrays["in_" + name] = a
        d[name] = nc.dram_tensor("in_" + name, a.shape, mybir.dt.from_np(a.dtype), kind="ExternalInput").ap()
    for name, shape in OUTPUTS:
        d[name] = nc.dram_tensor("out_" + name, shape, F32, kind="ExternalOutput").ap()
    build(nc, d)
    r = run(nc, [arrays], core_ids=[0])
    return tuple(r.results[0]["out_" + name] for name, _ in OUTPUTS)
```

```python
from collections import namedtuple
from contextlib import ExitStack

import concourse.bass as bass
from concourse import mybir

F32 = mybir.dt.float32
F32R = mybir.dt.float32r
BF16 = mybir.dt.bfloat16
ALU = mybir.AluOpType
ACT = mybir.ActivationFunctionType

P = 128
D = 1024
KC = D // P
META, SEQ, NB, DS, PAST = 16, 1024, 8, 16, 512
HEADS, HD = 8, 128
PT = SEQ // P
SAMPLE0 = META + SEQ
TOK = SAMPLE0 + NB * DS
LIVE = TOK - META
TILES = PT + 2
SAMPLE_TILE, META_TILE = PT, PT + 1
EPS = 1e-6
SCALE = HD ** -0.5
HIDDEN = -1e30
OFF = {n: i * D for i, n in enumerate(["B", "C", "h", "z_c", "q", "k", "v", "z_s", "g_c", "g_s"])}
CH = [(0, META + 384), (META + 384, META + 768), (META + 768, TOK)]
CHL = [(META, META + 384), (META + 384, META + 768), (META + 768, TOK)]
LIVE_CHUNKS = [(a - META, e - META) for a, e in CHL]


def tile_cols(t):
    if t == META_TILE:
        return 0, META
    return META + t * P, META + (t + 1) * P


def row(t, i, a, b):
    return t[:, bass.ds(i, 1), a:b].rearrange("p o n -> p (o n)")


def split_product(pe, out, left, right, ks=range(KC)):
    (lh, ll), (rh, rl) = left, right
    for k in ks:
        pe.matmul(out, lh(k), rh(k), start=k == 0, stop=False)
        pe.matmul(out, lh(k), rl(k), start=False, stop=False)
        mm = pe.matmul(out, ll(k), rh(k), start=False, stop=k == KC - 1)
    return mm


class Group:
    pass


Programs = namedtuple("Programs", "sync gpsimd tensor scalar vector")


class Core:

    def __init__(self, nc, ctx):
        self.nc, self.ctx = nc, ctx

    def sem(self, name):
        return self.ctx.enter_context(self.nc.semaphore(name))

    def sb(self, ctx, name, shape, dt=F32):
        return ctx.enter_context(self.nc.sbuf_tensor(name, shape, dt))


HELD = {}


def hold(eng, sem, value):
    eng.wait_ge(sem, value)
    eng.sem_inc(HELD["waits_held"], 1)


class WeightTiles:

    def __init__(self, c, ctx, name, slots, per_round, after=None, rounds=0):
        self.slots, self.per_round, self.base = slots, per_round, 0
        if after is not None:
            self.base = after.base + rounds * after.per_round
            self.raw, self.hi, self.lo = after.raw, after.hi, after.lo
            self.raw_in, self.hi_ok, self.lo_ok = after.raw_in, after.hi_ok, after.lo_ok
            return
        self.raw = c.sb(ctx, name + "_raw", [P, slots, KC, P])
        self.hi = c.sb(ctx, name + "_hi", [P, slots, KC, P], F32R)
        self.lo = c.sb(ctx, name + "_lo", [P, slots, KC, P], F32R)
        self.raw_in = [c.sem(f"{name}_raw_in{s}") for s in range(slots)]
        self.hi_ok, self.lo_ok = c.sem(name + "_hi_ok"), c.sem(name + "_lo_ok")

    def continued(self, rounds, per_round):
        return WeightTiles(None, None, None, self.slots, per_round, self, rounds)

    def count(self, i, j):
        return i * self.per_round + (self.base + j)

    def start_pool(self, pool):
        pool.sem_inc(self.lo_ok, self.slots)

    def load(self, sp, i, j, src):
        s = j % self.slots
        sp.wait_ge(self.lo_ok, self.count(i, j) + 1)
        sp.dma_start(self.raw[:, s, :, :], src).then_inc(self.raw_in[s], 16)

    def split_hi(self, act, i, j):
        s = j % self.slots
        loads = i * (self.per_round // self.slots) + (self.base + j) // self.slots + 1
        act.wait_ge(self.raw_in[s], 16 * loads)
        act.activation(self.hi[:, s, :, :], self.raw[:, s, :, :], ACT.Copy).then_inc(self.hi_ok, 1)

    def split_lo(self, pool, i, j):
        s = j % self.slots
        pool.wait_ge(self.hi_ok, self.count(i, j) + 1)
        pool.tensor_tensor(self.lo[:, s, :, :], self.raw[:, s, :, :], self.hi[:, s, :, :].bitcast(F32),
                           ALU.subtract).then_inc(self.lo_ok, 1)

    def ready(self, pe, i, j):
        pe.wait_ge(self.lo_ok, self.count(i, j) + 1 + self.slots)

    def product(self, pe, j, out, right, ks=range(KC)):
        s = j % self.slots
        return split_product(pe, out, (lambda k: self.hi[:, s, k, :], lambda k: self.lo[:, s, k, :]), right, ks)


def x_moving(c, c0, c1):
    return (lambda k: c.xh[:, k, c0:c1], lambda k: c.xl[:, k, c0:c1])


NORM_ORDER = [META_TILE] + list(range(PT + 1))
CHUNK_TILES = [4, 7, 10]
C_HALVES = {5: (0, range(KC // 2)), 6: (0, range(KC // 2, KC)), 7: (1, range(KC // 2)), 9: (1, range(KC // 2, KC))}


def front(c, d):
    w_cols = d["w_in"][0].rearrange("(k p) (n e) -> p k n e", p=P, e=P)
    co_cols = d["w_conv_o"][0].rearrange("(k p) (n e) -> p k n e", p=P, e=P)
    names = ["C", "h", "B", "z_c"]
    with ExitStack() as ctx:
        conv_w = c.sb(ctx, "conv_w_turned", [P, KC, 3])
        state = c.sb(ctx, "state_turned", [P, KC, 2 * NB])
        w = WeightTiles(c, ctx, "w", 2, 4)
        wg = w.continued(KC, 6)
        last = c.sb(ctx, "last_u", [P, KC, 2 + NB * 2])
        last_rows = c.sb(ctx, "last_u_rows", [2 + NB * 2, D])
        with ExitStack() as conv:
            cs = c.sb(conv, "c_part", [P, TOK])
            up = c.sb(conv, "u_prompt", [P, SAMPLE0])
            us = c.sb(conv, "u_sample", [P, NB, DS + 2])
            tap = c.sb(conv, "conv_out", [P, LIVE])
            sg = c.sb(conv, "sig_z", [P, LIVE])
            yt = c.sb(conv, "y_conv", [P, LIVE])
            c.sb(conv, "room_for_w3", [P, 1000])
            with ExitStack() as norm:
                gb = c.sb(norm, "norm_gain", [1, D])
                ones = c.sb(norm, "ones", [1, P])
                b80 = c.sb(norm, "bias_rows", [80, P])
                cw3 = c.sb(norm, "conv_w_rows", [3, D])
                st16 = c.sb(norm, "state_rows", [NB * 2, D])
                xr = c.sb(norm, "x_rows", [P, 4, D])
                junk = c.sb(norm, "squares", [P, D])
                xn = c.sb(norm, "x_normed", [P, 3, D])
                ss = c.sb(norm, "sumsq", [P, TILES])
                ms = c.sb(norm, "meansq", [P, TILES])
                rs = c.sb(norm, "rstd", [P, TILES])
                half = c.sb(norm, "minus_half", [P, TILES])
            yh = c.sb(conv, "y_c_hi", [P, KC, LIVE], F32R)
            yl = c.sb(conv, "y_c_lo", [P, KC, LIVE], F32R)
        gate = c.sb(ctx, "gate_c", [P, LIVE])
        outs = c.sb(ctx, "gates_out", [P, 2, LIVE])

    x_in = [c.sem(f"x_in{i}") for i in range(4)]
    gain_in, gain_ok, small_in = c.sem("norm_gain_in"), c.sem("norm_gain_spread"), c.sem("small_in")
    made = c.sem("constants_made")
    squared, mean_ok, rstd_ok = c.sem("x_squared"), c.sem("x_mean"), c.sem("x_rstd")
    normed, turned = c.sem("x_is_normed"), c.sem("x_turned")
    hi_ok, lo_ok = c.sem("x_hi"), c.sem("x_lo")
    small_turned, small_out = c.sem("small_turned"), c.sem("small_out")

    full = c.sem("conv_bank_full")
    c_out = c.sem("c_out")
    d_out = c.sem("hbz_out")
    u_ok = c.sem("u_ok")
    tap_ok = c.sem("tap_ok")
    sig_ok = c.sem("sig_ok")
    y_ok = c.sem("y_ok")
    yh_ok = c.sem("yh_ok")
    yl_ok = c.sem("yl_ok")
    last_ok = c.sem("last_ok")
    last_turned, last_out = c.sem("last_turned"), c.sem("last_out")
    stored = c.sem("conv_state_stored")

    g_full = c.sem("gate_bank_full")
    g_ok = c.sem("gate_c_ok")
    m_ok = c.sem("m1_ok")
    s_ok = c.sem("gate_s_ok")
    m_stored, s_stored = c.sem("m1_stored"), c.sem("gate_s_stored")
    x_banks = [c.bank_t, (c.bank_s, c.bank_o)]
    small_bank = c.bank_p[1]
    banks = [c.bank_p[0], c.bank_p[1]]
    g_banks = [c.bank_p[0], c.bank_p[1], c.bank_o]
    rows = [META if t == META_TILE else P for t in NORM_ORDER]

    def source(t):
        if t == META_TILE:
            return d["meta_tokens"]
        if t == SAMPLE_TILE:
            return d["x_sample"].rearrange("b s d -> (b s) d")
        return d["x_prompt"][0, t * P:(t + 1) * P, :]

    def bias(name, i):
        return c.bias[:, bass.ds(i + OFF[name] // P, 1)]

    def gate_tile(j, i):
        b = i + j // 3
        if j % 3 == 1:
            return co_cols[:, :, bass.ds(b, 1), :]
        return w_cols[:, :, bass.ds(b + OFF["g_s" if j % 3 else "g_c"] // P, 1), :]

    def sync(sp, load_qkv, first_loads):
        def load_conv(i, j):
            w.load(sp, i, j, w_cols[:, :, bass.ds(i + OFF[names[j]] // P, 1), :])

        for p, t in enumerate(NORM_ORDER):
            if p >= 4:
                sp.wait_ge(normed, p - 3)
            sp.dma_start(xr[0:rows[p], p % 4, :], source(t)).then_inc(x_in[p % 4], 16)
            if p == 0:
                sp.dma_start(gb[:, :], d["norm_g"]).then_inc(gain_in, 16)
            if p == 2:
                load_conv(0, 0)
            if p == 3:
                sp.dma_start(b80[:, :], d["b_in"].rearrange("o (n p) -> (o n) p", p=P)).then_inc(small_in, 16)
                sp.dma_start(cw3[:, :], d["conv_w"][0]).then_inc(small_in, 16)
                sp.dma_start(st16[:, :], d["state_conv"][0].rearrange("b j c -> (b j) c")).then_inc(small_in, 16)
            if p == 5:
                load_conv(0, 1)
        load_conv(0, 2)
        load_conv(0, 3)
        with sp.Fori(1, KC) as i:
            for j in range(4):
                load_conv(i, j)

        sp.sem_inc(m_stored, 16)
        sp.sem_inc(s_stored, 16)

        def load_gate(i, j):
            i, j = (i, j) if j < 6 else (i + 1, j - 6)
            wg.load(sp, i, j, gate_tile(j, 2 * i))

        def two_blocks(i, more):
            for b in range(2):
                if b == 0 or more:
                    load_gate(i, 3 * b + 3)
                    load_gate(i, 3 * b + 4)
                n = 2 * i + b
                if b and not more:
                    sp.wait_ge(yl_ok, 3 * KC)
                    load_qkv(sp, 0)
                sp.wait_ge(m_ok, 3 * n + 3)
                sp.dma_start(d["m1"][bass.ds(n, 1)].rearrange("o p n -> (o p) n"), outs[:, 0, :]).then_inc(m_stored, 16)
                if b == 0 or more:
                    load_gate(i, 3 * b + 5)
                else:
                    first_loads(sp)
                sp.wait_ge(s_ok, 3 * n + 3 + 3)
                sp.dma_start(d["sgate"][bass.ds(n, 1)].rearrange("o p n -> (o p) n"), outs[:, 1, :]).then_inc(s_stored, 16)

        for j in range(3):
            load_gate(0, j)
        sp.wait_ge(last_out, 2)
        sp.dma_start(d["conv_prompt"][0, 0], last_rows[0:2, :]).then_inc(stored, 16)
        sp.dma_start(d["conv_sample"][0].rearrange("b j c -> (b j) c"), last_rows[2:18, :]).then_inc(stored, 16)
        with sp.Fori(0, KC // 2 - 1) as i:
            two_blocks(i, True)
        two_blocks(KC // 2 - 1, False)
        sp.wait_ge(stored, 32)
        sp.wait_ge(m_stored, 16 * (KC + 1))
        sp.wait_ge(s_stored, 16 * (KC + 1))

    def gpsimd(pool):
        w.start_pool(pool)
        pool.memset(c.ident[:, :], 0.0).then_inc(made, 1)
        pool.memset(half[:, :], -0.5).then_inc(made, 1)
        pool.memset(ones[:, :], 1.0).then_inc(made, 1)
        pool.wait_ge(made, 3)
        pool.affine_select(out=c.ident[:, :], in_=c.ident[:, :], compare_op=ALU.not_equal, fill=1.0, base=0,
                           pattern=[[-1, P]], channel_multiplier=1).then_inc(made, 1)
        for p, n in enumerate(rows):
            pool.wait_ge(squared, p + 1)
            pool.tensor_scalar(ms[0:n, p:p + 1], ss[0:n, p:p + 1], 1.0 / D, EPS,
                               ALU.mult, ALU.add).then_inc(mean_ok, 1)
            pool.wait_ge(mean_ok, p + 1)
            pool.tensor_tensor(rs[0:n, p:p + 1], ms[0:n, p:p + 1], half[0:n, p:p + 1],
                               ALU.pow).then_inc(rstd_ok, 1)
            if p == 5:
                w.split_lo(pool, 0, 0)
        w.split_lo(pool, 0, 1)
        for n, m in enumerate((c.identb, c.mask, c.mask_s)):
            pool.memset(m[:, :], 0.0).then_inc(made, 1)
            pool.wait_ge(made, 4 + 2 * n + 1)
            if n == 0:
                pool.affine_select(out=m[:, :], in_=m[:, :], compare_op=ALU.not_equal, fill=1.0, base=0,
                                   pattern=[[-1, P]], channel_multiplier=1).then_inc(made, 1)
            else:
                pool.affine_select(out=m[:, :], in_=m[:, :], compare_op=ALU.is_gt, fill=HIDDEN, base=0,
                                   pattern=[[-1, P]], channel_multiplier=1).then_inc(made, 1)
        pool.wait_ge(made, 10)
        pool.affine_select(out=c.mask_s[:, :].rearrange("p (b j) -> p b j", j=DS),
                           in_=c.mask_s[:, :].rearrange("p (b j) -> p b j", j=DS),
                           compare_op=ALU.is_gt, fill=HIDDEN, base=DS,
                           pattern=[[DS, NB], [0, DS]], channel_multiplier=-1).then_inc(made, 1)
        w.split_lo(pool, 0, 2)
        w.split_lo(pool, 0, 3)
        with pool.Fori(1, KC) as i:
            for j in range(4):
                w.split_lo(pool, i, j)
        with pool.Fori(0, KC // 2) as i:
            for j in range(6):
                wg.split_lo(pool, i, j)

    def tensor(pe):
        def turn(p):
            n = rows[p]
            pe.wait_ge(normed, p + 1)
            for j in range(2):
                if p >= 2:
                    pe.wait_ge(lo_ok, 2 * (p - 2) + j + 1)
                for k in range(4):
                    mm = pe.transpose(x_banks[p % 2][j][:, k * P:k * P + n],
                                      xn[0:n, p % 3, (4 * j + k) * P:(4 * j + k + 1) * P], c.ident[0:n, 0:n])
                mm.then_inc(turned, 1)

        def conv_chunk(i, j, n, ks=range(KC)):
            c0, c1 = (CH if names[j] in "Ch" else CHL)[n]
            q = 3 * j + n
            if q < 2:
                pe.wait_ge(d_out, 9 * i + q + 1)
            elif q < 5:
                pe.wait_ge(c_out, 3 * i + q - 1)
            else:
                pe.wait_ge(d_out, 9 * i + q - 4 + 2)
            mm = w.product(pe, j, banks[q % 2][:, 0:c1 - c0], x_moving(c, c0, c1), ks)
            if KC - 1 in ks:
                mm.then_inc(full, 1)

        pe.wait_ge(made, 4)
        pe.wait_ge(gain_in, 16)
        for j in range(2):
            mm = pe.matmul(c.bank_z[:, j * 512:(j + 1) * 512], ones[:, :], gb[:, j * 512:(j + 1) * 512],
                           start=True, stop=True)
        mm.then_inc(gain_ok, 1)
        for p in range(TILES):
            turn(p)
            if p == 4:
                pe.wait_ge(small_in, 48)
                pe.transpose(small_bank[:, 0:80], b80[:, :], c.ident[0:80, 0:80])
                for k in range(KC):
                    pe.transpose(small_bank[:, 80 + 3 * k:83 + 3 * k], cw3[:, k * P:(k + 1) * P], c.ident[0:3, 0:3])
                for k in range(KC):
                    mm = pe.transpose(small_bank[:, 128 + 16 * k:144 + 16 * k], st16[:, k * P:(k + 1) * P],
                                      c.ident[0:16, 0:16])
                mm.then_inc(small_turned, 1)
            if p in C_HALVES:
                n, ks = C_HALVES[p]
                if n == 0:
                    w.ready(pe, 0, 0)
                pe.wait_ge(lo_ok, 2 * CHUNK_TILES[n])
                conv_chunk(0, 0, n, ks)
        pe.wait_ge(lo_ok, 2 * CHUNK_TILES[2])
        conv_chunk(0, 0, 2)
        for j in range(1, 4):
            w.ready(pe, 0, j)
            for n in range(3):
                conv_chunk(0, j, n)
        with pe.Fori(1, KC) as i:
            for j in range(4):
                w.ready(pe, i, j)
                for n in range(3):
                    conv_chunk(i, j, n)
        pe.wait_ge(last_ok, 2 * KC)
        for k in range(KC):
            mm = pe.transpose(c.bank_z[0:18, k * P:(k + 1) * P], last[:, k, :], c.ident[:, :])
        mm.then_inc(last_turned, 1)

        def two_blocks(i, first):
            for j in range(6):
                b = 2 * i + j // 3
                wg.ready(pe, i, j)
                for n, (c0, c1) in enumerate(CHL):
                    if j % 3 == 0:
                        if first and j == 0:
                            pe.wait_ge(d_out, 9 * KC + min(n, 1) - 1 + 2)
                        pe.wait_ge(s_ok, 3 * b + n + 1)
                    elif j % 3 == 1:
                        if first and j == 1 and n == 0:
                            pe.wait_ge(yl_ok, 3 * KC)
                        pe.wait_ge(g_ok, 3 * b + n + 1)
                    else:
                        pe.wait_ge(m_ok, 3 * b + n + 1)
                    right = x_moving(c, c0, c1) if j % 3 != 1 else (
                        lambda k: yh[:, k, c0 - META:c1 - META], lambda k: yl[:, k, c0 - META:c1 - META])
                    wg.product(pe, j, g_banks[n][:, 0:c1 - c0], right).then_inc(g_full, 1)

        two_blocks(0, True)
        with pe.Fori(1, KC // 2) as i:
            two_blocks(i, False)

    def scalar(act, first_splits):
        def square(p):
            n = rows[p]
            act.wait_ge(x_in[p % 4], 16 * (p // 4 + 1))
            if p:
                act.wait_ge(squared, p)
            act.activation(junk[0:n, :], xr[0:n, p % 4, :], ACT.Square,
                           accum_out=ss[0:n, p:p + 1]).then_inc(squared, 1)

        def hi(p):
            n, (c0, c1) = rows[p], tile_cols(NORM_ORDER[p])
            for j in range(2):
                act.wait_ge(turned, 2 * p + j + 1)
                act.activation(c.xh[:, 4 * j:4 * j + 4, c0:c1],
                               x_banks[p % 2][j][:, :].rearrange("p (k n) -> p k n", k=4)[:, :, 0:n],
                               ACT.Copy).then_inc(hi_ok, 1)

        square(0)
        square(1)
        for p in range(TILES):
            if p + 2 < TILES:
                square(p + 2)
            hi(p)
            if p == 2:
                w.split_hi(act, 0, 0)
            if p == 5:
                w.split_hi(act, 0, 1)

        def one_conv(i, more):
            def rest_of_y(n):
                c0, c1 = CHL[n]
                hold(act, y_ok, 3 * i + n + 1)
                act.activation(row(yh, i, c0 - META, c1 - META),
                               yt[:, c0 - META:c1 - META], ACT.Copy).then_inc(yh_ok, 1)

            for n, (c0, c1) in enumerate(CH):
                hold(act, full, 12 * i + n + 1)
                act.activation(cs[:, c0:c1], banks[n % 2][:, 0:c1 - c0], ACT.Identity,
                               bias=bias("C", i)).then_inc(c_out, 1)
            w.split_hi(act, i, 2)
            act.wait_ge(full, 12 * i + 6)
            w.split_hi(act, i, 3)
            for n, (c0, c1) in enumerate(CHL):
                q = 9 + n
                hold(act, full, 12 * i + q + 1)
                act.activation(sg[:, c0 - META:c1 - META], banks[q % 2][:, 0:c1 - c0], ACT.Sigmoid,
                               bias=bias("z_c", i)).then_inc(sig_ok, 1)
                if n == 0:
                    if more:
                        w.split_hi(act, i + 1, 0)
                    else:
                        wg.split_hi(act, 0, 0)
                if n:
                    rest_of_y(n - 1)
            if more:
                w.split_hi(act, i + 1, 1)
            else:
                wg.split_hi(act, 0, 1)
            rest_of_y(2)

        act.wait_ge(small_out, 3)
        with act.Fori(0, KC - 1) as i:
            one_conv(i, True)
        one_conv(KC - 1, False)

        def two_blocks(i, more):
            for b in range(2):
                m = 2 * i + b

                def split(j):
                    if b == 0 or more or j < 3:
                        jj = 3 * b + j
                        wg.split_hi(act, *((i, jj) if jj < 6 else (i + 1, jj - 6)))

                for n, (c0, c1) in enumerate(CHL):
                    hold(act, g_full, 9 * m + n + 1)
                    act.activation(gate[:, c0 - META:c1 - META], g_banks[n][:, 0:c1 - c0], ACT.Sigmoid,
                                   bias=bias("g_c", m)).then_inc(g_ok, 1)
                split(2)
                act.wait_ge(g_full, 9 * m + 6)
                split(3)
                if b and not more:
                    first_splits(act)
                act.wait_ge(s_stored, 16 * m + 16)
                for n, (c0, c1) in enumerate(CHL):
                    hold(act, g_full, 9 * m + 6 + n + 1)
                    act.activation(outs[:, 1, c0 - META:c1 - META], g_banks[n][:, 0:c1 - c0], ACT.Sigmoid,
                                   bias=bias("g_s", m)).then_inc(s_ok, 1)
                split(4)

        act.sem_inc(s_ok, 3)
        act.wait_ge(yl_ok, 3 * KC)
        with act.Fori(0, KC // 2 - 1) as i:
            two_blocks(i, True)
        two_blocks(KC // 2 - 1, False)

    def vector(dve):
        def normalise(p):
            n = rows[p]
            dve.wait_ge(rstd_ok, p + 1)
            if p >= 3:
                dve.wait_ge(turned, 2 * (p - 2))
            dve.scalar_tensor_tensor(out=xn[0:n, p % 3, :], in0=xr[0:n, p % 4, :],
                                     scalar=rs[0:n, p:p + 1], in1=c.bank_z[0:n, 0:D],
                                     op0=ALU.mult, op1=ALU.mult).then_inc(normed, 1)

        def lo(p):
            n, (c0, c1) = rows[p], tile_cols(NORM_ORDER[p])
            for j in range(2):
                dve.wait_ge(hi_ok, 2 * p + j + 1)
                dve.tensor_tensor(c.xl[:, 4 * j:4 * j + 4, c0:c1],
                                  x_banks[p % 2][j][:, :].rearrange("p (k n) -> p k n", k=4)[:, :, 0:n],
                                  c.xh[:, 4 * j:4 * j + 4, c0:c1].bitcast(F32), ALU.subtract).then_inc(lo_ok, 1)

        dve.sem_inc(d_out, 2)
        dve.wait_ge(gain_ok, 1)
        normalise(0)
        normalise(1)
        for p in range(TILES):
            if p + 2 < TILES:
                normalise(p + 2)
            lo(p)
            if p == 5:
                dve.wait_ge(small_turned, 1)
                dve.tensor_copy(c.bias[:, :], small_bank[:, 0:80]).then_inc(small_out, 1)
                dve.tensor_copy(conv_w[:, :, :], small_bank[:, 80:104].rearrange("p (k j) -> p k j", j=3)).then_inc(small_out, 1)
                dve.tensor_copy(state[:, :, :], small_bank[:, 128:256].rearrange("p (k j) -> p k j", j=16)).then_inc(small_out, 1)
        dve.wait_ge(small_out, 3)

        def sample(t):
            return t[:, SEQ:LIVE].rearrange("p (b j) -> p b j", j=DS)

        with dve.Fori(0, KC) as i:
            dve.tensor_copy(us[:, :, 0:2], state[:, bass.ds(i, 1), :].rearrange("p o (b j) -> p (o b) j", j=2)
                            ).then_inc(u_ok, 1)
            for n, (c0, c1) in enumerate(CH):
                q = 3 + n
                dve.wait_ge(full, 12 * i + q + 1)
                dve.wait_ge(c_out, 3 * i + n + 1)
                e = min(c1, SAMPLE0)
                mm = dve.scalar_tensor_tensor(out=up[:, c0:e], in0=banks[q % 2][:, 0:e - c0], scalar=bias("h", i),
                                              in1=cs[:, c0:e], op0=ALU.add, op1=ALU.mult)
                if n < 2:
                    mm.then_inc(d_out, 1)
            mm.then_inc(u_ok, 1)
            dve.scalar_tensor_tensor(out=us[:, :, 2:DS + 2],
                                     in0=banks[1][:, 256:384].rearrange("p (b j) -> p b j", j=DS),
                                     scalar=bias("h", i),
                                     in1=cs[:, SAMPLE0:TOK].rearrange("p (b j) -> p b j", j=DS),
                                     op0=ALU.add, op1=ALU.mult).then_inc(d_out, 1)
            dve.wait_ge(u_ok, 2 * i + 2)
            dve.wait_ge(d_out, 9 * i + 3 + 2)
            for r in range(3):
                wr = conv_w[:, bass.ds(i, 1), r:r + 1].rearrange("p a b -> p (a b)")
                pairs = [(tap[:, 0:SEQ], up[:, META - 2 + r:SAMPLE0 - 2 + r]),
                         (sample(tap), us[:, :, r:r + DS])]
                if r:
                    dve.wait_ge(tap_ok, 6 * i + 2 * r)
                for dst, src in pairs:
                    if r == 0:
                        dve.tensor_scalar(dst, src, wr, None, ALU.mult).then_inc(tap_ok, 1)
                    else:
                        dve.scalar_tensor_tensor(out=dst, in0=src, scalar=wr, in1=dst,
                                                 op0=ALU.mult, op1=ALU.add).then_inc(tap_ok, 1)
            dve.tensor_copy(last[:, bass.ds(i, 1), 0:2].rearrange("p o j -> p (o j)"),
                            up[:, SAMPLE0 - 2:SAMPLE0]).then_inc(last_ok, 1)
            dve.tensor_copy(last[:, bass.ds(i, 1), 2:18].rearrange("p o (b j) -> p (o b) j", j=2),
                            us[:, :, DS:DS + 2]).then_inc(last_ok, 1)
            dve.wait_ge(tap_ok, 6 * i + 6)
            for n, (c0, c1) in enumerate(CHL):
                q = 6 + n
                t = tap[:, c0 - META:c1 - META]
                dve.wait_ge(full, 12 * i + q + 1)
                dve.scalar_tensor_tensor(out=t, in0=banks[q % 2][:, 0:c1 - c0], scalar=bias("B", i), in1=t,
                                         op0=ALU.add, op1=ALU.mult).then_inc(d_out, 1)
            for n, (c0, c1) in enumerate(CHL):
                q = 9 + n
                a, b = c0 - META, c1 - META
                dve.wait_ge(sig_ok, 3 * i + n + 1)
                dve.scalar_tensor_tensor(out=sg[:, a:b], in0=banks[q % 2][:, 0:c1 - c0], scalar=bias("z_c", i),
                                         in1=sg[:, a:b], op0=ALU.add, op1=ALU.mult).then_inc(d_out, 1)
                dve.wait_ge(d_out, 9 * i + 7 + n + 2)
                dve.tensor_tensor(yt[:, a:b], sg[:, a:b], tap[:, a:b], ALU.mult).then_inc(y_ok, 1)
                dve.wait_ge(yh_ok, 3 * i + n + 1)
                dve.tensor_tensor(row(yl, i, a, b), yt[:, a:b],
                                  row(yh, i, a, b).bitcast(F32), ALU.subtract).then_inc(yl_ok, 1)
        dve.wait_ge(last_turned, 1)
        dve.tensor_copy(last_rows[:, 0:512], c.bank_z[0:18, 0:512]).then_inc(last_out, 1)
        dve.tensor_copy(last_rows[:, 512:1024], c.bank_z[0:18, 512:1024]).then_inc(last_out, 1)

        with dve.Fori(0, KC) as i:
            dve.wait_ge(m_stored, 16 * i + 16)
            for n, (c0, c1) in enumerate(CHL):
                dve.wait_ge(g_full, 9 * i + 3 + n + 1)
                dve.wait_ge(g_ok, 3 * i + n + 1)
                dve.tensor_tensor(outs[:, 0, c0 - META:c1 - META], g_banks[n][:, 0:c1 - c0],
                                  gate[:, c0 - META:c1 - META], ALU.mult).then_inc(m_ok, 1)

    def y_c_used(eng):
        eng.wait_ge(g_full, 9 * (KC - 1) + 6)

    def bank_read(eng, n):
        eng.wait_ge(s_ok, 3 * (KC - 1) + n + 1 + 3)

    def all_stored(eng):
        eng.wait_ge(stored, 32)
        eng.wait_ge(m_stored, 16 * (KC + 1))
        eng.wait_ge(s_stored, 16 * (KC + 1))

    done = Group()
    done.y_c_used, done.bank_read, done.stored = y_c_used, bank_read, all_stored
    return Programs(sync, gpsimd, tensor, scalar, vector), done


ORDER = [7, 6, 5, 4, "samples", 3, 2, 1, 0]
UNITS = len(ORDER)
SAMPLE_UNIT = ORDER.index("samples")
PROMPT_UNITS = UNITS - 1
FIRST_P, NPROJ = TILES + 1, TILES + 3
FIRST_T, NT, NGROUPS = TILES, 44, 14


def width(u):
    return PAST + P if u == SAMPLE_UNIT else META + P * (ORDER[u] + 1)


def meta_apart(u):
    return u != SAMPLE_UNIT and (P * (ORDER[u] + 1)) % 512 == 0


def value_groups(u):
    if u == SAMPLE_UNIT:
        return [["new"], [0, 1, 2, 3]]
    items = ["meta"] + list(range(ORDER[u] + 1))
    return [items[i:i + 4] for i in range(0, len(items), 4)]


def prompt_units_before(u):
    return u - (u > SAMPLE_UNIT)


def groups_before(u):
    return sum(len(value_groups(v)) for v in range(u) if v != SAMPLE_UNIT)


def slot_steps(slot, nxt):
    before, after = [], []
    if slot < UNITS and meta_apart(slot):
        before.append(("m", slot))
    if slot == 0:
        before += [("k", 0), ("k", 1)]
    elif slot < UNITS + 1:
        groups = [("a", slot - 1, g) for g in range(len(value_groups(slot - 1)))]
        before += groups[:2]
        if slot <= 3:
            after += [("k", 2 * slot)] + groups[2:] + [("k", 2 * slot + 1)]
        if slot > SAMPLE_UNIT and slot < UNITS:
            after += [("v", 2 * (slot - SAMPLE_UNIT - 1)), ("v", 2 * (slot - SAMPLE_UNIT - 1) + 1)]
        if slot >= 2 and nxt:
            after.append(("x", slot - 2))
        if slot == UNITS and nxt:
            after += [("x", TILES - 2), ("x", TILES - 1)]
    return before, after


LATE_Z = 3
Y_AGAIN = {3: [0], 4: [1, 2], 5: [3], 6: [4], 7: [5, 6]}


def turn_plan(nxt):
    order = [step for slot in range(UNITS + 1) for part in slot_steps(slot, nxt) for step in part]
    assert not nxt or len(order) == NT
    return {key: n for n, key in enumerate(order)}


def attention(c, d, buf, front_stored, following):
    w_cols = d["w_in"][0].rearrange("(k p) (n e) -> p k n e", p=P, e=P)
    b_cols = d["b_in"].rearrange("o (n e) -> o n e", e=P)
    cache_k = d["cache_k"][0].rearrange("b (n p) h d -> b p n h d", p=P)
    cache_v = d["cache_v"][0].rearrange("b (n p) h d -> b p n h d", p=P)
    plans = {True: turn_plan(True), False: turn_plan(False)}
    wz, w3, w3h, w3l, bias3, gain, qk, v = buf.wz, buf.w3, buf.w3h, buf.w3l, buf.bias3, buf.gain, buf.qk, buf.v
    qkn, junk, ss, ms, rs, half = buf.qkn, buf.junk, buf.ss, buf.ms, buf.rs, buf.half
    beta, keep, at, ats, kc, vc, kt = buf.beta, buf.keep, buf.at, buf.ats, buf.kc, buf.vc, buf.kt
    qbd, ot, zs = buf.qbd, buf.ot, buf.zs
    y_again = w3[:, :, :].rearrange("p k e -> p (k e)")

    gain_in, half_ok = c.sem("gain_in"), c.sem("half_ok")
    w3_in, w3_hi, w3_lo = c.sem("wqkv_in"), c.sem("wqkv_hi_ok"), c.sem("wqkv_lo_ok")
    b3_in = [c.sem(f"bias_qkv_in{q}") for q in range(2)]
    proj_ok, proj_out = c.sem("proj_bank_full"), c.sem("proj_bank_out")
    t_full, t_out = c.sem("turn_bank_full"), c.sem("turn_bank_out")
    rows_ok, sq_ok, mean_ok, rstd_ok = c.sem("qk_rows_ok"), c.sem("qk_sq"), c.sem("qk_mean"), c.sem("qk_rstd_ok")
    norm_ok = c.sem("qk_norm_ok")
    k_stored = [c.sem(f"k_stored{s}") for s in range(2)]
    v_stored = [c.sem(f"v_stored{q}") for q in range(2)]
    score_ok, kq_ok = c.sem("scores_ok"), c.sem("cache_scores_ok")
    keep_ok, beta_ok = c.sem("keep_ok"), c.sem("beta_ok")
    scan_ok, a_ok = c.sem("scan_ok"), c.sem("a_ok")
    pv_ok, o_out = c.sem("value_group_ok"), c.sem("o_out")
    k_in = [c.sem(f"cache_k_in{s}") for s in range(2)]
    v_in = [c.sem(f"cache_v_in{s}") for s in range(2)]
    qbd_ok = c.sem("q_block_ok")
    zsig_ok = c.sem("z_sig_ok")
    y_ok, y_stored = c.sem("y_s_ok"), c.sem("y_s_stored")
    y_in = [c.sem(f"y_s_in{s}") for s in range(2)]
    yh_ok, yl_ok = c.sem("y_s_hi_ok"), c.sem("y_s_lo_ok")
    y_last_ok = c.sem("last_y_s_lo_ok")

    def rows_of(t):
        return META if t == META_TILE else P

    def turn_bank(h, plan, key):
        n = plan[key]
        return FIRST_T + NT * h + n, c.bank_t[n % 2]

    def proj_bank(h, par, n):
        return FIRST_P + NPROJ * h + n, c.bank_p[(FIRST_P + par + n) % 2]

    def z_bank(h, par, n):
        if n:
            return proj_bank(h, par, n - 1)
        return FIRST_P + NPROJ * h - 1, c.bank_p[(FIRST_P + par - 1) % 2]

    def head_block(name, h):
        return bass.ds(h + OFF[name] // P, 1)

    def all_heads(eng, head):
        with eng.Fori(0, HEADS // 2 - 1) as i:
            head(2 * i, 0, i, True, True)
            head(2 * i + 1, 1, i, True, True)
        head(HEADS - 2, 0, HEADS // 2 - 1, True, False)
        head(HEADS - 1, 1, HEADS // 2 - 1, False, False)

    def load_qkv(sp, h):
        for j, name in enumerate("qkv"):
            sp.dma_start(w3[:, :, j * P:(j + 1) * P], w_cols[:, :, head_block(name, h), :]).then_inc(w3_in, 16)

    def load_bias(sp, h, q):
        for j, name in enumerate("qkv"):
            sp.dma_start(bias3[:, q, j * P:(j + 1) * P],
                         b_cols[:, head_block(name, h), :].rearrange("o n e -> o (n e)").to_broadcast([P, P])
                         ).then_inc(b3_in[q], 16)

    def load_z(sp, h):
        sp.dma_start(wz.raw[:, 0, :, :], w_cols[:, :, head_block("z_s", h), :]).then_inc(wz.raw_in[0], 16)

    def first_loads(sp):
        load_bias(sp, 0, 0)
        sp.dma_start(gain[:, 0, :], d["q_norm_g"].to_broadcast([P, P])).then_inc(gain_in, 16)
        sp.dma_start(gain[:, 1, :], d["k_norm_g"].to_broadcast([P, P])).then_inc(gain_in, 16)
        load_z(sp, 0)

    def split_qkv_hi(act, h):
        act.wait_ge(w3_in, 48 * (h + 1))
        for j in range(4):
            k = slice(2 * j, 2 * j + 2)
            act.activation(w3h[:, k, :], w3[:, k, :], ACT.Copy).then_inc(w3_hi, 1)

    def first_splits(act):
        split_qkv_hi(act, 0)

    def sync(sp):
        def load_k(h, b):
            sp.dma_start(kc[:, b % 2, :, :], cache_k[b][:, :, bass.ds(h, 1), :].rearrange("p n o d -> p n (o d)")
                         ).then_inc(k_in[b % 2], 16)

        def load_v(h, b):
            sp.dma_start(vc[:, b % 2, :, :], cache_v[b][:, :, bass.ds(h, 1), :].rearrange("p n o d -> p n (o d)")
                         ).then_inc(v_in[b % 2], 16)

        def store(h, q, t):
            n = rows_of(t)
            sp.wait_ge(norm_ok, TILES * h + t + 1)
            if t == SAMPLE_TILE:
                dk, dv = (d[x][0].rearrange("b s h d -> (b s) h d") for x in ("k_sample", "v_sample"))
            else:
                c0, c1 = tile_cols(t)
                dk, dv = (d[x][0, 0, c0:c1] for x in ("k_prompt", "v_prompt"))
            sp.dma_start(dk[:, bass.ds(h, 1), :].rearrange("t o d -> t (o d)"),
                         qkn[0:n, t % 2, P:2 * P]).then_inc(k_stored[t % 2], 16)
            sp.dma_start(dv[:, bass.ds(h, 1), :].rearrange("t o d -> t (o d)"),
                         v[0:n, q, t, :]).then_inc(v_stored[q], 16)

        def head(h, par, pairs, nxt, nxt2):
            plan = plans[nxt]

            def next_cache(kind, load, b):
                if b + 2 < NB or nxt:
                    hold(sp, t_full, turn_bank(h, plan, (kind, b))[0] + 1)
                    load(h if b + 2 < NB else h + 1, (b + 2) % NB)

            for slot in range(UNITS):
                if slot <= 3:
                    next_cache("k", load_k, 2 * slot)
                    next_cache("k", load_k, 2 * slot + 1)
                if slot == 0 and nxt2:
                    sp.wait_ge(w3_lo, 4 * h + 8)
                    load_qkv(sp, h + 2)
                    load_bias(sp, h + 2, par)
                if slot == 1 and nxt2:
                    sp.wait_ge(wz.lo_ok, h + 2 + 1)
                    load_z(sp, h + 2)
                for k in [] if nxt else Y_AGAIN.get(slot, []):
                    if k == 0:
                        sp.wait_ge(w3_lo, 4 * HEADS)
                        sp.wait_ge(y_stored, 16 * HEADS)
                    if k >= 2:
                        sp.wait_ge(yl_ok, k - 1)
                    sp.dma_start(y_again[:, (k % 2) * LIVE:(k % 2 + 1) * LIVE], d["ys"][k]).then_inc(y_in[k % 2], 16)
                if slot == UNITS - 4 and not nxt:
                    sp.wait_ge(proj_ok, FIRST_P + NPROJ * (HEADS - 1))
                    following.first_loads(sp)
                if slot > SAMPLE_UNIT:
                    for b in range(2):
                        next_cache("v", load_v, 2 * (slot - SAMPLE_UNIT - 1) + b)
                if slot and nxt:
                    store(h + 1, 1 - par, slot - 1)
            if nxt:
                store(h + 1, 1 - par, TILES - 2)
                sp.wait_ge(y_ok, h + 1)
                sp.dma_start(d["ys"][bass.ds(h, 1)].rearrange("o p n -> (o p) n"), ot[:, :]).then_inc(y_stored, 16)
                store(h + 1, 1 - par, TILES - 1)

        for s in range(2):
            sp.sem_inc(k_stored[s], 16)
            sp.sem_inc(v_stored[s], 16)
        sp.sem_inc(y_stored, 16)
        for b in range(2):
            load_k(0, b)
            load_v(0, b)
        sp.wait_ge(w3_lo, 4)
        load_qkv(sp, 1)
        load_bias(sp, 1, 1)
        sp.wait_ge(wz.lo_ok, 1 + 1)
        load_z(sp, 1)
        for t in range(TILES):
            store(0, 0, t)
        all_heads(sp, head)
        for s in range(2):
            sp.wait_ge(k_stored[s], 16 * (HEADS * TILES // 2 + 1))
            sp.wait_ge(v_stored[s], 16 * (HEADS * TILES // 2 + 1))

    def gpsimd(pool):
        def rstd(h, t):
            n, s = rows_of(t), t % 2
            a = 1 if t == META_TILE else 0
            hold(pool, sq_ok, TILES * h + t + 1)
            pool.tensor_scalar(ms[0:n, s, a:2], ss[0:n, s, a:2], 1.0 / HD, EPS, ALU.mult, ALU.add).then_inc(mean_ok, 1)
            pool.wait_ge(mean_ok, TILES * h + t + 1)
            pool.tensor_tensor(rs[0:n, s, a:2], ms[0:n, s, a:2], half[0:n, a:2], ALU.pow).then_inc(rstd_ok, 1)

        def split_qkv_lo(h):
            for j in range(4):
                k = slice(2 * j, 2 * j + 2)
                pool.wait_ge(w3_hi, 4 * h + j + 1)
                pool.tensor_tensor(w3l[:, k, :], w3[:, k, :], w3h[:, k, :].bitcast(F32),
                                   ALU.subtract).then_inc(w3_lo, 1)

        def head(h, par, pairs, nxt, nxt2):
            pool.wait_ge(t_out, FIRST_T + NT * h + 1)
            hold(pool, kq_ok, NB * h + 2)
            pool.tensor_copy(qbd[:, :].rearrange("p (b w) -> p b w", w=P + DS)[:, :, 0:DS],
                             qk[:, par, 0, SAMPLE0:TOK].rearrange("p (b j) -> p b j", j=DS)).then_inc(qbd_ok, 1)
            if nxt:
                split_qkv_lo(h + 1)
                rstd(h + 1, 0)
                wz.split_lo(pool, h + 1, 0)
                for t in range(1, TILES):
                    rstd(h + 1, t)
            else:
                following.weights.start_pool(pool)
                for k in range(HEADS - 1):
                    pool.wait_ge(yh_ok, k + 1)
                    pool.tensor_tensor(c.xl[:, k, 0:LIVE], y_again[:, (k % 2) * LIVE:(k % 2 + 1) * LIVE],
                                       c.xh[:, k, 0:LIVE].bitcast(F32), ALU.subtract).then_inc(yl_ok, 1)
                    if k == HEADS - 4:
                        following.weights.split_lo(pool, 0, 0)
                        following.weights.split_lo(pool, 0, 1)

        wz.start_pool(pool)
        front_stored.y_c_used(pool)
        pool.memset(half[:, :], -0.5).then_inc(half_ok, 1)
        pool.memset(qbd[:, :], 0.0).then_inc(half_ok, 1)
        pool.wait_ge(half_ok, 2)
        split_qkv_lo(0)
        wz.split_lo(pool, 0, 0)
        for t in range(TILES):
            rstd(0, t)
        all_heads(pool, head)

    def tensor(pe):
        def project(h, t, number, between=None):
            n, (c0, c1) = rows_of(t), tile_cols(t)
            a = P if t == META_TILE else 0
            num, bank = number
            pe.wait_ge(proj_out, num + 1)
            for j in range(4):
                if j == 2 and between:
                    between()
                if t == 0:
                    pe.wait_ge(w3_lo, 4 * h + j + 1)
                mm = split_product(pe, bank[0:n, a:3 * P], (lambda k: c.xh[:, k, c0:c1], lambda k: c.xl[:, k, c0:c1]),
                                   (lambda k: w3h[:, k, a:3 * P], lambda k: w3l[:, k, a:3 * P]), (2 * j, 2 * j + 1))
            mm.then_inc(proj_ok, 1)

        def turn_rows(h, t, number):
            n = rows_of(t)
            num, bank = number
            pe.wait_ge(norm_ok, TILES * h + t + 1)
            if t == META_TILE:
                hold(pe, t_out, num + 1)
            else:
                pe.wait_ge(t_out, num + 1)
                pe.transpose(bank[:, 0:P], qkn[0:n, t % 2, 0:P], c.ident[0:n, 0:n])
            pe.transpose(bank[:, P:P + n], qkn[0:n, t % 2, P:2 * P], c.ident[0:n, 0:n]).then_inc(t_full, 1)

        def silu_gate(h, n, number, between=None):
            c0, c1 = CHL[n]
            num, bank = number
            if n == 0:
                wz.ready(pe, h, 0)
            pe.wait_ge(proj_out, num + 1)
            wz.product(pe, 0, bank[:, 0:c1 - c0], x_moving(c, c0, c1), range(KC - 2))
            if between:
                between()
            wz.product(pe, 0, bank[:, 0:c1 - c0], x_moving(c, c0, c1), range(KC - 2, KC)).then_inc(proj_ok, 1)

        def scores(h, par, u, plan):
            pe.wait_ge(beta_ok, UNITS * h + u + 1)
            if u == SAMPLE_UNIT:
                pe.matmul(c.bank_z[:, 0:P], qk[:, par, 0, SAMPLE0:TOK], qk[:, par, 1, SAMPLE0:TOK],
                          start=True, stop=False)
                pe.matmul(c.bank_z[:, 0:P], c.identb[:, :], c.mask_s[:, :], start=False, stop=True).then_inc(score_ok, 1)
                return
            b = ORDER[u]
            q = qk[:, par, 0, META + b * P:META + (b + 1) * P]
            skip = META if meta_apart(u) else 0
            w = META + P * (b + 1) - skip
            for a in range(0, w, 512):
                e = min(a + 512, w)
                pe.matmul(c.bank_z[:, a:e], q, qk[:, par, 1, skip + a:skip + e], start=True, stop=e < w)
            pe.matmul(c.bank_z[:, w - P:w], c.identb[:, :], c.mask[:, :], start=False, stop=True).then_inc(score_ok, 1)
            if not skip:
                return
            num, bank = turn_bank(h, plan, ("m", u))
            pe.wait_ge(t_out, num + 1)
            pe.matmul(bank[:, 0:META], q, qk[:, par, 1, 0:META], start=True, stop=True).then_inc(t_full, 1)

        def turn_cache(h, plan, b):
            num, bank = turn_bank(h, plan, ("k", b))
            pe.wait_ge(k_in[b % 2], 16 * (NB // 2 * h + b // 2 + 1))
            pe.wait_ge(t_out, num + 1)
            for n in range(PAST // P):
                mm = pe.transpose(bank[:, n * P:(n + 1) * P], kc[:, b % 2, n, :], c.ident[:, :])
            mm.then_inc(t_full, 1)

        def cache_scores(h, plan, b):
            if b == 0:
                pe.wait_ge(qbd_ok, h + 1)
            pe.wait_ge(t_out, turn_bank(h, plan, ("k", b))[0] + 1 + 2)
            pe.matmul(c.bank_s[:, 0:PAST], qbd[:, b * P:(b + 1) * P], kt[:, b % 2, :],
                      start=b == 0, stop=b == NB - 1).then_inc(kq_ok, 1)

        def turn_a(h, par, plan, u, g):
            slot = (par + u) % 2
            num, bank = turn_bank(h, plan, ("a", u, g))
            if g == 0:
                pe.wait_ge(a_ok, UNITS * h + u + 1)
            pe.wait_ge(t_out, num + 1)
            for m, item in enumerate(value_groups(u)[g]):
                if item == "meta":
                    src, n = beta[:, slot, 0:META], META
                elif item == "new":
                    src, n = beta[:, slot, PAST:PAST + P], P
                else:
                    a = item * P + (0 if u == SAMPLE_UNIT else META)
                    src, n = beta[:, slot, a:a + P], P
                mm = pe.transpose(bank[0:n, m * P:(m + 1) * P], src, c.ident[:, :])
            mm.then_inc(t_full, 1)

        def weigh(h, par, plan, u, g):
            groups, gg = value_groups(u), groups_before(u) + g
            pe.wait_ge(t_out, turn_bank(h, plan, ("a", u, g))[0] + 1 + 2)
            if g == 0:
                pe.wait_ge(o_out, PROMPT_UNITS * h + prompt_units_before(u) + 1)
            for m, item in enumerate(groups[g]):
                t = META_TILE if item == "meta" else item
                n = rows_of(t)
                mm = pe.matmul(c.bank_o[:, 0:P], v[0:n, par, t, :], at[0:n, gg % 2, m * P:(m + 1) * P],
                               start=g == 0 and m == 0, stop=g == len(groups) - 1 and m == len(groups[g]) - 1)
            mm.then_inc(pv_ok, 1)

        def cache_values(h, par, plan, b):
            num, bank = turn_bank(h, plan, ("v", b))
            pe.wait_ge(t_out, num + 1)
            pe.wait_ge(t_out, turn_bank(h, plan, ("a", SAMPLE_UNIT, 1))[0] + 1 + 2)
            pe.wait_ge(v_in[b % 2], 16 * (NB // 2 * h + b // 2 + 1))
            pe.matmul(bank[:, 0:DS], v[:, par, SAMPLE_TILE, :], ats[:, PAST + b * DS:PAST + (b + 1) * DS],
                      start=True, stop=False)
            for n in range(PAST // P):
                mm = pe.matmul(bank[:, 0:DS], vc[:, b % 2, n, :], ats[:, n * P + b * DS:n * P + (b + 1) * DS],
                               start=False, stop=n == PAST // P - 1)
            mm.then_inc(t_full, 1)

        def head(h, par, pairs, nxt, nxt2):
            plan = plans[nxt]
            pe.wait_ge(t_out, FIRST_T + NT * h + 2)
            scores(h, par, 0, plan)
            turn_cache(h, plan, 0)
            turn_cache(h, plan, 1)
            silu_gate(h, 1, z_bank(h, par, 1))
            cache_scores(h, plan, 0)
            cache_scores(h, plan, 1)
            if nxt:
                silu_gate(h, 2, z_bank(h, par, 2))
            for slot in range(1, UNITS + 1):
                u = slot - 1
                if slot < UNITS:
                    scores(h, par, slot, plan)
                groups = len(value_groups(u))
                for g in range(min(groups, 2)):
                    turn_a(h, par, plan, u, g)
                if nxt:
                    project(h + 1, u, proj_bank(h, par, 2 + u))
                elif slot == LATE_Z:
                    silu_gate(h, 2, z_bank(h, par, 2))
                weighed = 0
                for step in slot_steps(slot, nxt)[1]:
                    if slot == UNITS and step[0] == "x" and step[1] >= TILES - 2:
                        break
                    if step[0] == "k":
                        turn_cache(h, plan, step[1])
                    elif step[0] == "a":
                        turn_a(h, par, plan, u, step[2])
                    elif step[0] == "v":
                        cache_values(h, par, plan, step[1])
                    else:
                        turn_rows(h + 1, step[1], turn_bank(h, plan, step))
                    if u != SAMPLE_UNIT and weighed < groups:
                        weigh(h, par, plan, u, weighed)
                        weighed += 1
                if u != SAMPLE_UNIT:
                    for g in range(weighed, groups):
                        weigh(h, par, plan, u, g)
                if slot <= 3:
                    cache_scores(h, plan, 2 * slot)
                    cache_scores(h, plan, 2 * slot + 1)
            if nxt:
                project(h + 1, TILES - 1, proj_bank(h, par, 2 + TILES - 1))
                turn_rows(h + 1, TILES - 2, turn_bank(h, plan, ("x", TILES - 2)))
                silu_gate(h + 1, 0, proj_bank(h, par, 2 + TILES),
                          lambda: turn_rows(h + 1, TILES - 1, turn_bank(h, plan, ("x", TILES - 1))))

        def turn_first(t):
            turn_rows(0, t, (t, c.bank_t[t % 2]))

        pe.sem_inc(kq_ok, 2)
        pe.sem_inc(pv_ok, 2)
        for t in range(TILES):
            if t < 2:
                front_stored.bank_read(pe, t)
            project(0, t, (t, c.bank_p[t % 2]), (lambda: turn_first(t - 2)) if t >= 2 else None)
        turn_first(TILES - 2)
        silu_gate(0, 0, (TILES, c.bank_p[TILES % 2]), lambda: turn_first(TILES - 1))
        all_heads(pe, head)

    def scalar(act):
        def squares(h, t):
            n, s = rows_of(t), t % 2
            act.wait_ge(rows_ok, TILES * h + t + 1)
            for j in range(1 if t == META_TILE else 0, 2):
                mm = act.activation(junk[0:n, j, :], qkn[0:n, s, j * P:(j + 1) * P], ACT.Square,
                                    accum_out=ss[0:n, s, j:j + 1])
            mm.then_inc(sq_ok, 1)

        def copy_rows(q, t, number):
            n, (c0, c1) = rows_of(t), tile_cols(t)
            num, bank = number
            act.wait_ge(t_full, num + 1)
            if t == META_TILE:
                act.activation(qk[:, q, 1, c0:c1], bank[:, P:P + n], ACT.Copy).then_inc(t_out, 1)
            else:
                act.activation(qk[:, q, :, c0:c1], bank[:, 0:2 * P].rearrange("p (a n) -> p a n", a=2),
                               ACT.Copy).then_inc(t_out, 1)

        def sigmoids(slot, parts, first, second):
            for m, (dst, scale, sem) in enumerate([(keep, -SCALE, first), (beta, SCALE, second)]):
                for n, (a, e, z) in enumerate(parts):
                    mm = act.activation(dst[:, slot, a:e], z, ACT.Sigmoid, scale=scale)
                if sem is not None:
                    mm.then_inc(sem, 1)

        def betas(h, par, u, plan):
            slot, w = (par + u) % 2, width(u)
            act.wait_ge(score_ok, UNITS * h + u + 1)
            if u == SAMPLE_UNIT:
                act.wait_ge(kq_ok, NB * h + NB + 2)
                sigmoids(slot, [(0, PAST, c.bank_s[:, :]), (PAST, PAST + P, c.bank_z[:, 0:P])], keep_ok, beta_ok)
                return
            if not meta_apart(u):
                sigmoids(slot, [(0, w, c.bank_z[:, 0:w])], keep_ok, beta_ok)
                return
            num, bank = turn_bank(h, plan, ("m", u))
            act.wait_ge(t_full, num + 1)
            sigmoids(slot, [(0, META, bank[:, 0:META])], None, t_out)
            sigmoids(slot, [(META, w, c.bank_z[:, 0:w - META])], keep_ok, beta_ok)

        def copy_cache_k(h, plan, b):
            num, bank = turn_bank(h, plan, ("k", b))
            act.wait_ge(t_full, num + 1)
            act.wait_ge(kq_ok, NB * h + b + 1)
            act.activation(kt[:, b % 2, :], bank[:, :], ACT.Copy).then_inc(t_out, 1)

        def copy_a(h, plan, u, g):
            items, gg = value_groups(u)[g], groups_before(u) + g
            num, bank = turn_bank(h, plan, ("a", u, g))
            act.wait_ge(t_full, num + 1)
            if u == SAMPLE_UNIT:
                a, n = (PAST, P) if items == ["new"] else (0, PAST)
                act.activation(ats[:, a:a + n], bank[:, 0:n], ACT.Copy).then_inc(t_out, 1)
                return
            act.wait_ge(pv_ok, NGROUPS * h + gg + 1)
            a = 0
            if items[0] == "meta":
                a = P
                act.activation(at[0:META, gg % 2, 0:P], bank[0:META, 0:P], ACT.Copy)
            act.activation(at[:, gg % 2, a:len(items) * P], bank[:, a:len(items) * P], ACT.Copy).then_inc(t_out, 1)

        def copy_o(h, plan, b):
            num, bank = turn_bank(h, plan, ("v", b))
            act.wait_ge(t_full, num + 1)
            act.activation(ot[:, SEQ + b * DS:SEQ + (b + 1) * DS], bank[:, 0:DS], ACT.Copy).then_inc(t_out, 1)

        def z_sigmoid(h, n, number):
            c0, c1 = CHL[n]
            num, bank = number
            hold(act, proj_ok, num + 1)
            act.activation(zs[:, c0 - META:c1 - META], bank[:, 0:c1 - c0], ACT.Sigmoid,
                           bias=c.bias[:, head_block("z_s", h)]).then_inc(zsig_ok, 1)

        def split_y_hi(k, src):
            act.activation(c.xh[:, k, 0:LIVE], src, ACT.Copy).then_inc(yh_ok, 1)

        def head(h, par, pairs, nxt, nxt2):
            plan = plans[nxt]

            def turned(step):
                if step[0] == "k":
                    copy_cache_k(h, plan, step[1])
                elif step[0] == "a":
                    copy_a(h, plan, step[1], step[2])
                elif step[0] == "v":
                    copy_o(h, plan, step[1])
                elif step[0] == "x":
                    copy_rows(1 - par, step[1], turn_bank(h, plan, step))

            betas(h, par, 0, plan)
            turned(("k", 0))
            turned(("k", 1))
            if nxt:
                split_qkv_hi(act, h + 1)
            z_sigmoid(h, 1, z_bank(h, par, 1))
            if nxt:
                z_sigmoid(h, 2, z_bank(h, par, 2))
            for slot in range(1, UNITS + 1):
                before, after = slot_steps(slot, nxt)
                if slot < UNITS:
                    betas(h, par, slot, plan)
                for step in before:
                    turned(step)
                if slot == LATE_Z and not nxt:
                    z_sigmoid(h, 2, z_bank(h, par, 2))
                if slot == UNITS - 3 and not nxt:
                    following.first_splits(act)
                for step in after:
                    if slot < UNITS or step[1] < TILES - 2:
                        turned(step)
                if nxt:
                    squares(h + 1, slot - 1)
                if slot == 1 and nxt:
                    wz.split_hi(act, h + 1, 0)
                for k in [] if nxt else Y_AGAIN.get(slot, []):
                    act.wait_ge(y_in[k % 2], 16 * (k // 2 + 1))
                    split_y_hi(k, y_again[:, (k % 2) * LIVE:(k % 2 + 1) * LIVE])
            if nxt:
                turned(("x", TILES - 2))
                squares(h + 1, TILES - 1)
                turned(("x", TILES - 1))
                act.wait_ge(y_ok, h + 1)
                z_sigmoid(h + 1, 0, proj_bank(h, par, 2 + TILES))
            else:
                for n, (a, e) in enumerate(LIVE_CHUNKS):
                    act.wait_ge(y_ok, HEADS + n)
                    act.activation(c.xh[:, HEADS - 1, a:e], ot[:, a:e], ACT.Copy).then_inc(yh_ok, 1)

        act.sem_inc(t_out, 2)
        act.sem_inc(beta_ok, 1)
        for t in range(TILES):
            squares(0, t)
            if t == 0:
                wz.split_hi(act, 0, 0)
            if t:
                copy_rows(0, t - 1, (t - 1, c.bank_t[(t - 1) % 2]))
        front_stored.stored(act)
        copy_rows(0, TILES - 1, (TILES - 1, c.bank_t[(TILES - 1) % 2]))
        z_sigmoid(0, 0, (TILES, c.bank_p[TILES % 2]))
        all_heads(act, head)

    def vector(dve):
        def rows(h, q, pairs, t, number):
            n, s = rows_of(t), t % 2
            a = P if t == META_TILE else 0
            num, bank = number
            dve.wait_ge(proj_ok, num + 1)
            if t == 0:
                dve.wait_ge(b3_in[q], 48 * (pairs + 1))
                dve.wait_ge(v_stored[q], 16 * TILES * pairs + 16)
            dve.wait_ge(k_stored[s], 16 * (TILES // 2) * h + 16 * (t // 2) + 16)
            dve.tensor_tensor(qkn[0:n, s, a:2 * P], bank[0:n, a:2 * P], bias3[0:n, q, a:2 * P],
                              ALU.add).then_inc(rows_ok, 1)
            dve.tensor_tensor(v[0:n, q, t, :], bank[0:n, 2 * P:3 * P], bias3[0:n, q, 2 * P:3 * P],
                              ALU.add).then_inc(proj_out, 1)

        def normalise(h, t):
            n, s = rows_of(t), t % 2
            dve.wait_ge(rstd_ok, TILES * h + t + 1)
            for j in range(1 if t == META_TILE else 0, 2):
                mm = dve.scalar_tensor_tensor(out=qkn[0:n, s, j * P:(j + 1) * P], in0=qkn[0:n, s, j * P:(j + 1) * P],
                                              scalar=rs[0:n, s, j:j + 1], in1=gain[0:n, j, :],
                                              op0=ALU.mult, op1=ALU.mult)
            mm.then_inc(norm_ok, 1)

        def sticks(h, par, u):
            slot, w, n = (par + u) % 2, width(u), UNITS * h + u
            dve.wait_ge(keep_ok, n + 1)
            young_first = keep[:, slot, 0:w][:, ::-1]
            dve.tensor_tensor_scan(young_first, young_first, young_first, 1.0,
                                   ALU.mult, ALU.bypass).then_inc(scan_ok, 1)
            dve.wait_ge(scan_ok, n + 1)
            dve.wait_ge(beta_ok, n + 1 + 1)
            dve.tensor_tensor(beta[:, slot, 0:w - 1], beta[:, slot, 0:w - 1], keep[:, slot, 1:w],
                              ALU.mult).then_inc(a_ok, 1)

        def take_o(h, u):
            if u == SAMPLE_UNIT:
                return
            if u == 0:
                dve.wait_ge(y_stored, 16 * h + 16)
            a = ORDER[u] * P
            dve.wait_ge(pv_ok, NGROUPS * h + groups_before(u + 1) + 2)
            dve.tensor_copy(ot[:, a:a + P], c.bank_o[:, 0:P]).then_inc(o_out, 1)

        def z_silu(h, n, number):
            c0, c1 = CHL[n]
            z = zs[:, c0 - META:c1 - META]
            dve.wait_ge(zsig_ok, 3 * h + n + 1)
            dve.scalar_tensor_tensor(out=z, in0=number[1][:, 0:c1 - c0],
                                     scalar=c.bias[:, head_block("z_s", h)], in1=z,
                                     op0=ALU.add, op1=ALU.mult).then_inc(proj_out, 1)

        def head(h, par, pairs, nxt, nxt2):
            plan = plans[nxt]
            sticks(h, par, 0)
            for n in (1, 2) if nxt else (1,):
                z_silu(h, n, z_bank(h, par, n))
            for slot in range(1, UNITS + 1):
                if slot < UNITS:
                    sticks(h, par, slot)
                if slot == LATE_Z and not nxt:
                    z_silu(h, 2, z_bank(h, par, 2))
                if nxt:
                    rows(h + 1, 1 - par, pairs + par, slot - 1, proj_bank(h, par, 2 + slot - 1))
                take_o(h, slot - 1)
                if nxt:
                    normalise(h + 1, slot - 1)
            dve.wait_ge(o_out, PROMPT_UNITS * h + PROMPT_UNITS + 1)
            dve.wait_ge(t_out, turn_bank(h, plan, ("v", NB - 1))[0] + 1 + 2)
            for a, e in [(0, LIVE)] if nxt else LIVE_CHUNKS:
                dve.tensor_tensor(ot[:, a:e], zs[:, a:e], ot[:, a:e], ALU.mult).then_inc(y_ok, 1)
            if nxt:
                rows(h + 1, 1 - par, pairs + par, TILES - 1, proj_bank(h, par, 2 + TILES - 1))
                normalise(h + 1, TILES - 1)
                z_silu(h + 1, 0, proj_bank(h, par, 2 + TILES))
            else:
                for n, (a, e) in enumerate(LIVE_CHUNKS):
                    dve.wait_ge(yh_ok, HEADS + n)
                    dve.tensor_tensor(c.xl[:, HEADS - 1, a:e], ot[:, a:e], c.xh[:, HEADS - 1, a:e].bitcast(F32),
                                      ALU.subtract).then_inc(y_last_ok, 1)

        dve.sem_inc(proj_out, 2)
        dve.sem_inc(o_out, 1)
        dve.wait_ge(gain_in, 32)
        for t in range(TILES):
            rows(0, 0, 0, t, (t, c.bank_p[t % 2]))
            normalise(0, t)
        z_silu(0, 0, (TILES, c.bank_p[TILES % 2]))
        all_heads(dve, head)

    def last_y_split(pe, n):
        pe.wait_ge(y_last_ok, n + 1)

    def y_split(eng):
        eng.wait_ge(yl_ok, HEADS - 1)

    heads = Group()
    heads.load_qkv, heads.first_loads, heads.first_splits = load_qkv, first_loads, first_splits
    heads.y_split, heads.last_y_split = y_split, last_y_split
    return Programs(sync, gpsimd, tensor, scalar, vector), heads


def merge_and_output(c, d, e):
    so_cols = d["w_sb_o"][0].rearrange("(k p) (n e) -> p k n e", p=P, e=P)
    o_cols = d["w_o"][0].rearrange("(k p) (n e) -> p k n e", p=P, e=P)
    x_tiles = d["x_prompt"][0].rearrange("(t p) (n e) -> p t n e", p=P, e=P)
    y_tiles = d["y_prompt"][0].rearrange("(t p) (n e) -> p t n e", p=P, e=P)
    xs_rows = d["x_sample"].rearrange("b s (n e) -> (b s) n e", e=P)
    ys_rows = d["y_sample"].rearrange("b s (n e) -> (b s) n e", e=P)
    groups = [(0, 4), (4, 8), (8, 9)]
    ROUNDS = KC // 2
    w, mh, ml, sg, m1, xt, yt, yo = e.w, e.mh, e.ml, e.sg, e.m1, e.xt, e.yt, e.yo
    wo = w.continued(ROUNDS, 2)

    g_in = [c.sem(f"gate_s_in{s}") for s in range(2)]
    m_in = [c.sem(f"m_part_in{s}") for s in range(2)]
    so_full = c.sem("so_bank_full")
    gated, summed = c.sem("so_gated"), c.sem("m_summed")
    mh_ok, ml_ok = c.sem("m_hi_ok"), c.sem("m_lo_ok")
    x_in = [c.sem(f"x_again_in{s}") for s in range(2)]
    full = c.sem("o_bank_full")
    copied = c.sem("o_copied")
    turned = c.sem("o_turned")
    added = c.sem("o_added")
    stored = [c.sem(f"y_stored{s}") for s in range(2)]
    so_banks = [c.bank_p[0], c.bank_p[1], c.bank_o, c.bank_z[:, 0:512], c.bank_z[:, 512:1024], c.bank_s[:, :]]
    o_banks = [c.bank_p[0], c.bank_p[1], c.bank_o]
    turn_banks = [c.bank_t[0], c.bank_t[1], c.bank_z[:, 0:512]]
    chunks = LIVE_CHUNKS

    def first_loads(sp):
        for s in range(2):
            w.load(sp, 0, s, so_cols[:, :, s, :])

    def sync(sp, parts_free):
        def load_parts(i, s):
            n = bass.ds(2 * i + s, 1)
            sp.dma_start(sg[:, s, :], d["sgate"][n].rearrange("o p n -> (o p) n")).then_inc(g_in[s], 16)
            sp.dma_start(m1[:, s, :], d["m1"][n].rearrange("o p n -> (o p) n")).then_inc(m_in[s], 16)

        def load_x(i, s):
            n = bass.ds(2 * i + s, 1)
            sp.dma_start(xt[:, s, 0:PT, :], x_tiles[:, :, n, :].rearrange("p t o e -> p t (o e)")).then_inc(x_in[s], 16)
            sp.dma_start(xt[:, s, PT, :], xs_rows[:, n, :].rearrange("p o e -> p (o e)")).then_inc(x_in[s], 16)

        parts_free(sp)
        for s in range(2):
            load_parts(0, s)
        with sp.Fori(0, ROUNDS - 1) as i:
            for s in range(2):
                w.load(sp, i + 1, s, so_cols[:, :, bass.ds(2 * i + 2 + s, 1), :])
                sp.wait_ge(ml_ok, 6 * i + 3 * s + 3)
                load_parts(i + 1, s)
        for s in range(2):
            sp.sem_inc(stored[s], 32)
            wo.load(sp, 0, s, o_cols[:, :, s, :])
            if s == 0:
                sp.wait_ge(ml_ok, 1)
            load_x(0, s)

        def one_pair(i, more):
            for s in range(2):
                n = bass.ds(2 * i + s, 1)
                if more:
                    wo.load(sp, i + 1, s, o_cols[:, :, bass.ds(2 * i + 2 + s, 1), :])
                sp.wait_ge(added, 6 * i + 3 * s + 3 + 6)
                sp.dma_start(y_tiles[:, :, n, :].rearrange("p t o e -> p t (o e)"), yo[:, s, 0:PT, :]).then_inc(stored[s], 16)
                sp.dma_start(ys_rows[:, n, :].rearrange("p o e -> p (o e)"), yo[:, s, PT, :]).then_inc(stored[s], 16)
                if more:
                    load_x(i + 1, s)

        with sp.Fori(0, ROUNDS - 1) as i:
            one_pair(i, True)
        one_pair(ROUNDS - 1, False)
        for s in range(2):
            sp.wait_ge(stored[s], 32 * (ROUNDS + 1))

    def gpsimd(pool):
        with pool.Fori(1, 2 * ROUNDS) as i:
            w.split_lo(pool, i, 0)
            w.split_lo(pool, i, 1)

    def first_splits(act):
        w.split_hi(act, 0, 0)
        w.split_hi(act, 0, 1)

    def scalar(act):
        def merge_pair(i, more):
            for s in range(2):
                for n, (a, b) in enumerate(chunks):
                    if n == 2:
                        act.wait_ge(so_full, 6 * i + 3 * s + 3)
                        if more:
                            w.split_hi(act, i + 1, s)
                        else:
                            wo.split_hi(act, 0, s)
                    hold(act, summed, 6 * i + 3 * s + n + 1)
                    act.activation(row(mh, 2 * i + s, a, b), m1[:, s, a:b], ACT.Copy).then_inc(mh_ok, 1)

        with act.Fori(0, ROUNDS - 1) as i:
            merge_pair(i, True)
        merge_pair(ROUNDS - 1, False)

        def output_pair(i, more):
            for s in range(2):
                for n, (a, b) in enumerate(chunks):
                    act.wait_ge(full, 6 * i + 3 * s + n + 1)
                    act.activation(yt[:, s, a:b], o_banks[n][:, 0:b - a], ACT.Copy).then_inc(copied, 1)
                if more:
                    wo.split_hi(act, i + 1, s)

        with act.Fori(0, ROUNDS - 1) as i:
            output_pair(i, True)
        output_pair(ROUNDS - 1, False)

    def credits(dve):
        dve.sem_inc(gated, 6)

    def vector(dve):
        with dve.Fori(0, ROUNDS) as i:
            for s in range(2):
                def low(n):
                    a, b = chunks[n]
                    dve.wait_ge(mh_ok, 6 * i + 3 * s + n + 1)
                    dve.tensor_tensor(row(ml, 2 * i + s, a, b), m1[:, s, a:b],
                                      row(mh, 2 * i + s, a, b).bitcast(F32), ALU.subtract).then_inc(ml_ok, 1)

                dve.wait_ge(g_in[s], 16 * i + 16)
                dve.wait_ge(m_in[s], 16 * i + 16)
                for n, (a, b) in enumerate(chunks):
                    dve.wait_ge(so_full, 6 * i + 3 * s + n + 1)
                    dve.tensor_tensor(sg[:, s, a:b], so_banks[3 * s + n][:, 0:b - a], sg[:, s, a:b], ALU.mult).then_inc(gated, 1)
                    dve.wait_ge(gated, 6 * i + 3 * s + n + 1 + 6)
                    dve.tensor_tensor(m1[:, s, a:b], m1[:, s, a:b], sg[:, s, a:b], ALU.add).then_inc(summed, 1)
                    if n:
                        low(n - 1)
                low(2)
        dve.sem_inc(added, 6)
        with dve.Fori(0, ROUNDS) as i:
            for s in range(2):
                dve.wait_ge(x_in[s], 32 * i + 32)
                dve.wait_ge(stored[s], 32 * i + 32)
                for g, (a, b) in enumerate(groups):
                    dve.wait_ge(turned, 6 * i + 3 * s + g + 1)
                    dve.tensor_tensor(yo[:, s, a:b, :], turn_banks[g][:, 0:(b - a) * P].rearrange("p (t e) -> p t e", e=P),
                                      xt[:, s, a:b, :], ALU.add).then_inc(added, 1)

    def tensor(pe, y_split, last_y_split):
        def merge_pair(i, first):
            for s in range(2):
                w.ready(pe, i, s)
                for n, (a, b) in enumerate(chunks):
                    out, y = so_banks[3 * s + n][:, 0:b - a], x_moving(c, a, b)
                    pe.wait_ge(gated, 6 * i + 3 * s + n + 1)
                    if first and s == 0:
                        if n == 0:
                            y_split(pe)
                        w.product(pe, s, out, y, range(KC - 1))
                        last_y_split(pe, n)
                        mm = w.product(pe, s, out, y, range(KC - 1, KC))
                    else:
                        mm = w.product(pe, s, out, y)
                    mm.then_inc(so_full, 1)

        merge_pair(0, True)
        with pe.Fori(1, ROUNDS) as i:
            merge_pair(i, False)

        def product(i, s, first=False):
            wo.ready(pe, i, s)
            for n, (a, b) in enumerate(chunks):
                if first:
                    pe.wait_ge(ml_ok, 6 * (ROUNDS - 1) + 3 + n + 1)
                else:
                    pe.wait_ge(copied, 6 * i + 3 * s + n + 1 - 3)
                wo.product(pe, s, o_banks[n][:, 0:b - a],
                           (lambda k: mh[:, k, a:b], lambda k: ml[:, k, a:b])).then_inc(full, 1)

        def turn(i, s):
            for g, (a, b) in enumerate(groups):
                pe.wait_ge(copied, 6 * i + 3 * s + (2, 3, 3)[g])
                pe.wait_ge(added, 6 * i + 3 * s + g + 1 + 3)
                for t in range(a, b):
                    mm = pe.transpose(turn_banks[g][:, (t - a) * P:(t - a + 1) * P], yt[:, s, t * P:(t + 1) * P],
                                      c.ident[:, :])
                mm.then_inc(turned, 1)

        product(0, 0, first=True)
        with pe.Fori(0, ROUNDS - 1) as i:
            product(i, 1)
            turn(i, 0)
            product(i + 1, 0)
            turn(i, 1)
        product(ROUNDS - 1, 1)
        turn(ROUNDS - 1, 0)
        turn(ROUNDS - 1, 1)

    first = Group()
    first.weights, first.first_loads, first.first_splits, first.credits = w, first_loads, first_splits, credits
    return Programs(sync, gpsimd, tensor, scalar, vector), first


def late_buffers(c):
    b, e = Group(), Group()
    with ExitStack() as low:
        e.mh = c.sb(low, "m_hi", [P, KC, LIVE], F32R)
        with ExitStack() as parts:
            e.sg = c.sb(parts, "gate_s", [P, 2, LIVE])
            e.m1 = c.sb(parts, "m_part", [P, 2, LIVE])
        e.yt = c.sb(low, "y_turned", [P, 2, LIVE])
        e.yo = c.sb(low, "y_rows", [P, 2, PT + 1, P])
    with ExitStack() as ctx:
        b.beta = c.sb(ctx, "beta", [P, 2, SAMPLE0])
        b.keep = c.sb(ctx, "one_minus_beta", [P, 2, SAMPLE0])
        b.at = c.sb(ctx, "a_turned", [P, 2, 4 * P])
        b.ats = c.sb(ctx, "a_samples_turned", [P, PAST + P])
        b.ot = c.sb(ctx, "o_turned", [P, LIVE])
        b.zs = c.sb(ctx, "silu_z", [P, LIVE])
        b.vc = c.sb(ctx, "cache_v_rows", [P, 2, PAST // P, P])
        b.kt = c.sb(ctx, "cache_k_turned", [P, 2, PAST])
        b.kc = c.sb(ctx, "cache_k_rows", [P, 2, PAST // P, P])
        b.w3 = c.sb(ctx, "wqkv_raw", [P, KC, 3 * P])
        with ExitStack() as weights:
            b.w3h = c.sb(weights, "wqkv_hi", [P, KC, 3 * P], F32R)
            b.w3l = c.sb(weights, "wqkv_lo", [P, KC, 3 * P], F32R)
        e.w = WeightTiles(c, ctx, "wm", 2, 2)
        with ExitStack() as rest:
            b.wz = WeightTiles(c, rest, "wz", 1, 1)
            b.bias3 = c.sb(rest, "bias_qkv", [P, 2, 3 * P])
            b.gain = c.sb(rest, "qk_gain", [P, 2, P])
            b.qk = c.sb(rest, "qk_turned", [P, 2, 2, TOK])
            b.v = c.sb(rest, "v_rows", [P, 2, TILES, P])
            b.qkn = c.sb(rest, "qk_rows", [P, 2, 2 * P])
            b.junk = c.sb(rest, "squares2", [P, 2, P])
            b.ss = c.sb(rest, "qk_sumsq", [P, 2, 2])
            b.ms = c.sb(rest, "qk_meansq", [P, 2, 2])
            b.rs = c.sb(rest, "qk_rstd", [P, 2, 2])
            b.half = c.sb(rest, "minus_half2", [P, 2])
            b.qbd = c.sb(rest, "q_block_diagonal", [P, NB * (P + DS)])
        e.ml = c.sb(ctx, "m_lo", [P, KC, LIVE], F32R)
        e.xt = c.sb(ctx, "x_again", [P, 2, PT + 1, P])
    return b, e


def build(nc, d):
    d["m1"] = nc.dram_tensor("m_part_scratch", (KC, P, LIVE), F32).ap()
    d["sgate"] = nc.dram_tensor("gate_scratch", (KC, P, LIVE), F32).ap()
    d["ys"] = nc.dram_tensor("y_s_scratch", (HEADS, P, LIVE), F32).ap()
    with ExitStack() as ctx:
        c = Core(nc, ctx)
        HELD["waits_held"] = c.sem("waits_held")
        c.bank_z = ctx.enter_context(nc.psum_tensor("bank_z", [P, 2 * 512], F32))
        c.bank_s = ctx.enter_context(nc.psum_tensor("bank_s", [P, 512], F32))
        c.bank_p = [ctx.enter_context(nc.psum_tensor(f"bank_p{i}", [P, 512], F32)) for i in range(2)]
        c.bank_t = [ctx.enter_context(nc.psum_tensor(f"bank_t{i}", [P, 512], F32)) for i in range(2)]
        c.bank_o = ctx.enter_context(nc.psum_tensor("bank_o", [P, 512], F32))
        c.ident, c.identb = c.sb(ctx, "ident", [P, P]), c.sb(ctx, "ident_bf16", [P, P], BF16)
        c.mask, c.mask_s = c.sb(ctx, "mask", [P, P], BF16), c.sb(ctx, "mask_samples", [P, P], BF16)
        c.bias = c.sb(ctx, "bias_turned", [P, 80])
        c.xh = c.sb(ctx, "x_hi", [P, KC, TOK], F32R)
        c.xl = c.sb(ctx, "x_lo", [P, KC, TOK], F32R)
        first, front_done = front(c, d)
        buf, end = late_buffers(c)
        last, first_of_last = merge_and_output(c, d, end)
        middle, heads = attention(c, d, buf, front_done, first_of_last)
        with nc.Block() as block:
            @block.sync
            def _(sp):
                first.sync(sp, heads.load_qkv, heads.first_loads)
                middle.sync(sp)
                last.sync(sp, heads.y_split)

            @block.gpsimd
            def _(pool):
                first.gpsimd(pool)
                middle.gpsimd(pool)
                last.gpsimd(pool)

            @block.tensor
            def _(pe):
                first.tensor(pe)
                middle.tensor(pe)
                last.tensor(pe, heads.y_split, heads.last_y_split)

            @block.scalar
            def _(act):
                first.scalar(act, heads.first_splits)
                middle.scalar(act)
                last.scalar(act)

            @block.vector
            def _(dve):
                first_of_last.credits(dve)
                first.vector(dve)
                middle.vector(dve)
                last.vector(dve)


INPUTS = ["x_prompt", "x_sample", "cache_k", "cache_v", "state_conv", "meta_tokens", "norm_g", "w_in", "b_in",
          "q_norm_g", "k_norm_g", "conv_w", "w_conv_o", "w_sb_o", "w_o"]
OUTPUTS = [("y_prompt", (1, SEQ, D)), ("y_sample", (NB, DS, D)), ("k_prompt", (1, 1, SAMPLE0, HEADS, HD)),
           ("v_prompt", (1, 1, SAMPLE0, HEADS, HD)), ("conv_prompt", (1, 1, 2, D)),
           ("k_sample", (1, NB, DS, HEADS, HD)), ("v_sample", (1, NB, DS, HEADS, HD)), ("conv_sample", (1, NB, 2, D))]


def kernel(**inputs):
    import numpy as np
    import concourse.bacc as bacc
    from concourse.bass_utils import run_bass_kernel_spmd as run

    nc = bacc.Bacc("TRN2", target_bir_lowering=False, num_devices=1)
    arrays, d = {}, {}
    for name in INPUTS:
        a = np.ascontiguousarray(inputs[name])
        arrays["in_" + name] = a
        d[name] = nc.dram_tensor("in_" + name, a.shape, mybir.dt.from_np(a.dtype), kind="ExternalInput").ap()
    for name, shape in OUTPUTS:
        d[name] = nc.dram_tensor("out_" + name, shape, F32, kind="ExternalOutput").ap()
    build(nc, d)
    r = run(nc, [arrays], core_ids=[0])
    return tuple(r.results[0]["out_" + name] for name, _ in OUTPUTS)
```
